# Optimizing a Trainium2 kernel written in Bass

```python
import jax, jax.numpy as jnp
from jax import lax
import numpy as np

D_MODEL = 1024
BATCH = 1
SEQ = 512
DEPTH = 2

A_HEADS = 4
A_DK = 128
A_DV = 128
A_KD = A_HEADS * A_DK
A_WIDTH = A_HEADS * A_DV
A_CHUNK = 64
B_Q_HEADS = 8
B_KV_HEADS = 2
B_HEAD_DIM = 64
B_WIDTH = B_Q_HEADS * B_HEAD_DIM
B_KV_WIDTH = B_KV_HEADS * B_HEAD_DIM
WINDOW = 128
ROPE_DIM = B_HEAD_DIM // 4
ROPE_THETA = 500000.0
AB_IN_WIDTH = 2 * A_KD + 2 * A_WIDTH + B_WIDTH + 2 * B_KV_WIDTH
AB_OUT_WIDTH = A_WIDTH + B_WIDTH
POOL_WINDOWS = (2, 4, 8, 16)
POOL_GROUPS = 4
POOL_GROUP = D_MODEL // POOL_GROUPS
D_FF = 2816
CONV_WIDTH = 3
N_EVEN = (DEPTH + 1) // 2
N_ODD = DEPTH // 2
ALPHA = (2.0 * DEPTH) ** 0.25
BETA = (8.0 * DEPTH) ** -0.25
LN_EPS = 1e-5
RMS_EPS = 1e-6


F32 = jnp.float32

def _layer_norm(x, g, b):
    xf = x.astype(F32)
    mu = xf.mean(-1, keepdims=True)
    var = jnp.mean(jnp.square(xf - mu), -1, keepdims=True)
    return ((xf - mu) * lax.rsqrt(var + LN_EPS) * g + b).astype(x.dtype)

def _rope(x, cos, sin):
    half = ROPE_DIM // 2
    x1 = x[..., :half].astype(F32)
    x2 = x[..., half:ROPE_DIM].astype(F32)
    r1 = x1 * cos - x2 * sin
    r2 = x2 * cos + x1 * sin
    return jnp.concatenate([r1.astype(x.dtype), r2.astype(x.dtype), x[..., ROPE_DIM:]], -1)

def _hgrn2(q, fz, i, lb):
    Bn, T = q.shape[:2]
    fzf = fz.astype(F32)
    f = lb + (1.0 - lb) * jax.nn.sigmoid(fzf)
    logf = jnp.log(f)
    k = (1.0 - lb) * jax.nn.sigmoid(-fzf)
    nc = T // A_CHUNK

    def to_chunks(a):
        a = a.reshape(Bn, nc, A_CHUNK, A_HEADS, a.shape[-1])
        return a.transpose(1, 0, 3, 2, 4)

    qc, kc, vc, gc = (to_chunks(a) for a in (q.astype(F32), k, i.astype(F32), logf))
    causal = jnp.tril(jnp.ones((A_CHUNK, A_CHUNK), bool))[:, :, None]

    def step(S, inp):
        qb, kb, vb, gb = inp
        b = jnp.cumsum(gb, axis=2)
        o_inter = jnp.einsum('bhtk,bhkv->bhtv', qb * jnp.exp(b), S)
        diff = b[:, :, :, None, :] - b[:, :, None, :, :]
        decay = jnp.exp(jnp.where(causal, diff, -jnp.inf))
        att = jnp.einsum('bhtk,bhsk,bhtsk->bhts', qb, kb, decay)
        o = o_inter + jnp.einsum('bhts,bhsv->bhtv', att, vb)
        b_last = b[:, :, -1:, :]
        S = jnp.exp(b_last[:, :, 0])[..., None] * S + jnp.einsum(
            'bhsk,bhsv->bhkv', kb * jnp.exp(b_last - b), vb)
        return S, o

    S0 = jnp.zeros((Bn, A_HEADS, A_DK, A_DV), F32)
    _, o = lax.scan(step, S0, (qc, kc, vc, gc))
    return o.transpose(1, 0, 3, 2, 4).reshape(Bn, T, A_HEADS, A_DV)

def _swa(q, k, v, sinks):
    Bn, T = q.shape[:2]
    nb = T // WINDOW
    G = B_Q_HEADS // B_KV_HEADS
    qb = q.reshape(Bn, nb, WINDOW, B_KV_HEADS, G, B_HEAD_DIM)

    def band(a):
        a = a.reshape(Bn, nb, WINDOW, B_KV_HEADS, B_HEAD_DIM)
        prev = jnp.pad(a, ((0, 0), (1, 0), (0, 0), (0, 0), (0, 0)))[:, :-1]
        return jnp.concatenate([prev, a], axis=2)

    kb, vb = band(k), band(v)
    s = jnp.einsum('bnqhgd,bnkhd->bnhgqk', qb, kb).astype(F32) * (B_HEAD_DIM ** -0.5)
    qi = jnp.arange(WINDOW)[:, None] + WINDOW
    ki = jnp.arange(2 * WINDOW)[None, :]
    rel = qi - ki
    allowed = (rel >= 0) & (rel < WINDOW)
    blk = jnp.arange(nb)[:, None, None]
    valid = allowed[None] & ((blk > 0) | (ki[None] >= WINDOW))
    s = jnp.where(valid[None, :, None, None], s, -jnp.inf)
    sink = sinks.astype(F32).reshape(B_KV_HEADS, G)[None, None, :, :, None, None]
    m = jnp.maximum(s.max(-1, keepdims=True), sink)
    p = jnp.exp(s - m)
    p = p / (p.sum(-1, keepdims=True) + jnp.exp(sink - m))
    o = jnp.einsum('bnhgqk,bnkhd->bnqhgd', p.astype(v.dtype), vb)
    return o.reshape(Bn, T, B_WIDTH)

def _even_mixer(h, w_in, w_out, lb, norm_g, sinks, cos, sin):
    Bn, T, _ = h.shape
    z = h @ w_in
    widths = [A_KD, A_KD, A_WIDTH, A_WIDTH, B_WIDTH, B_KV_WIDTH, B_KV_WIDTH]
    idx = np.cumsum(widths)[:-1].tolist()
    aq, af, ai, ag, bq, bk, bv = jnp.split(z, idx, axis=-1)
    oa = _hgrn2(aq.reshape(Bn, T, A_HEADS, A_DK), af.reshape(Bn, T, A_HEADS, A_DK),
                ai.reshape(Bn, T, A_HEADS, A_DV), lb.reshape(A_HEADS, A_DK))
    oa = oa * lax.rsqrt(jnp.mean(oa * oa, -1, keepdims=True) + RMS_EPS) * norm_g
    oa = oa.reshape(Bn, T, A_WIDTH).astype(h.dtype) * jax.nn.silu(ag)
    q = _rope(bq.reshape(Bn, T, B_Q_HEADS, B_HEAD_DIM), cos, sin)
    k = _rope(bk.reshape(Bn, T, B_KV_HEADS, B_HEAD_DIM), cos, sin)
    v = bv.reshape(Bn, T, B_KV_HEADS, B_HEAD_DIM)
    ob = _swa(q, k, v, sinks).astype(h.dtype)
    return jnp.concatenate([oa, ob], axis=-1) @ w_out

def _pool_mixer(h, w_grp, scale):
    Bn, T, D = h.shape
    hf = h.astype(F32).reshape(Bn, T, POOL_GROUPS, POOL_GROUP)
    t = jnp.arange(T)
    outs = []
    for gi, w in enumerate(POOL_WINDOWS):
        xg = hf[:, :, gi]
        cs = jnp.cumsum(jnp.pad(xg, ((0, 0), (w, 0), (0, 0))), axis=1)
        win_sum = cs[:, w:] - cs[:, :T]
        cnt = jnp.minimum(t + 1, w).astype(F32)[None, :, None]
        outs.append(win_sum / cnt - xg)
    pooled = jnp.stack(outs, axis=2).astype(h.dtype)
    y = jnp.einsum('btgc,gcd->btgd', pooled, w_grp)
    return y.reshape(Bn, T, D) * scale

def _conv_ffn(h, w_up, conv_w, conv_b, w_down):
    T = h.shape[1]
    u, v = jnp.split(h @ w_up, 2, axis=-1)
    up = jnp.pad(u, ((0, 0), (CONV_WIDTH - 1, 0), (0, 0)))
    uc = conv_b
    for j in range(CONV_WIDTH):
        uc = uc + up[:, j:j + T] * conv_w[j]
    return (jax.nn.silu(uc) * v) @ w_down

def first_inputs(seed: int = 0) -> dict:
    key = jax.random.key(seed)
    ks = jax.random.split(key, 20)
    n = jax.random.normal
    D = D_MODEL
    x = n(ks[0], (BATCH, SEQ, D), F32)
    c = n(ks[1], (BATCH, D), F32)
    offs = jax.random.randint(ks[2], (BATCH, 1), 0, 4096, dtype=jnp.int32)
    positions = offs + jnp.arange(SEQ, dtype=jnp.int32)[None, :]
    ada_w = n(ks[3], (DEPTH, D, 6 * D), F32) * D ** -0.5
    ada_b = 0.02 * n(ks[4], (DEPTH, 6 * D), F32)
    ln_g = 1.0 + 0.02 * n(ks[5], (DEPTH, 2, D), F32)
    ln_b = 0.02 * n(ks[6], (DEPTH, 2, D), F32)
    ab_w_in = n(ks[7], (N_EVEN, D, AB_IN_WIDTH), F32) * D ** -0.5
    ab_w_out = n(ks[8], (N_EVEN, AB_OUT_WIDTH, D), F32) * (AB_OUT_WIDTH ** -0.5 * BETA)
    hgrn_lb_raw = 0.5 * n(ks[9], (N_EVEN, A_KD), F32)
    hgrn_norm_g = 1.0 + 0.02 * n(ks[10], (N_EVEN, A_DV), F32)
    attn_sinks = 0.5 * n(ks[11], (N_EVEN, B_Q_HEADS), F32)
    pool_w = n(ks[12], (N_ODD, POOL_GROUPS, POOL_GROUP, POOL_GROUP), F32) * (POOL_GROUP ** -0.5 * BETA)
    pool_scale = 1.0 + 0.02 * n(ks[13], (N_ODD, D), F32)
    ffn_w_up = n(ks[14], (DEPTH, D, 2 * D_FF), F32) * D ** -0.5
    ffn_conv_w = n(ks[15], (DEPTH, CONV_WIDTH, D_FF), F32) * CONV_WIDTH ** -0.5
    ffn_conv_b = 0.02 * n(ks[16], (DEPTH, D_FF), F32)
    ffn_w_down = n(ks[17], (DEPTH, D_FF, D), F32) * (D_FF ** -0.5 * BETA)
    return {"x": x, "c": c, "positions": positions, "ada_w": ada_w, "ada_b": ada_b,
            "ln_g": ln_g, "ln_b": ln_b, "ab_w_in": ab_w_in, "ab_w_out": ab_w_out,
            "hgrn_lb_raw": hgrn_lb_raw, "hgrn_norm_g": hgrn_norm_g, "attn_sinks": attn_sinks,
            "pool_w": pool_w, "pool_scale": pool_scale, "ffn_w_up": ffn_w_up,
            "ffn_conv_w": ffn_conv_w, "ffn_conv_b": ffn_conv_b, "ffn_w_down": ffn_w_down}

def first_block(x, c, positions, ada_w, ada_b, ln_g, ln_b, ab_w_in, ab_w_out,
              hgrn_lb_raw, hgrn_norm_g, attn_sinks, pool_w, pool_scale,
              ffn_w_up, ffn_conv_w, ffn_conv_b, ffn_w_down):
    lb_p = jax.nn.softmax(hgrn_lb_raw.astype(F32), axis=0)
    lower_bounds = jnp.cumsum(lb_p, axis=0) - lb_p[0]
    inv_freq = ROPE_THETA ** (-jnp.arange(0, ROPE_DIM, 2, dtype=F32) / ROPE_DIM)
    ang = positions.astype(F32)[..., None] * inv_freq
    cos = jnp.cos(ang)[:, :, None, :]
    sin = jnp.sin(ang)[:, :, None, :]
    c_act = jax.nn.silu(c)
    for l in range(DEPTH):
        mod = c_act @ ada_w[l] + ada_b[l]
        sh1, sc1, g1, sh2, sc2, g2 = [m[:, None, :] for m in jnp.split(mod, 6, axis=-1)]
        h = x * (1.0 + sc1) + sh1
        if l % 2 == 0:
            e = l // 2
            y = _even_mixer(h, ab_w_in[e], ab_w_out[e], lower_bounds[e], hgrn_norm_g[e],
                            attn_sinks[e], cos, sin)
        else:
            o = l // 2
            y = _pool_mixer(h, pool_w[o], pool_scale[o])
        x = _layer_norm(ALPHA * x + g1 * y, ln_g[l, 0], ln_b[l, 0])
        h = x * (1.0 + sc2) + sh2
        y = _conv_ffn(h, ffn_w_up[l], ffn_conv_w[l], ffn_conv_b[l], ffn_w_down[l])
        x = _layer_norm(ALPHA * x + g2 * y, ln_g[l, 1], ln_b[l, 1])
    return x


GRID_W = 64
CTX_LEN = 256
N_EVEN_2 = (DEPTH + 1) // 2
N_ODD_2 = DEPTH // 2
EPS = 1e-6

RWKV_HEAD = 64
RWKV_HEADS = (3 * D_MODEL // 4) // RWKV_HEAD
RWKV_W = RWKV_HEADS * RWKV_HEAD
LORA_W = 64
LORA_A = 64
FOUR_GROUPS = 4
FOUR_W = D_MODEL - RWKV_W
FOUR_GROUP_W = FOUR_W // FOUR_GROUPS
MIX_W = RWKV_W + FOUR_W
N_SHIFT = 3 * RWKV_W + 2 * LORA_W + 2 * LORA_A
EVEN_IN = N_SHIFT + RWKV_W + 2 * FOUR_W
RWKV_GN_EPS = 64e-5

RET_HEADS = 8
RET_HEAD = D_MODEL // RET_HEADS
RET_W = RET_HEADS * RET_HEAD
ODD_IN = 4 * RET_W
RET_CHUNK = 128
ROPE_BASE = 10000.0


def rmsnorm(x, g):
    xf = x.astype(jnp.float32)
    y = xf * lax.rsqrt(jnp.mean(xf * xf, axis=-1, keepdims=True) + EPS)
    return (y * g.astype(jnp.float32)).astype(x.dtype)

def qshift(u, rows):
    b, l, ch = u.shape
    g = u.reshape(b, rows, GRID_W, ch // 4, 4)
    left = jnp.pad(g[:, :, :-1, :, 0], ((0, 0), (0, 0), (1, 0), (0, 0)))
    right = jnp.pad(g[:, :, 1:, :, 1], ((0, 0), (0, 0), (0, 1), (0, 0)))
    up = jnp.pad(g[:, :-1, :, :, 2], ((0, 0), (1, 0), (0, 0), (0, 0)))
    down = jnp.pad(g[:, 1:, :, :, 3], ((0, 0), (0, 1), (0, 0), (0, 0)))
    return jnp.stack([left, right, up, down], axis=-1).reshape(b, l, ch)

def bishift(u):
    b, l, ch = u.shape
    g = u.reshape(b, l, ch // 2, 2)
    prev = jnp.pad(g[:, :-1, :, 0], ((0, 0), (1, 0), (0, 0)))
    nxt = jnp.pad(g[:, 1:, :, 1], ((0, 0), (0, 1), (0, 0)))
    return jnp.stack([prev, nxt], axis=-1).reshape(b, l, ch)

def rwkv_dir_terms(r, k0, v, wl, al, w0, w2, a0, a2, k_k, k_a, r_k):
    b, l, _ = r.shape
    hs = lambda t: t.reshape(b, l, RWKV_HEADS, RWKV_HEAD)
    w_log = -jax.nn.softplus(-(w0 + jnp.tanh(wl) @ w2)) - 0.5
    decay = jnp.exp(-jnp.exp(w_log))
    a = jax.nn.sigmoid(a0 + al @ a2)
    kk = hs(k0 * k_k)
    kk = kk / jnp.maximum(jnp.sqrt(jnp.sum(kk * kk, axis=-1, keepdims=True)), 1e-12)
    k = hs(k0 * (1.0 + (a - 1.0) * k_a))
    rh, vh = hs(r), hs(v)
    bonus = jnp.sum(rh * k * r_k, axis=-1, keepdims=True) * vh
    return rh, hs(decay), k, vh, kk, kk * hs(a), bonus

def rwkv7_scan(r, w, k, v, kk, bb, s0, reverse):
    def step(s, inp):
        r_t, w_t, k_t, v_t, kk_t, b_t = inp
        sa = jnp.einsum('bhij,bhj->bhi', s, kk_t)
        s = s * w_t[:, :, None, :] - sa[..., None] * b_t[:, :, None, :] + v_t[..., None] * k_t[:, :, None, :]
        return s, jnp.einsum('bhij,bhj->bhi', s, r_t)
    xs = tuple(jnp.moveaxis(t, 1, 0) for t in (r, w, k, v, kk, bb))
    s, ys = lax.scan(step, s0, xs, reverse=reverse)
    return s, jnp.moveaxis(ys, 0, 1)

def fourier_mix(u):
    b, l, _ = u.shape
    g = u.astype(jnp.float32).reshape(b, l, FOUR_GROUPS, FOUR_GROUP_W)
    f = jnp.fft.fft2(g, axes=(1, 3), norm='ortho').real
    return f.reshape(b, l, FOUR_W).astype(u.dtype)

def even_mixer(hc, hl, rows, w_in, mu, w0, w2, a0, a2, k_k, k_a, r_k, lnx_g, lnx_b, w_out, need_ctx):
    cuts = np.cumsum([RWKV_W, RWKV_W, RWKV_W, LORA_W, LORA_W, LORA_A]).tolist()

    def proj(h, shift_fn):
        u = h @ w_in
        s, gate_r, four, gate_f = jnp.split(u, [N_SHIFT, N_SHIFT + RWKV_W, N_SHIFT + RWKV_W + FOUR_W], axis=-1)
        s = (s + (shift_fn(s) - s) * mu).astype(jnp.float32)
        r, k0, v, wl_f, wl_b, al_f, al_b = jnp.split(s, cuts, axis=-1)
        return r, k0, v, (wl_f, wl_b), (al_f, al_b), gate_r, four, gate_f

    pc = proj(hc, bishift)
    pl = proj(hl, lambda t: qshift(t, rows))
    bsz = hl.shape[0]
    zeros = jnp.zeros((bsz, RWKV_HEADS, RWKV_HEAD, RWKV_HEAD), jnp.float32)
    oc, ol = 0.0, 0.0
    for d in range(2):
        tc = rwkv_dir_terms(pc[0], pc[1], pc[2], pc[3][d], pc[4][d], w0[d], w2[d], a0[d], a2[d], k_k, k_a, r_k)
        tl = rwkv_dir_terms(pl[0], pl[1], pl[2], pl[3][d], pl[4][d], w0[d], w2[d], a0[d], a2[d], k_k, k_a, r_k)
        s_ctx, yc = rwkv7_scan(*tc[:6], zeros, d == 1)
        _, yl = rwkv7_scan(*tl[:6], s_ctx, d == 1)
        oc = oc + yc + tc[6]
        ol = ol + yl + tl[6]

    def finish(o, gate_r, four, gate_f):
        b, l = o.shape[:2]
        mean = jnp.mean(o, axis=-1, keepdims=True)
        var = jnp.mean(jnp.square(o - mean), axis=-1, keepdims=True)
        o = ((o - mean) * lax.rsqrt(var + RWKV_GN_EPS)).reshape(b, l, RWKV_W) * lnx_g + lnx_b
        yr = o.astype(gate_r.dtype) * jax.nn.silu(gate_r)
        yf = fourier_mix(four) * jax.nn.silu(gate_f)
        return jnp.concatenate([yr, yf], axis=-1) @ w_out

    out_l = finish(ol, pl[5], pl[6], pl[7])
    out_c = finish(oc, pc[5], pc[6], pc[7]) if need_ctx else None
    return out_c, out_l

def axial_rope(t):
    l = t.shape[1]
    pos = jnp.arange(l)
    rc = jnp.stack([pos // GRID_W, pos % GRID_W], axis=-1).astype(jnp.float32)
    half = RET_HEAD // 2
    inv = ROPE_BASE ** (-jnp.arange(0, half, 2, dtype=jnp.float32) / half)
    ang = (rc[:, :, None] * inv).reshape(l, half)[:, None, :]
    cos, sin = jnp.cos(ang), jnp.sin(ang)
    t1, t2 = t[..., :half], t[..., half:]
    return jnp.concatenate([t1 * cos - t2 * sin, t1 * sin + t2 * cos], axis=-1)

def retention_scan(q, k, v, log_gamma, r0, strict):
    bsz, l, h, dk = q.shape
    dv = v.shape[-1]
    n_chunks = l // RET_CHUNK
    pos = jnp.arange(RET_CHUNK, dtype=jnp.float32)
    diff = pos[:, None] - pos[None, :]
    mask = diff > 0 if strict else diff >= 0
    dmat = jnp.where(mask[None], jnp.exp(jnp.where(mask, diff, 0.0)[None] * log_gamma[:, None, None]), 0.0)
    xi = jnp.exp((pos[:, None] + 1.0) * log_gamma[None, :])
    zeta = jnp.exp((RET_CHUNK - 1.0 - pos[:, None]) * log_gamma[None, :])
    g_chunk = jnp.exp(RET_CHUNK * log_gamma)

    def chunk(r, inp):
        qc, kc, vc = inp
        sc = jnp.einsum('bihd,bjhd->bhij', qc, kc) * dmat
        inner = jnp.einsum('bhij,bjhe->bihe', sc, vc)
        cross = jnp.einsum('bihd,bhde->bihe', qc, r) * xi[None, :, :, None]
        r = r * g_chunk[None, :, None, None] + jnp.einsum('bjhd,bjhe->bhde', kc * zeta[None, :, :, None], vc)
        return r, inner + cross

    to_chunks = lambda t: jnp.moveaxis(t.reshape(bsz, n_chunks, RET_CHUNK, h, t.shape[-1]), 1, 0)
    r, o = lax.scan(chunk, r0, (to_chunks(q), to_chunks(k), to_chunks(v)))
    return r, jnp.moveaxis(o, 0, 1).reshape(bsz, l, h, dv)

def odd_mixer(hc, hl, w_in, decay_logit, w_out, need_ctx):
    bsz = hl.shape[0]

    def proj(h, rope):
        u = h @ w_in
        q, k, v, g = jnp.split(u, 4, axis=-1)
        l = h.shape[1]
        hs = lambda t: t.astype(jnp.float32).reshape(bsz, l, RET_HEADS, RET_HEAD)
        q, k, v = hs(q), hs(k) * (RET_HEAD ** -0.5), hs(v)
        if rope:
            q, k = axial_rope(q), axial_rope(k)
        return q, k, v, g

    qc, kc, vc, gc = proj(hc, False)
    ql, kl, vl, gl = proj(hl, True)
    lg = jax.nn.log_sigmoid(decay_logit.astype(jnp.float32))
    zeros = jnp.zeros((bsz, RET_HEADS, RET_HEAD, RET_HEAD), jnp.float32)
    flip = lambda t: jnp.flip(t, axis=1)
    rc_f, oc_f = retention_scan(qc, kc, vc, lg[0], zeros, False)
    _, ol_f = retention_scan(ql, kl, vl, lg[0], rc_f, False)
    rc_b, oc_b = retention_scan(flip(qc), flip(kc), flip(vc), lg[1], zeros, True)
    _, ol_b = retention_scan(flip(ql), flip(kl), flip(vl), lg[1], rc_b, True)

    def finish(of, ob, g):
        o = of + flip(ob)
        o = o * lax.rsqrt(jnp.mean(o * o, axis=-1, keepdims=True) + EPS)
        o = o.reshape(o.shape[0], o.shape[1], RET_W).astype(g.dtype)
        return (o * jax.nn.silu(g)) @ w_out

    out_l = finish(ol_f, ol_b, gl)
    out_c = finish(oc_f, oc_b, gc) if need_ctx else None
    return out_c, out_l

def second_inputs(seed: int = 0) -> dict:
    key = jax.random.key(seed)
    ks = jax.random.split(key, 24)
    f32 = jnp.float32
    nrm = lambda k, shape, s: jax.random.normal(k, shape, f32) * s
    D = D_MODEL
    gam = 1.0 - 2.0 ** (-5.0 - jnp.arange(RET_HEADS, dtype=f32))
    return {
        'x': nrm(ks[0], (BATCH, SEQ, D), 1.0),
        'c': nrm(ks[1], (BATCH, D), 1.0),
        'ctx': nrm(ks[2], (BATCH, CTX_LEN, D), 1.0),
        'c_ctx': nrm(ks[3], (D,), 1.0),
        'ada_w': nrm(ks[4], (DEPTH, D, 3 * D), D ** -0.5),
        'ada_b': nrm(ks[5], (DEPTH, 3 * D), 0.02),
        'norm_pre': 1.0 + nrm(ks[6], (DEPTH, D), 0.05),
        'norm_post': 1.0 + nrm(ks[7], (DEPTH, D), 0.05),
        'ev_w_in': nrm(ks[8], (N_EVEN_2, D, EVEN_IN), D ** -0.5),
        'ev_mu': jax.random.uniform(ks[9], (N_EVEN_2, N_SHIFT), f32),
        'ev_w0': jax.random.uniform(ks[10], (N_EVEN_2, 2, RWKV_W), f32, -4.0, 0.5),
        'ev_w2': nrm(ks[11], (N_EVEN_2, 2, LORA_W, RWKV_W), 0.1 * LORA_W ** -0.5),
        'ev_a0': nrm(ks[12], (N_EVEN_2, 2, RWKV_W), 0.5),
        'ev_a2': nrm(ks[13], (N_EVEN_2, 2, LORA_A, RWKV_W), 0.1 * LORA_A ** -0.5),
        'ev_k_k': 0.85 + nrm(ks[14], (N_EVEN_2, RWKV_W), 0.05),
        'ev_k_a': 1.0 + nrm(ks[15], (N_EVEN_2, RWKV_W), 0.05),
        'ev_r_k': nrm(ks[16], (N_EVEN_2, RWKV_HEADS, RWKV_HEAD), 0.1),
        'ev_lnx_g': 1.0 + nrm(ks[17], (N_EVEN_2, RWKV_W), 0.05),
        'ev_lnx_b': nrm(ks[18], (N_EVEN_2, RWKV_W), 0.02),
        'ev_w_out': nrm(ks[19], (N_EVEN_2, MIX_W, D), MIX_W ** -0.5),
        'od_w_in': nrm(ks[20], (N_ODD_2, D, ODD_IN), D ** -0.5),
        'od_decay_logit': (jnp.log(gam) - jnp.log1p(-gam)) + nrm(ks[21], (N_ODD_2, 2, RET_HEADS), 0.1),
        'od_w_out': nrm(ks[22], (N_ODD_2, RET_W, D), RET_W ** -0.5),
    }

def second_block(x, c, ctx, c_ctx, ada_w, ada_b, norm_pre, norm_post, ev_w_in, ev_mu, ev_w0, ev_w2, ev_a0, ev_a2,
              ev_k_k, ev_k_a, ev_r_k, ev_lnx_g, ev_lnx_b, ev_w_out, od_w_in, od_decay_logit, od_w_out):
    rows = x.shape[1] // GRID_W
    xl, xc = x, ctx
    sc, scc = jax.nn.silu(c), jax.nn.silu(c_ctx)
    for layer in range(DEPTH):
        need_ctx = layer < DEPTH - 1
        shift_l, scale_l, gate_l = jnp.split(sc @ ada_w[layer] + ada_b[layer], 3, axis=-1)
        shift_c, scale_c, gate_c = jnp.split(scc @ ada_w[layer] + ada_b[layer], 3, axis=-1)
        hl = rmsnorm(xl, norm_pre[layer]) * (1.0 + scale_l[:, None, :]) + shift_l[:, None, :]
        hc = rmsnorm(xc, norm_pre[layer]) * (1.0 + scale_c) + shift_c
        if layer % 2 == 0:
            i = layer // 2
            oc, ol = even_mixer(hc, hl, rows, ev_w_in[i], ev_mu[i], ev_w0[i], ev_w2[i], ev_a0[i], ev_a2[i],
                                ev_k_k[i], ev_k_a[i], ev_r_k[i], ev_lnx_g[i], ev_lnx_b[i], ev_w_out[i], need_ctx)
        else:
            i = layer // 2
            oc, ol = odd_mixer(hc, hl, od_w_in[i], od_decay_logit[i], od_w_out[i], need_ctx)
        xl = xl + gate_l[:, None, :] * rmsnorm(ol, norm_post[layer])
        if need_ctx:
            xc = xc + gate_c * rmsnorm(oc, norm_post[layer])
    return xl


def setup_inputs(seed=0):
    out = dict(first_inputs(seed))
    for name, value in second_inputs(seed + 1).items():
        if name != "x":
            out[name + "_2"] = value
    return out


def reference(
    x, c, positions, ada_w, ada_b, ln_g, ln_b, ab_w_in, ab_w_out, hgrn_lb_raw, hgrn_norm_g,
    attn_sinks, pool_w, pool_scale, ffn_w_up, ffn_conv_w, ffn_conv_b, ffn_w_down, c_2, ctx_2,
    c_ctx_2, ada_w_2, ada_b_2, norm_pre_2, norm_post_2, ev_w_in_2, ev_mu_2, ev_w0_2, ev_w2_2,
    ev_a0_2, ev_a2_2, ev_k_k_2, ev_k_a_2, ev_r_k_2, ev_lnx_g_2, ev_lnx_b_2, ev_w_out_2,
    od_w_in_2, od_decay_logit_2, od_w_out_2,
):
    x = first_block(
        x, c, positions, ada_w, ada_b, ln_g, ln_b, ab_w_in, ab_w_out, hgrn_lb_raw, hgrn_norm_g,
        attn_sinks, pool_w, pool_scale, ffn_w_up, ffn_conv_w, ffn_conv_b, ffn_w_down,
    )
    return second_block(
        x, c_2, ctx_2, c_ctx_2, ada_w_2, ada_b_2, norm_pre_2, norm_post_2, ev_w_in_2, ev_mu_2,
        ev_w0_2, ev_w2_2, ev_a0_2, ev_a2_2, ev_k_k_2, ev_k_a_2, ev_r_k_2, ev_lnx_g_2,
        ev_lnx_b_2, ev_w_out_2, od_w_in_2, od_decay_logit_2, od_w_out_2,
    )


_drawn_inputs = setup_inputs


def setup_inputs(seed=0):
    import zlib

    import numpy as np

    out = dict(_drawn_inputs(seed))
    spreads = {}
    factors = {'hgrn_norm_g': 8.0,
     'attn_sinks': 8.0,
     'pool_scale': 8.0,
     'ffn_conv_b': 7.052,
     'ev_w2_2': 5.269,
     'ev_lnx_b_2': 4.407}
    for name, (base, spread) in spreads.items():
        noise = np.random.default_rng([zlib.crc32(name.encode()), seed]).standard_normal(out[name].shape)
        drawn = base * np.exp(spread * noise) if base else spread * noise
        out[name] = __import__('jax').numpy.asarray(drawn.astype(out[name].dtype))
    for name, factor in factors.items():
        out[name] = (out[name] * factor).astype(out[name].dtype)
    return out
```

```python
from contextlib import ExitStack
import math

import numpy as np
import concourse.bass as bass
from concourse import mybir

F32 = mybir.dt.float32
I32 = mybir.dt.int32
ALU = mybir.AluOpType
ACT = mybir.ActivationFunctionType
AX = mybir.AxisListType

P = 128
D = 1024
DT = D // P
T = 512
TC = 256
TA = T + TC
DEPTH = 2
FF = 2816
FT = FF // P
ALPHA = (2.0 * DEPTH) ** 0.25
LN_EPS, RMS_EPS, EPS, GN_EPS = 1e-5, 1e-6, 1e-6, 64e-5
ROPE_THETA, ROPE_BASE = 500000.0, 10000.0
AH = 4
BH, BD = 8, 64
RT = 6
RH = 8
GRID_W = 64
POOL_WINDOWS = (2, 4, 8, 16)
NSLOT = 2
SLOT = FT * P
CH = 128
LEVELS = 7

PARAMS = [
    ("c", 8), ("c2", 16),
    ("ada_b0", 48), ("ada_b1", 48), ("ada_b2_0", 24), ("ada_b2_1", 24),
    ("ln_g", 32), ("ln_b", 32), ("lb_raw", 4), ("norm_g", 1), ("sinks", 8), ("pool_scale", 8),
    ("conv0", 4 * FT), ("conv1", 4 * FT),
    ("norm_pre", 16), ("norm_post", 16),
    ("mu", 20), ("rw", 9 * RT),
    ("decay", 16),
]
CONSTS = [
    ("ident", P), ("ones", P), ("blk64", P), ("rope_perm", P), ("swap64", P),
    ("inv_freq", 1), ("rope_sign", 1), ("type4", 4), ("type2", 2),
    ("low", (LEVELS + 1) * P),
    ("up", (LEVELS + 1) * P),
    ("band", 256), ("pool_cnt", 4 * 16), ("scan_reset", TA),
    ("strict_low", P), ("strict_up", P), ("incl_low", P), ("incl_up", P), ("ident64", 64), ("top_ident", P),
]
CONSTS2 = [
    ("dist_f", P), ("dist_b", P), ("pos1", P), ("pos1r", P), ("zpos", 2),
    ("ax_cos", T), ("ax_sin", T),
]
DFT = [("c512", 4 * T), ("s512", 4 * T), ("c256", 2 * TC), ("s256", 2 * TC), ("f64", 2 * P)]


def offsets(items):
    at, out = 0, {}
    for name, n in items:
        out[name] = (at, n)
        at += n
    return out, at


P_AT, P_N = offsets(PARAMS)
C_AT, C_N = offsets(CONSTS)
C2_AT, C2_N = offsets(CONSTS2)
F_AT, F_N = offsets(DFT)


def constants():
    p = np.arange(P)
    t = {}
    t["ident"] = np.eye(P)
    t["ones"] = np.ones((P, P))
    t["blk64"] = (p[:, None] // 64 == p[None] // 64)
    perm = np.zeros((P, P))
    for m in range(P):
        if m % 64 < 8:
            perm[m + 8, m] = 1
        elif m % 64 < 16:
            perm[m - 8, m] = 1
    t["rope_perm"] = perm
    t["swap64"] = (p[:, None] == (p[None] + 64) % P)
    inv = ROPE_THETA ** (-np.arange(0, 16, 2) / 16.0)
    t["inv_freq"] = np.where(p % 64 < 16, inv[p % 8], 0.0)[:, None]
    t["rope_sign"] = np.where(p % 64 < 8, -1.0, 1.0)[:, None]
    t["type4"] = (p[:, None] % 4 == np.arange(4)[None])
    t["type2"] = (p[:, None] % 2 == np.arange(2)[None])
    low = np.zeros((P, LEVELS + 1, P))
    for m in range(LEVELS):
        n = 2 << m
        same = p[:, None] // n == p[None] // n
        low[:, m] = same & (p[:, None] % n >= n // 2) & (p[None] % n < n // 2)
    low[:, LEVELS] = np.eye(P)
    t["low"] = low.reshape(P, -1)
    t["up"] = low.transpose(2, 1, 0).reshape(P, -1)
    k = np.arange(256)
    rel = p[:, None] + 128 - k[None]
    t["band"] = np.where((rel >= 0) & (rel < 128), 0.0, -1e30)
    w = np.array(POOL_WINDOWS)[:, None]
    t["pool_cnt"] = np.broadcast_to((1.0 / np.minimum(np.arange(16)[None] + 1, w)).reshape(1, -1), (P, 64))
    t["scan_reset"] = np.broadcast_to((np.arange(TA) % CH != 0)[None], (P, TA))
    t["strict_low"] = p[:, None] > p[None]
    t["strict_up"] = p[:, None] < p[None]
    t["incl_low"] = p[:, None] >= p[None]
    t["incl_up"] = p[:, None] <= p[None]
    t["ident64"] = p[:, None] % 64 == np.arange(64)[None]
    t["top_ident"] = p[:, None] % 64 == p[None]
    c1 = np.concatenate([np.asarray(t[n], np.float32) for n, _ in CONSTS], 1)
    q = {}
    q["dist_f"] = np.maximum(p[None] - p[:, None], 0)
    q["dist_b"] = np.maximum(p[:, None] - p[None], 0)
    q["pos1"] = np.broadcast_to(p[None] + 1, (P, P))
    q["pos1r"] = np.broadcast_to(P - p[None], (P, P))
    q["zpos"] = np.stack([P - 1 - p, p], 1)
    rope = ROPE_BASE ** (-np.arange(0, 64, 2) / 64.0)
    pos = np.arange(T)
    rc = np.stack([pos // GRID_W, pos % GRID_W], 1)
    ang = (rc[:, :, None] * rope.astype(np.float32)).reshape(T, 64).T
    q["ax_cos"] = np.concatenate([np.cos(ang), np.cos(ang)])
    q["ax_sin"] = np.concatenate([-np.sin(ang), np.sin(ang)])
    c2 = np.concatenate([np.asarray(q[n], np.float32) for n, _ in CONSTS2], 1)
    f = {}
    for n, L in ((512, T), (256, TC)):
        a = 2 * np.pi * np.outer(np.arange(L), np.arange(L)) / L
        s = 1.0 / math.sqrt(L * 64)
        f[f"c{n}"] = (s * np.cos(a)).reshape(L // P, P, L).transpose(1, 0, 2).reshape(P, -1)
        f[f"s{n}"] = (-s * np.sin(a)).reshape(L // P, P, L).transpose(1, 0, 2).reshape(P, -1)
    a = 2 * np.pi * np.outer(np.arange(64), np.arange(64)) / 64
    z = np.zeros((64, 64))
    f["f64"] = np.concatenate([np.block([[g, z], [z, g]]) for g in (np.cos(a), np.sin(a))], 1)
    c3 = np.concatenate([np.asarray(f[n], np.float32) for n, _ in DFT], 1)
    return c1, c2, c3


class Queue:

    def __init__(self, eng, sem):
        self.eng, self.sem, self.n, self.seen = eng, sem, 0, {}

    def wait(self, *tokens):
        for sem, value in tokens:
            if self.seen.get(sem.num, 0) < value:
                self.eng.wait_ge(sem, value)
                self.seen[sem.num] = value

    def go(self, ins):
        ins.then_inc(self.sem, 1)
        self.n += 1
        return (self.sem, self.n)

    def wait_reg(self, sem, value, frees=None):
        self.eng.wait_ge(sem, value)
        nop = self.eng.nop()
        if frees is not None:
            nop.then_inc(frees, 1)


class Core:
    def __init__(self, nc, ctx, dram):
        self.nc, self.ctx, self.dram = nc, ctx, dram
        sems = [ctx.enter_context(nc.semaphore(n)) for n in (
            "pe_done", "dve_done", "act_done", "pool_done",
            "mm_a", "mm_b", "free_a", "free_b", "loop_1", "loop_2", "loop_3", "loop_4", "chain", "loads")]
        self.cleared = range(sems[0].num, sems[-1].num + 1)
        assert [s.num for s in sems] == list(self.cleared)
        self.pe = Queue(nc.tensor, sems[0])
        self.dve = Queue(nc.vector, sems[1])
        self.act = Queue(nc.scalar, sems[2])
        self.pool = Queue(nc.gpsimd, sems[3])
        (self.mm_a, self.mm_b, self.free_a, self.free_b, self.l1, self.l2, self.l3, self.l4,
         self.chain, self.loads) = sems[4:]
        self.n_loads = 0
        self.full = [ctx.enter_context(nc.semaphore(f"slot_full{i}")) for i in range(NSLOT)]
        self.free = [ctx.enter_context(nc.semaphore(f"slot_free{i}")) for i in range(NSLOT)]
        self.ring = self.sb("ring", [P, NSLOT, SLOT])
        self.slab = 0
        self.ps = ctx.enter_context(nc.psum_tensor("ps", [P, 8, 512], F32))
        for s in self.free:
            nc.sync.sem_inc(s, 1)

    def sb(self, name, shape, ctx=None, dt=F32):
        return (ctx or self.ctx).enter_context(self.nc.sbuf_tensor(name, shape, dt))

    def phase_end(self):
        assert self.n_loads == 0
        self.nc.multi_engine_barrier([q.eng.engine for q in (self.pe, self.dve, self.act, self.pool)],
                                     sems_to_clear=self.cleared)
        for q in (self.pe, self.dve, self.act, self.pool):
            q.n, q.seen = 0, {}

    def load(self, out, in_, *after):
        self.act.wait(*after)
        self.nc.scalar.dma_start(out, in_).then_inc(self.loads, 16)
        self.n_loads += 16
        return (self.loads, self.n_loads)

    def loaded(self, q, token):
        q.wait((self.loads, self.n_loads))

    def fetch(self, src, kt, width, i=0, per=0):
        slot, use = self.slab % NSLOT, self.slab // NSLOT
        self.nc.sync.wait_ge(self.free[slot], use + 1 + i * per)
        self.nc.sync.dma_start(self.ring[:, slot, 0:kt * width], src).then_inc(self.full[slot], 16)

    def slab_view(self, kt, width):
        return self.ring[:, self.slab % NSLOT, 0:kt * width].rearrange("p (k n) -> p k n", k=kt)

    def slab_wait(self, i=0, per=0):
        slot, use = self.slab % NSLOT, self.slab // NSLOT
        self.nc.tensor.wait_ge(self.full[slot], 16 * (use + 1) + i * (16 * per))
        if per:
            self.nc.tensor.nop()

    def slab_next(self):
        self.slab += 1
        return self.free[(self.slab - 1) % NSLOT]

    def slab_loop(self, iters):
        self.slab += NSLOT * (iters - 1)


def dense_fm(k, name, slabs, rhs, splits, evac, kt=8, tiles=2, first=0, end=True):
    nc, pe = k.nc, k.pe
    w = k.dram[name]
    nb = len(splits)
    per_iter = NSLOT * tiles
    assert per_iter * nb <= 8
    nc.vector.sem_inc(k.free_a, per_iter)

    def body(i, n_slabs, per):
        k.chain_n = 0
        for s in range(n_slabs):
            k.fetch(w[first + i * NSLOT + s], kt, tiles * P, i * per, 1)
            k.slab_wait(i * per, 1)
            wv = k.slab_view(kt, tiles * P)
            slot = k.slab_next()
            for a in range(tiles):
                g = s * tiles + a
                pe.wait_reg(k.free_a, i * per_iter + g + 1)
                for b, (t0, tn) in enumerate(splits):
                    for kk in range(kt):
                        mm = nc.tensor.matmul(k.ps[:, g * nb + b, 0:tn], wv[:, kk, a * P:(a + 1) * P],
                                              rhs[:, kk, t0:t0 + tn], start=(kk == 0), stop=(kk == kt - 1))
                mm.then_inc(k.mm_a, 1)
                k.dve.wait_reg(k.mm_a, i * per_iter + g + 1, slot if a == tiles - 1 else None)
                evac(i * per_iter + g, [k.ps[:, g * nb + b, 0:tn] for b, (_, tn) in enumerate(splits)])\
                    .then_inc(k.free_a, 1)
        if k.chain_n:
            nc.vector.wait_ge(k.chain, k.chain_n)
            nc.vector.nop()
            nc.vector.sem_clear(k.chain)

    iters = slabs // NSLOT
    if iters:
        with nc.Fori(0, iters) as i:
            body(i, NSLOT, 1)
        k.slab_loop(iters)
    if slabs % NSLOT:
        body(iters, 1, 0)
    if end:
        k.phase_end()


def chained(k, ins):
    k.chain_n += 1
    ins.then_inc(k.chain, 1)
    k.nc.vector.wait_ge(k.chain, k.chain_n)
    k.nc.vector.nop()


def ada(k, name, slabs, c, n, out, bias):
    nc, pe = k.nc, k.pe
    per_iter = 2 * NSLOT
    nc.vector.sem_inc(k.free_a, NSLOT)
    with nc.Fori(0, slabs // NSLOT) as i:
        for s in range(NSLOT):
            k.fetch(k.dram[name][i * NSLOT + s], DT, 2 * P, i, 1)
            k.slab_wait(i, 1)
            wv = k.slab_view(DT, 2 * P)
            slot = k.slab_next()
            pe.wait_reg(k.free_a, i * NSLOT + s + 1)
            for a in range(2):
                for kk in range(DT):
                    mm = nc.tensor.matmul(k.ps[:, s, a * n:(a + 1) * n], wv[:, kk, a * P:(a + 1) * P],
                                          c[:, kk, :], start=(kk == 0), stop=(kk == DT - 1))
            mm.then_inc(k.mm_a, 1)
            k.dve.wait_reg(k.mm_a, i * NSLOT + s + 1, slot)
            at = i * per_iter + 2 * s
            b = bias[:, bass.ds(at, 2)]
            o = out[:, bass.ds(at, 2), :]
            nc.vector.tensor_tensor(o, k.ps[:, s, 0:2 * n].rearrange("p (a n) -> p a n", n=n),
                                    b.unsqueeze(2).broadcast_to([P, 2, n]), ALU.add).then_inc(k.free_a, 1)
    k.slab_loop(slabs // NSLOT)
    k.phase_end()


def layer_norm(k, ctx, R, eps, outs, what):
    nc, pe, dve, act = k.nc, k.pe, k.dve, k.act
    sq = k.sb("ln_sq_" + what, [P, DT, T], ctx)
    mu = k.sb("ln_mu_" + what, [P, T], ctx)
    rs = k.sb("ln_rs_" + what, [P, T], ctx)
    for kk in range(DT):
        mm = nc.tensor.matmul(k.ps[:, 0, :], k.ones, R[:, kk, :], start=(kk == 0), stop=(kk == DT - 1))
    t_sum = pe.go(mm)
    dve.wait(t_sum)
    dve.wait(dve.go(nc.vector.tensor_scalar(mu[:], k.ps[:, 0, :], 1.0 / D, None, ALU.mult)))
    half = DT // 2
    for j in range(2):
        r = R[:, j * half:(j + 1) * half, :]
        t_sub = dve.go(nc.vector.tensor_tensor(r, r, mu[:].unsqueeze(1).broadcast_to([P, half, T]), ALU.subtract))
        act.wait(t_sub)
        t_sq = act.go(nc.scalar.activation(sq[:, j * half:(j + 1) * half, :], r, ACT.Square))
        pe.wait(t_sq)
        for kk in range(j * half, (j + 1) * half):
            mm = nc.tensor.matmul(k.ps[:, 1, :], k.ones, sq[:, kk, :], start=(kk == 0), stop=(kk == DT - 1))
    t_var = pe.go(mm)
    rstd(k, rs[:], k.ps[:, 1, :], 1.0 / D, eps, t_var)
    for j in range(2):
        r = R[:, j * half:(j + 1) * half, :]
        t_n = dve.go(nc.vector.tensor_tensor(r, r, rs[:].unsqueeze(1).broadcast_to([P, half, T]), ALU.mult))
        for q, dst, scale, bias in outs:
            q.wait(t_n)
            for kk in range(j * half, (j + 1) * half):
                affine(q, dst[:, kk, :], R[:, kk, :], scale[:, kk:kk + 1], bias[:, kk:kk + 1])


def affine(q, out, x, scale, bias):
    if hasattr(q.eng, "activation"):
        return q.go(q.eng.activation(out, x, ACT.Identity, bias=bias, scale=scale))
    return q.go(q.eng.tensor_scalar(out, x, scale, bias, ALU.mult, ALU.add))


def rstd(k, out, x, scale, eps, token):
    nc, dve, act = k.nc, k.dve, k.act
    dve.wait(token)
    t = dve.go(nc.vector.tensor_scalar(out, x, scale, eps, ALU.mult, ALU.add))
    act.wait(t)
    t = act.go(nc.scalar.activation(out, out, ACT.Sqrt))
    dve.wait(t)
    t = dve.go(nc.vector.reciprocal(out, out))
    dve.wait(t)
    return t


def transpose_fp32(k, out, x):
    return k.nc.tensor.transpose(out, x, k.ident)


def setup(k):
    nc, act, dve = k.nc, k.act, k.dve
    k.par = k.sb("params_sb", [P, P_N])
    k.cst = k.sb("consts_sb", [P, C_N])
    k.XA = k.sb("XA", [P, DT, T])
    k.H = k.sb("H", [P, DT, TA])
    k.MOD = [k.sb("mod0", [P, 48, 1]), k.sb("mod1", [P, 48, 1])]
    k.sc = k.sb("scalars", [P, 8, 8])
    k.p = lambda name, a=0, n=None: k.par[:, P_AT[name][0] + a:P_AT[name][0] + a + (P_AT[name][1] - a if n is None else n)]
    k.c = lambda name, a=0, n=None: k.cst[:, C_AT[name][0] + a:C_AT[name][0] + a + (C_AT[name][1] - a if n is None else n)]
    k.ident, k.ones = k.c("ident"), k.c("ones")
    k.load(k.par[:], k.dram["params"])
    k.load(k.cst[:], k.dram["consts"])
    t = k.load(k.XA[:], k.dram["x"])
    k.loaded(act, t)
    k.loaded(dve, t)
    k.loaded(k.pe, t)
    k.loaded(k.pool, t)
    for name in ("c", "c2"):
        act.go(nc.scalar.activation(k.p(name), k.p(name), ACT.Silu))
    k.n_loads = 0
    k.phase_end()


def block1_input(k, ctx, l, scale_only=False):
    nc, dve, act, pool = k.nc, k.dve, k.act, k.pool
    m = k.MOD[l]
    one_sc = k.sc[:, 0, :]
    t = dve.go(nc.vector.tensor_scalar(one_sc, m[:, 8:16, 0], 1.0, None, ALU.add))
    act.wait(t)
    for kk in range(DT):
        t = affine(act, k.H[:, kk, 0:T], k.XA[:, kk, :], one_sc[:, kk:kk + 1], m[:, kk, :])
        dve.wait(t)
        dve.go(nc.vector.tensor_scalar(k.XA[:, kk, :], k.XA[:, kk, :], ALPHA, None, ALU.mult))
    k.phase_end()


def ln_scalars(k, l, i, sh, sc, final=False):
    nc, dve = k.nc, k.dve
    g, b = k.p("ln_g", (2 * l + i) * 8, 8), k.p("ln_b", (2 * l + i) * 8, 8)
    if final:
        return g, b, None, None
    ga, ba, gh, bh = (k.sc[:, j, :] for j in range(1, 5))
    dve.go(nc.vector.tensor_scalar(ga, g, ALPHA, None, ALU.mult))
    dve.go(nc.vector.tensor_scalar(ba, b, ALPHA, None, ALU.mult))
    t = dve.go(nc.vector.tensor_scalar(bh, sc, 1.0, None, ALU.add))
    dve.wait(t)
    dve.wait(dve.go(nc.vector.tensor_tensor(gh, g, bh, ALU.mult)))
    dve.wait(dve.go(nc.vector.tensor_tensor(bh, b, bh, ALU.mult)))
    dve.wait(dve.go(nc.vector.tensor_tensor(bh, bh, sh, ALU.add)))
    return ga, ba, gh, bh


def residual_norm(k, R, l, i):
    m = k.MOD
    with ExitStack() as ctx:
        if i == 0:
            ga, ba, gh, bh = ln_scalars(k, l, 0, m[l][:, 24:32, 0], m[l][:, 32:40, 0])
        elif l + 1 < DEPTH:
            ga, ba, gh, bh = ln_scalars(k, l, 1, m[l + 1][:, 0:8, 0], m[l + 1][:, 8:16, 0])
        else:
            ga, ba, gh, bh = ln_scalars(k, l, 1, None, None, final=True)
        outs = [(k.act, k.H[:, :, 0:T], gh, bh), (k.pool, k.XA, ga, ba)]
        if gh is None:
            outs = [(k.act, k.XA, ga, ba)]
        layer_norm(k, ctx, R, LN_EPS, outs, f"{l}{i}")
        k.phase_end()


def ffn(k, l, R):
    nc, pe, dve, act = k.nc, k.pe, k.dve, k.act
    with ExitStack() as ctx:
        G = k.sb(f"G{l}", [P, FT, T], ctx)
        U = k.sb(f"U{l}", [P, NSLOT, T + 2], ctx)
        C = k.sb(f"C{l}", [P, NSLOT, T], ctx)
        cw = k.p(f"conv{l}")
        dve.go(nc.vector.memset(U[:, :, 0:2], 0.0))
        for s in (k.free_a, k.free_b, k.l2):
            nc.vector.sem_inc(s, NSLOT)
        k.phase_end_keep()
        with nc.Fori(0, FT // NSLOT) as i:
            for s in range(NSLOT):
                n = i * NSLOT + s
                k.fetch(k.dram[f"w_up{l}"][i * NSLOT + s], DT, 2 * P, i, 1)
                k.slab_wait(i, 1)
                wv = k.slab_view(DT, 2 * P)
                slot = k.slab_next()
                pu, pv = k.ps[:, 2 * s, :], k.ps[:, 2 * s + 1, :]
                pe.wait_reg(k.free_a, n + 1)
                for kk in range(DT):
                    mm = nc.tensor.matmul(pu, wv[:, kk, 0:P], k.H[:, kk, 0:T], start=(kk == 0), stop=(kk == DT - 1))
                mm.then_inc(k.mm_a, 1)
                pe.wait_reg(k.free_b, n + 1)
                for kk in range(DT):
                    mm = nc.tensor.matmul(pv, wv[:, kk, P:2 * P], k.H[:, kk, 0:T], start=(kk == 0), stop=(kk == DT - 1))
                mm.then_inc(k.mm_b, 1)
                act.wait_reg(k.mm_a, n + 1)
                act.wait_reg(k.l2, n + 1)
                nc.scalar.copy(U[:, s, 2:T + 2], pu).then_inc(k.free_a, 1)
                dve.wait_reg(k.free_a, n + 1 + NSLOT)
                w = lambda j: cw[:, bass.ds(4 * n + j, 1)]
                dve.eng.tensor_scalar(C[:, s, :], U[:, s, 2:T + 2], w(2), w(3), ALU.mult, ALU.add).then_inc(k.chain, 1)
                dve.eng.wait_ge(k.chain, 2 * s + 1)
                dve.eng.nop()
                dve.eng.scalar_tensor_tensor(C[:, s, :], U[:, s, 1:T + 1], w(1), C[:, s, :], ALU.mult, ALU.add).then_inc(k.chain, 1)
                dve.eng.wait_ge(k.chain, 2 * s + 2)
                dve.eng.nop()
                dve.eng.scalar_tensor_tensor(C[:, s, :], U[:, s, 0:T], w(0), C[:, s, :], ALU.mult, ALU.add).then_inc(k.l2, 1)
                act.wait_reg(k.l2, n + 1 + NSLOT)
                nc.scalar.activation(C[:, s, :], C[:, s, :], ACT.Silu).then_inc(k.l3, 1)
                dve.wait_reg(k.l3, n + 1)
                dve.wait_reg(k.mm_b, n + 1, slot)
                dve.eng.tensor_tensor(G[:, bass.ds(n, 1), :].rearrange("p a t -> p (a t)"), C[:, s, :], pv, ALU.mult).then_inc(k.free_b, 1)
            nc.vector.sem_clear(k.chain)
        k.slab_loop(FT // NSLOT)
        k.phase_end()
        g2 = k.MOD[l][:, 40:48, 0]

        def evac(n, banks):
            return nc.vector.scalar_tensor_tensor(
                R[:, bass.ds(n, 1), :].rearrange("p a t -> p (a t)"), banks[0], g2[:, bass.ds(n, 1)],
                k.XA[:, bass.ds(n, 1), :].rearrange("p a t -> p (a t)"), ALU.mult, ALU.add)
        dense_fm(k, f"w_down{l}", 8, G, [(0, T)], evac, kt=FT, tiles=1)


def phase_end_keep(self):
    self.nc.multi_engine_barrier([q.eng.engine for q in (self.pe, self.dve, self.act, self.pool)],
                                 sems_to_clear=range(self.pe.sem.num, self.pool.sem.num + 1))
    for q in (self.pe, self.dve, self.act, self.pool):
        q.n, q.seen = 0, {}


Core.phase_end_keep = phase_end_keep


def tile_of(buf, n):
    return buf[:, bass.ds(n, 1), :].rearrange("p a t -> p (a t)")


def sincos(k, ctx, COS, SIN):
    nc, dve, act = k.nc, k.dve, k.act
    pos = k.sb("pos_i", [P, T], ctx, I32)
    ang = k.sb("ang", [P, T], ctx)
    n = k.sb("turns", [P, T], ctx)
    t = k.load(pos[:], k.dram["positions"].partition_broadcast(P))
    k.loaded(dve, t)
    v = nc.vector

    def step(ins):
        t = dve.go(ins)
        dve.wait(t)
        return t
    step(v.tensor_copy(ang[:], pos[:]))
    step(v.tensor_scalar(ang[:], ang[:], k.c("inv_freq"), None, ALU.mult))
    magic = 1.5 * 2.0 ** 23
    step(v.tensor_scalar(n[:], ang[:], 1.0 / (2 * math.pi), magic, ALU.mult, ALU.add))
    step(v.tensor_scalar(n[:], n[:], magic, None, ALU.subtract))
    c1 = 6.28125
    c2 = math.floor((2 * math.pi - c1) * 2 ** 22) / 2 ** 22
    c3 = 2 * math.pi - c1 - c2
    for c in (c1, c2, c3):
        step(v.scalar_tensor_tensor(ang[:], n[:], -c, ang[:], ALU.mult, ALU.add))
    top = 3.1415925
    step(v.tensor_scalar(ang[:], ang[:], top, -top, ALU.min, ALU.max))
    step(v.tensor_scalar(COS[:], ang[:], math.pi / 2, None, ALU.add))
    step(v.tensor_scalar(n[:], COS[:], math.pi, -2 * math.pi, ALU.is_gt, ALU.mult))
    step(v.tensor_tensor(COS[:], COS[:], n[:], ALU.add))
    t = step(v.tensor_scalar(COS[:], COS[:], top, -top, ALU.min, ALU.max))
    act.wait(t)
    act.go(nc.scalar.activation(COS[:], COS[:], ACT.Sin))
    t = act.go(nc.scalar.activation(SIN[:], ang[:], ACT.Sin))
    dve.wait(t)
    step(v.tensor_scalar(SIN[:], SIN[:], k.c("rope_sign"), None, ALU.mult))


def even_mixer1(k, R):
    nc, pe, dve, act, pool = k.nc, k.pe, k.dve, k.act, k.pool
    v = nc.vector
    with ExitStack() as ctx:
        Z = k.sb("Z", [P, 17, T], ctx)
        VA = k.sb("VA", [P, 4, 512], ctx)
        VB = k.sb("VB", [P, 4, P], ctx)
        dense_fm(k, "ab_in", 8, k.H, [(0, T)], lambda n, banks: v.tensor_copy(tile_of(Z, n), banks[0]))
        w = k.dram["ab_in"]
        for s in range(3):
            k.fetch(w[8 + s], DT, 2 * P)
            k.slab_wait()
            wv = k.slab_view(DT, 2 * P)
            slot = k.slab_next()
            if s == 0:
                for kk in range(DT):
                    mm = nc.tensor.matmul(k.ps[:, 0, :], wv[:, kk, 0:P], k.H[:, kk, 0:T], start=(kk == 0), stop=(kk == DT - 1))
                t_k = pe.go(mm)
                act.wait(t_k)
                t_copied = act.go(nc.scalar.copy(Z[:, 16, :], k.ps[:, 0, :]))
                t_read = []
            lo, hi = (P, 2 * P) if s == 0 else (0, 2 * P)
            for t in range(4):
                bank = k.ps[:, (4 * (s + 1) + t) % 8, 0:hi - lo]
                if s == 1 and t == 0:
                    pe.wait(t_copied)
                if s == 2:
                    pe.wait(t_read[t])
                for kk in range(DT):
                    mm = nc.tensor.matmul(bank, k.H[:, kk, t * P:(t + 1) * P], wv[:, kk, lo:hi], start=(kk == 0), stop=(kk == DT - 1))
                t_v = pe.go(mm)
                dve.wait(t_v)
                dst = VB[:, t, :] if s == 0 else VA[:, t, (s - 1) * 256:s * 256]
                t_read.append(dve.go(v.tensor_copy(dst, bank)))
            dve.eng.nop().then_inc(slot, 1)
        k.phase_end()
        OA = k.H[:, 0:4, 0:T]
        hgrn(k, Z, VA, OA)
        OB = k.H[:, 4:8, 0:T]
        attention(k, Z, VB, OB)
    g1 = k.MOD[0][:, 16:24, 0]
    dense_fm(k, "ab_out", 4, k.H, [(0, T)], lambda n, banks: v.scalar_tensor_tensor(
        tile_of(R, n), banks[0], g1[:, bass.ds(n, 1)], tile_of(k.XA, n), ALU.mult, ALU.add))


def hgrn(k, Z, VA, OA):
    nc, pe, dve, act, pool = k.nc, k.pe, k.dve, k.act, k.pool
    v = nc.vector
    NCH = T // CH
    with ExitStack() as ctx:
        B = k.sb("B", [P, AH, T], ctx)
        K = k.sb("K", [P, AH, T], ctx)
        E = k.sb("E", [P, AH, T], ctx)
        S = k.sb("S", [P, 2, AH, P], ctx)
        ATT = k.sb("ATT", [P, AH, T], ctx)
        KT = k.sb("KT", [P, AH, T], ctx)
        lbs = k.sb("lbs", [P, 3, AH], ctx)
        q, fz, ag = Z[:, 0:4, :], Z[:, 4:8, :], Z[:, 8:12, :]

        def step(ins):
            t = dve.go(ins)
            dve.wait(t)
            return t
        raw, lb, one = k.p("lb_raw"), lbs[:, 0, :], lbs[:, 1, :]
        step(v.tensor_tensor(lb, raw, raw, ALU.subtract))
        act.wait(dve.go(v.memset(lbs[:, 2, :], 0.0)))
        t = act.go(nc.scalar.activation(one, lb, ACT.Exp))
        dve.wait(t)
        step(v.reciprocal(lbs[:, 2, :], one))
        step(v.tensor_tensor(one, one, lbs[:, 2, :], ALU.mult))
        step(v.tensor_tensor(lb, one, one, ALU.subtract))
        step(v.tensor_scalar(one, lb, -1.0, 1.0, ALU.mult, ALU.add))
        act.go(nc.scalar.activation(K[:], fz, ACT.Sigmoid, scale=-1.0))
        t = act.go(nc.scalar.activation(B[:], fz, ACT.Sigmoid))
        dve.wait(t)
        for h in range(AH):
            dve.go(v.tensor_scalar(K[:, h, :], K[:, h, :], one[:, h:h + 1], None, ALU.mult))
            dve.go(v.tensor_scalar(B[:, h, :], B[:, h, :], one[:, h:h + 1], lb[:, h:h + 1], ALU.mult, ALU.add))
        t = (dve.sem, dve.n)
        dve.wait(t)
        t = step(v.tensor_scalar(B[:], B[:], 2.0 ** -63, None, ALU.max))
        act.wait(t)
        t = act.go(nc.scalar.activation(E[:], B[:], ACT.Ln))
        dve.wait(t)
        for h in range(AH):
            t = dve.go(v.tensor_tensor_scan(B[:, h, :], k.c("scan_reset", 0, T), E[:, h, :], 0.0, ALU.mult, ALU.add))
        dve.wait(t)
        t_scores = None
        for m in range(LEVELS + 1):
            if m < LEVELS:
                half = 1 << m
                vw = lambda a: a.rearrange("p h (b s j) -> p (h b) s j", s=2, j=half)
                nb = AH * T // (2 * half)
                b4, e4 = vw(B[:]), vw(E[:])
                mid = b4[:, :, 0, half - 1:half].broadcast_to([P, nb, half])
                if t_scores is not None:
                    dve.wait(t_scores)
                dve.go(v.tensor_tensor(e4[:, :, 1, :], b4[:, :, 1, :], mid, ALU.subtract))
                t = dve.go(v.tensor_tensor(e4[:, :, 0, :], mid, b4[:, :, 0, :], ALU.subtract))
                act.wait(t)
                t = act.go(nc.scalar.activation(E[:], E[:], ACT.Exp))
                dve.wait(t)
                dve.go(v.tensor_tensor(e4[:, :, 1, :], e4[:, :, 1, :], vw(q)[:, :, 1, :], ALU.mult))
                t = dve.go(v.tensor_tensor(e4[:, :, 0, :], e4[:, :, 0, :], vw(K[:])[:, :, 0, :], ALU.mult))
                lhs, rhs = E, E
            else:
                lhs, rhs = K, q
            pe.wait(t)
            base = 4 * (m % 2)
            if m >= 2:
                pe.wait(t_copied[m % 2])
            for h in range(AH):
                for c in range(NCH):
                    a = slice(c * CH, (c + 1) * CH)
                    mm = nc.tensor.matmul(k.ps[:, base + h, a], lhs[:, h, a], rhs[:, h, a], start=True, stop=True)
            t_scores = pe.go(mm)
            dve.wait(t_scores)
            scores = k.ps[:, base:base + AH, :].rearrange("p h (c t) -> p (h c) t", t=CH)
            out = ATT[:].rearrange("p h (c t) -> p (h c) t", t=CH)
            mask = k.c("up", m * P, P).unsqueeze(1).broadcast_to([P, AH * NCH, CH])
            if m == 0:
                tok = dve.go(v.tensor_tensor(out, scores, mask, ALU.mult))
                t_copied = [tok, None]
            else:
                dve.wait(tok)
                tok = dve.go(v.copy_predicated(out, mask.bitcast(I32), scores))
                t_copied[m % 2] = tok
        b4 = B[:].rearrange("p h (c t) -> p (h c) t", t=CH)
        e4 = E[:].rearrange("p h (c t) -> p (h c) t", t=CH)
        last = b4[:, :, CH - 1:CH].broadcast_to([P, AH * NCH, CH])
        t = dve.go(v.tensor_tensor(e4, last, b4, ALU.subtract))
        act.wait(t)
        t = act.go(nc.scalar.activation(E[:], E[:], ACT.Exp))
        dve.wait(t)
        t = step(v.tensor_tensor(E[:], E[:], K[:], ALU.mult))
        pe.wait(t, *[x for x in t_copied if x])
        for h in range(AH):
            for c in range(NCH):
                a = slice(c * CH, (c + 1) * CH)
                mm = nc.tensor.transpose(k.ps[:, h, a], E[:, h, a], k.ident)
        t = pe.go(mm)
        act.wait(t)
        t_kt = act.go(nc.scalar.copy(KT[:], k.ps[:, 0:4, :]))
        t = act.go(nc.scalar.activation(B[:], B[:], ACT.Exp))
        dve.wait(t)
        t_q = dve.go(v.tensor_tensor(K[:], B[:], q, ALU.mult))
        pe.wait(t_kt)
        for c in range(NCH - 1):
            for h in range(AH):
                mm = nc.tensor.matmul(k.ps[:, 4 + c, h * P:(h + 1) * P], KT[:, h, c * CH:(c + 1) * CH],
                                      VA[:, c, h * P:(h + 1) * P], start=True, stop=True)
        t_kv = pe.go(mm)
        dve.wait(t_kv)
        pe.wait(t_q)
        t_o = None
        for c in range(NCH):
            for h in range(AH):
                o = k.ps[:, h, c * CH:(c + 1) * CH]
                mm = nc.tensor.matmul(o, VA[:, c, h * P:(h + 1) * P], ATT[:, h, c * CH:(c + 1) * CH], start=True, stop=(c == 0))
                if c > 0:
                    pe.wait(t_state)
                    mm = nc.tensor.matmul(o, S[:, c % 2, h, :], K[:, h, c * CH:(c + 1) * CH], start=False, stop=True)
            t_o = pe.go(mm)
            if c + 1 < NCH:
                if c == 0:
                    t_state = dve.go(v.tensor_copy(S[:, 1, :, :], k.ps[:, 4, :].rearrange("p (h d) -> p h d", h=AH)))
                else:
                    dve.wait(t_state, t_prev_o)
                    for h in range(AH):
                        end = B[:, h, (c + 1) * CH - 1:(c + 1) * CH]
                        t_state = dve.go(v.scalar_tensor_tensor(S[:, (c + 1) % 2, h, :], S[:, c % 2, h, :], end,
                                                                k.ps[:, 4 + c, h * P:(h + 1) * P], ALU.mult, ALU.add))
            t_prev_o = t_o
        act.wait(t_o)
        t = act.go(nc.scalar.copy(ATT[:], k.ps[:, 0:4, :]))
        t = act.go(nc.scalar.activation(E[:], k.ps[:, 0:4, :], ACT.Square))
        pe.wait(t)
        dve.wait(t)
        for h in range(AH):
            mm = nc.tensor.matmul(k.ps[:, 4 + h, :], k.ones, E[:, h, :], start=True, stop=True)
        t = pe.go(mm)
        t_n = rstd(k, B[:], k.ps[:, 4:8, :], 1.0 / CH, RMS_EPS, t)
        t_s = act.go(nc.scalar.activation(K[:], ag, ACT.Silu))
        step(v.scalar_tensor_tensor(flat(ATT[:]), flat(ATT[:]), k.p("norm_g"), flat(B[:]), ALU.mult, ALU.mult))
        dve.wait(t_s)
        dve.go(v.tensor_tensor(OA, ATT[:], K[:], ALU.mult))
        k.phase_end()


def flat(a):
    return a.rearrange("p a t -> p (a t)")


def attention(k, Z, VB, OB):
    nc, pe, dve, act = k.nc, k.pe, k.dve, k.act
    v = nc.vector
    NB = T // P
    with ExitStack() as ctx:
        COS, SIN = k.sb("COS", [P, T], ctx), k.sb("SIN", [P, T], ctx)
        with ExitStack() as inner:
            sincos(k, inner, COS, SIN)
            k.n_loads = 0
            k.phase_end()
        ROT = k.sb("ROT", [P, 2, T], ctx)
        tok = [None, None]
        for j in range(5):
            x = Z[:, 12 + j, :]
            if tok[j % 2]:
                pe.wait(tok[j % 2])
            t = pe.go(nc.tensor.matmul(k.ps[:, j % 2, :], k.c("rope_perm"), x, start=True, stop=True))
            dve.wait(t)
            tok[j % 2] = dve.go(v.tensor_tensor(ROT[:, j % 2, :], k.ps[:, j % 2, :], SIN[:], ALU.mult))
            t = dve.go(v.tensor_tensor(x, x, COS[:], ALU.mult))
            dve.wait(tok[j % 2], t)
            t_rope = dve.go(v.tensor_tensor(x, x, ROT[:, j % 2, :], ALU.add))
        k.phase_end()
        S = k.sb("scores", [P, BH, 256], ctx)
        PT = k.sb("probs_T", [P, 2 * BH, P], ctx)
        st = k.sb("stats", [P, 4, BH], ctx)
        sink = k.p("sinks")
        for b in range(NB):
            ks = 0 if b else P
            w = 256 - ks
            for g in range(BH):
                j, r = g % 4, g // 4
                rows = slice(64 * r, 64 * r + 64)
                mm = nc.tensor.matmul(k.ps[:, g // 2, (g % 2) * 256 + ks:(g % 2 + 1) * 256],
                                      Z[rows, 12 + j, b * P:(b + 1) * P],
                                      Z[rows, 16, (b - 1) * P + ks:(b + 1) * P], start=True, stop=True)
            t_s = pe.go(mm)
            sc = k.ps[:, 0:4, :].rearrange("p j (r k) -> p (j r) k", r=2)[:, :, ks:256]
            s = S[:, :, ks:256]
            band = k.c("band")[:, ks:256].unsqueeze(1).broadcast_to([P, BH, w])
            m, neg, den = st[:, 0, :], st[:, 1, :], st[:, 2, :]

            def step(ins):
                t = dve.go(ins)
                dve.wait(t)
                return t
            dve.wait(t_s)
            step(v.scalar_tensor_tensor(s, sc, BD ** -0.5, band, ALU.mult, ALU.add))
            step(v.tensor_reduce(m, s, AX.X, ALU.max))
            step(v.tensor_tensor(m, m, sink, ALU.max))
            t_d = step(v.tensor_tensor(neg, sink, m, ALU.subtract))
            t_m = step(v.tensor_tensor(s, s, m.unsqueeze(2).broadcast_to([P, BH, w]), ALU.subtract))
            act.wait(t_m)
            act.go(nc.scalar.activation(neg, neg, ACT.Exp))
            t_e = act.go(nc.scalar.activation(s, s, ACT.Exp))
            dve.wait(t_e)
            step(v.tensor_reduce(den, s, AX.X, ALU.add))
            step(v.tensor_tensor(den, den, neg, ALU.add))
            step(v.reciprocal(den, den))
            t_p = step(v.tensor_tensor(s, s, den.unsqueeze(2).broadcast_to([P, BH, w]), ALU.mult))
            pe.wait(t_p)
            if b:
                pe.wait(t_pt)
            for g in range(BH):
                for e in range(2 if b else 1):
                    e = e if b else 1
                    mm = nc.tensor.transpose(k.ps[:, 4 + g // 2, ((g % 2) * 2 + e) * P:((g % 2) * 2 + e + 1) * P],
                                             S[:, g, e * P:(e + 1) * P], k.ident)
            t_t = pe.go(mm)
            act.wait(t_t)
            e0 = 0 if b else 1
            src = k.ps[:, 4:8, :].rearrange("p a (g e k) -> p (a g) e k", g=2, e=2)[:, :, e0:2, :]
            dst = PT[:].rearrange("p (g e) k -> p g e k", e=2)[:, :, e0:2, :]
            t_pt = act.go(nc.scalar.copy(dst, src))
            pe.wait(t_pt)
            for j in range(4):
                for r in range(2):
                    g = 4 * r + j
                    for e in range(e0, 2):
                        mm = nc.tensor.matmul(k.ps[64 * r:64 * r + 64, 0, j * P:(j + 1) * P],
                                              VB[:, b - 1 + e, 64 * r:64 * r + 64], PT[:, 2 * g + e, :],
                                              start=(e == e0), stop=(e == 1))
            t_o = pe.go(mm)
            act.wait(t_o)
            t_oc = act.go(nc.scalar.copy(OB[:, :, b * P:(b + 1) * P], k.ps[:, 0, :].rearrange("p (j t) -> p j t", j=4)))
            pe.wait(t_oc)
        k.phase_end()


def pool_mixer(k, R):
    nc, pe, dve, act = k.nc, k.pe, k.dve, k.act
    v = nc.vector
    PAD = 16
    with ExitStack() as ctx:
        A = k.sb("pool_a", [P, 2, T + PAD], ctx)
        Bf = k.sb("pool_b", [P, 2, T + PAD], ctx)
        Y = k.sb("pooled", [P, DT, T], ctx)

        def step(ins):
            t = dve.go(ins)
            dve.wait(t)
            return t
        dve.go(v.memset(A[:, :, 0:PAD], 0.0))
        step(v.memset(Bf[:, :, 0:PAD], 0.0))
        for g, w in enumerate(POOL_WINDOWS):
            h = k.H[:, 2 * g:2 * g + 2, 0:T]
            step(v.tensor_copy(A[:, :, PAD:], h))
            src, dst = A, Bf
            n = 1
            while n < w:
                step(v.tensor_tensor(dst[:, :, PAD:], src[:, :, PAD:], src[:, :, PAD - n:PAD - n + T], ALU.add))
                src, dst = dst, src
                n *= 2
            y = Y[:, 2 * g:2 * g + 2, :]
            cnt = k.c("pool_cnt", g * 16, 16).unsqueeze(1).broadcast_to([P, 2, 16])
            step(v.tensor_tensor(src[:, :, PAD:PAD + 16], src[:, :, PAD:PAD + 16], cnt, ALU.mult))
            step(v.tensor_scalar(src[:, :, PAD + 16:], src[:, :, PAD + 16:], 1.0 / w, None, ALU.mult))
            t_y = step(v.tensor_tensor(y, src[:, :, PAD:], h, ALU.subtract))
        pg = k.sc[:, 5, :]
        step(v.tensor_tensor(pg, k.p("pool_scale"), k.MOD[1][:, 16:24, 0], ALU.mult))
        k.fetch(k.dram["pool_w"][0], DT, 2 * P)
        k.slab_wait()
        wv = k.slab_view(DT, 2 * P)
        slot = k.slab_next()
        pe.wait(t_y)
        for n in range(DT):
            g, a = n // 2, n % 2
            for kk in range(2):
                mm = nc.tensor.matmul(k.ps[:, n, :], wv[:, 2 * g + kk, a * P:(a + 1) * P], Y[:, 2 * g + kk, :],
                                      start=(kk == 0), stop=(kk == 1))
            t = pe.go(mm)
            dve.wait(t)
            if n == DT - 1:
                dve.eng.nop().then_inc(slot, 1)
            dve.go(v.scalar_tensor_tensor(R[:, n, :], k.ps[:, n, :], pg[:, n:n + 1], k.XA[:, n, :], ALU.mult, ALU.add))
        k.phase_end()


def pre_norm(k, ctx, layer, MOD, XC, all_tokens=True):
    nc, pe, dve, act = k.nc, k.pe, k.dve, k.act
    v = nc.vector
    sq = k.sb(f"sq{layer}", [P, DT, T], ctx)
    rs = k.sb(f"rs{layer}", [P, T], ctx)
    g = k.p("norm_pre", layer * 8, 8)
    for n, (X, t0, tn) in enumerate(((k.XA, TC, T), (XC, 0, TC))):
        sc = k.sc[:, 6 + n, :]
        t = dve.go(v.tensor_scalar(sc, MOD[:, 8:16, n], 1.0, None, ALU.add))
        dve.wait(t)
        dve.go(v.tensor_tensor(sc, sc, g, ALU.mult))
        if n:
            act.wait(t_mm)
        half = DT // 2
        for j in range(2):
            hs = slice(j * half, (j + 1) * half)
            t = act.go(nc.scalar.activation(sq[:, hs, 0:tn], X[:, hs, :], ACT.Square))
            pe.wait(t)
            for kk in range(j * half, (j + 1) * half):
                mm = nc.tensor.matmul(k.ps[:, n, 0:tn], k.ones, sq[:, kk, 0:tn], start=(kk == 0), stop=(kk == DT - 1))
        t_mm = pe.go(mm)
        if n:
            dve.wait(t_h)
        rstd(k, rs[:, 0:tn], k.ps[:, n, 0:tn], 1.0 / D, EPS, t_mm)
        H = k.H[:, :, t0:t0 + tn]
        t_h = dve.go(v.tensor_tensor(H, X[:], rs[:, 0:tn].unsqueeze(1).broadcast_to([P, DT, tn]), ALU.mult))
        act.wait(t_h)
        for kk in range(DT):
            affine(act, H[:, kk, :], H[:, kk, :], sc[:, kk:kk + 1], MOD[:, kk, n:n + 1])
    k.phase_end()


def post_norm(k, ctx, name, layer, MOD, OUT, X, n, t0, tn):
    nc, pe, dve, act = k.nc, k.pe, k.dve, k.act
    v = nc.vector
    sq = k.sb("psq" + name, [P, DT, T], ctx)
    rs = k.sb("prs" + name, [P, T], ctx)
    gg = k.sc[:, 5, :]
    dve.go(v.tensor_tensor(gg, MOD[:, 16:24, n], k.p("norm_post", layer * 8, 8), ALU.mult))
    O = OUT[:, :, t0:t0 + tn]
    t = act.go(nc.scalar.activation(sq[:, :, 0:tn], O, ACT.Square))
    pe.wait(t)
    for kk in range(DT):
        mm = nc.tensor.matmul(k.ps[:, 0, 0:tn], k.ones, sq[:, kk, 0:tn], start=(kk == 0), stop=(kk == DT - 1))
    t = pe.go(mm)
    rstd(k, rs[:, 0:tn], k.ps[:, 0, 0:tn], 1.0 / D, EPS, t)
    t = dve.go(v.tensor_tensor(O, O, rs[:, 0:tn].unsqueeze(1).broadcast_to([P, DT, tn]), ALU.mult))
    dve.wait(t)
    for kk in range(DT):
        dve.go(v.scalar_tensor_tensor(X[:, kk, :], O[:, kk, :], gg[:, kk:kk + 1], X[:, kk, :], ALU.mult, ALU.add))
    k.phase_end()


def mix(k, step, out, pc, pl, s):
    v = k.nc.vector
    oc, ol = out[:, 0:TC], out[:, TC:TA]
    g = lambda a: a.rearrange("p (r w) -> p r w", w=GRID_W)
    step(v.tensor_scalar(oc, pc, s[:, 0:1], None, ALU.mult))
    step(v.tensor_scalar(ol, pl, s[:, 0:1], None, ALU.mult))

    def add(o, i, j):
        return v.scalar_tensor_tensor(o, i, s[:, j:j + 1], o, ALU.mult, ALU.add)
    step(add(oc[:, 1:TC], pc[:, 0:TC - 1], 5))
    step(add(g(ol)[:, :, 1:], g(pl)[:, :, :-1], 1))
    step(add(oc[:, 0:TC - 1], pc[:, 1:TC], 6))
    step(add(g(ol)[:, :, :-1], g(pl)[:, :, 1:], 2))
    step(add(ol[:, GRID_W:], pl[:, :-GRID_W], 3))
    return step(add(ol[:, :-GRID_W], pl[:, GRID_W:], 4))


def flat_ps(k, bank, n):
    return k.ps[:, bank:bank + 2, :].rearrange("p a b -> p (a b)")[:, 0:n]


def slab_tiles(k, w, idx, banks, waits, i=0, per=0):
    nc, pe = k.nc, k.pe
    k.fetch(w[idx], DT, 2 * P, i, per)
    k.slab_wait(i, per)
    wv = k.slab_view(DT, 2 * P)
    slot = k.slab_next()
    out = []
    for a in range(2):
        pe.wait(*waits[a])
        for b, (t0, tn) in enumerate(((0, TC), (TC, T))):
            for kk in range(DT):
                mm = nc.tensor.matmul(k.ps[:, banks[a] + b, 0:tn], wv[:, kk, a * P:(a + 1) * P],
                                      k.H[:, kk, t0:t0 + tn], start=(kk == 0), stop=(kk == DT - 1))
        out.append(pe.go(mm))
    return out, slot


def even_mixer2(k, ctx, OUT):
    nc, pe, dve, act, pool = k.nc, k.pe, k.dve, k.act, k.pool
    v = nc.vector
    w = k.dram["ev_in"]
    with ExitStack() as ctx:
        O = k.sb("O", [P, DT, TA], ctx)
        with ExitStack() as c2:
            WL = k.sb("WL", [P, TA], c2)
            AL = k.sb("AL", [P, TA], c2)
            MUX = k.sb("MUX", [P, 20, 7], c2)
            with ExitStack() as c3:
                FOUR = k.sb("FOUR", [P, 2, TA], c3)
                GF = k.sb("GF", [P, 2, TA], c3)

                def step(ins):
                    t = dve.go(ins)
                    dve.wait(t)
                    return t
                mu = k.p("mu")
                step(v.tensor_scalar(MUX[:, :, 0], mu, -1.0, 1.0, ALU.mult, ALU.add))
                for j in range(6):
                    m = k.c("type4", j, 1) if j < 4 else k.c("type2", j - 4, 1)
                    step(v.tensor_scalar(MUX[:, :, 1 + j], mu, m, None, ALU.mult))
                (ta, tb), slot = slab_tiles(k, w, 0, (0, 2), ((), ()))
                dve.wait(ta)
                mix(k, step, WL, k.ps[:, 0, 0:TC], k.ps[:, 1, :], MUX[:, 18, :])
                dve.wait(tb)
                dve.eng.nop().then_inc(slot, 1)
                t_al = mix(k, step, AL, k.ps[:, 2, 0:TC], k.ps[:, 3, :], MUX[:, 19, :])
                act.wait(t_al)
                act.go(nc.scalar.activation(WL[:], WL[:], ACT.Tanh))
                (ta, tb), slot = slab_tiles(k, w, 1, (4, 6), ((), ()))
                act.wait(ta)
                for a, t in ((0, ta), (1, tb)):
                    act.wait(t)
                    act.go(nc.scalar.copy(FOUR[:, a, 0:TC], k.ps[:, 4 + 2 * a, 0:TC]))
                    act.go(nc.scalar.copy(FOUR[:, a, TC:TA], k.ps[:, 5 + 2 * a, :]))
                act.eng.nop().then_inc(slot, 1)
                (ta, tb), slot = slab_tiles(k, w, 2, (0, 2), ((t_al,), ()))
                for a, t in ((0, ta), (1, tb)):
                    act.wait(t)
                    act.go(nc.scalar.activation(GF[:, a, 0:TC], k.ps[:, 2 * a, 0:TC], ACT.Silu))
                    act.go(nc.scalar.activation(GF[:, a, TC:TA], k.ps[:, 1 + 2 * a, :], ACT.Silu))
                act.eng.nop().then_inc(slot, 1)
                k.phase_end()
                fourier(k, FOUR, GF, O)
            rwkv(k, c2, WL, AL, MUX, O)
        dense_fm(k, "ev_out", 4, O, [(0, TC), (TC, T)], lambda n, banks: two_copies(k, OUT, n, banks))


def two_copies(k, OUT, n, banks):
    v = k.nc.vector
    o = tile_of(OUT, n)
    v.tensor_copy(o[:, 0:TC], banks[0])
    return v.tensor_copy(o[:, TC:TA], banks[1])


def fourier(k, FOUR, GF, O):
    nc, pe, dve, act = k.nc, k.pe, k.dve, k.act
    v = nc.vector
    with ExitStack() as ctx:
        dft = k.sb("dft_sb", [P, F_N], ctx)
        t_ld = k.load(dft[:], k.dram["dft"])
        k.loaded(pe, t_ld)
        f = lambda name: dft[:, F_AT[name][0]:F_AT[name][0] + F_AT[name][1]]
        PQ = k.sb("PQ", [P, TA // P, 2, 2 * P], ctx)
        for t in range(TA // P):
            for a in range(2):
                mm = nc.tensor.matmul(k.ps[:, t, a * 256:(a + 1) * 256], FOUR[:, a, t * P:(t + 1) * P], f("f64"),
                                      start=True, stop=True)
            tok = pe.go(mm)
            act.wait(tok)
            t_pq = act.go(nc.scalar.copy(PQ[:, t, :, :], k.ps[:, t, :].rearrange("p (a n) -> p a n", a=2)))
        pe.wait(t_pq)
        for a in range(2):
            for b, (c, s, t0, tn, u0) in enumerate((("c256", "s256", 0, TC, 0), ("c512", "s512", TC, T, 2))):
                n = tn // P
                out = k.ps[:, 2 * a + b, 0:tn]
                cw = f(c).rearrange("p (u t) -> p u t", u=n)
                sw = f(s).rearrange("p (u t) -> p u t", u=n)
                for u in range(n):
                    nc.tensor.matmul(out, PQ[:, u0 + u, a, 0:P], cw[:, u, :], start=(u == 0), stop=False)
                    mm = nc.tensor.matmul(out, PQ[:, u0 + u, a, P:2 * P], sw[:, u, :], start=False, stop=(u == n - 1))
                tok = pe.go(mm)
                dve.wait(tok)
                dve.go(v.tensor_tensor(O[:, RT + a, t0:t0 + tn], out, GF[:, a, t0:t0 + tn], ALU.mult))
        k.n_loads = 0
        k.phase_end()


def rwkv(k, ctx, WL, AL, MUX, O):
    nc, pe, dve, act, pool = k.nc, k.pe, k.dve, k.act, k.pool
    v = nc.vector
    w = k.dram["ev_in"]
    NC = TA // CH
    W2, A2 = k.sb("W2", [P, RT * P], ctx), k.sb("A2", [P, RT * P], ctx)
    t = k.load(W2[:], k.dram["w2"])
    t = k.load(A2[:], k.dram["a2"])
    k.loaded(dve, t)
    k.n_loads = 0
    ws = k.sb("w2a2", [P, 2, P], ctx)
    MS = k.sb("mix_scal", [P, 3, 7], ctx)
    RW = k.sb("rw_scal", [P, 10], ctx)
    SRC = k.sb("rkv", [P, 3, TA], ctx)
    GR = k.sb("gate_r", [P, TA], ctx)
    LW, F, X1, X2, E3, A, KD, KK = (k.sb(n, [P, TA], ctx) for n in ("LW", "F", "X1", "X2", "E3", "A", "KD", "KK"))
    KS = k.sb("KS", [P, TA], ctx)
    AR = k.sb("AR", [P, NC, 320], ctx)
    BP, KP = k.sb("beta", [P, TA], ctx), k.sb("kappa", [P, TA], ctx)
    VP = k.sb("VP", [P, NC, 2, P], ctx)
    BB, KB = k.sb("BB", [P, 4, 192], ctx), k.sb("KB", [P, 4, 192], ctx)
    AMV = k.sb("AMV", [P, 4, P], ctx)
    NLT, MT, X, Y, T1 = (k.sb(n, [P, 4, P], ctx) for n in ("NLT", "MT", "X", "Y", "T1"))
    QG = k.sb("QG", [P, NC, 2, 192], ctx)
    EV = k.sb("EV", [P, 2, NC], ctx)
    HAT = k.sb("HAT", [P, NC], ctx)
    TI = k.sb("TI", [P, 2, 2, 64], ctx)
    r, k0, val = SRC[:, 0, :], SRC[:, 1, :], SRC[:, 2, :]
    ch = lambda a: a.rearrange("p (c t) -> p c t", t=CH)
    dve.go(v.memset(VP[:], 0.0))
    dve.go(v.memset(EV[:], 1.0))
    for j in range(2):
        for h in range(2):
            dve.go(v.tensor_copy(TI[64:128, j, h, :], k.c("ident64")[64:128, :]))
    k.phase_end()
    with nc.Fori(0, RT) as p:
        def step(ins):
            t = dve.go(ins)
            dve.wait(t)
            return t
        dve.go(v.tensor_copy(MS[:].unsqueeze(2), MUX[:, 0:18, :].rearrange("p (a q) s -> p a q s", q=RT)[:, :, bass.ds(p, 1), :]))
        dve.go(v.tensor_copy(ws[:, 0, :], W2[:, bass.ds(p * P, P)]))
        dve.go(v.tensor_copy(ws[:, 1, :], A2[:, bass.ds(p * P, P)]))
        step(v.tensor_copy(RW[:, 0:9], k.p("rw")[:, bass.ds(p * 9, 9)]))
        t_ws = step(v.tensor_scalar(RW[:, 9:10], RW[:, 5:6], -1.0, 1.0, ALU.mult, ALU.add))
        rw = lambda j: RW[:, j:j + 1]
        (ta, tb), slot = slab_tiles(k, w, 3 + p * 2, (0, 2), ((), ()), p, 1)
        dve.wait(ta)
        mix(k, step, r, k.ps[:, 0, 0:TC], k.ps[:, 1, :], MS[:, 0, :])
        dve.wait(tb)
        dve.eng.nop().then_inc(slot, 1)
        t_k0 = mix(k, step, k0, k.ps[:, 2, 0:TC], k.ps[:, 3, :], MS[:, 1, :])
        (ta, tb), slot = slab_tiles(k, w, 4 + p * 2, (4, 6), ((), ()), p, 1)
        dve.wait(ta)
        t_v = mix(k, step, val, k.ps[:, 4, 0:TC], k.ps[:, 5, :], MS[:, 2, :])
        act.wait(tb)
        act.eng.nop().then_inc(slot, 1)
        act.go(nc.scalar.activation(GR[:, 0:TC], k.ps[:, 6, 0:TC], ACT.Silu))
        t_gr = act.go(nc.scalar.activation(GR[:, TC:TA], k.ps[:, 7, :], ACT.Silu))
        t = step(v.tensor_scalar(KK[:], k0, rw(4), None, ALU.mult))
        act.wait(t)
        t_sq = act.go(nc.scalar.activation(X1[:], KK[:], ACT.Square))
        pe.wait(t_sq, t_v)
        nrm = flat_ps(k, 0, TA)
        two_mm(k, 0, k.c("blk64"), X1)
        t = pe.go(k.last_mm)
        act.wait(t)
        t = act.go(nc.scalar.activation(X2[:], nrm, ACT.Sqrt))
        dve.wait(t)
        step(v.tensor_scalar(X2[:], X2[:], 1e-12, None, ALU.max))
        step(v.reciprocal(X2[:], X2[:]))
        step(v.tensor_tensor(KK[:], KK[:], X2[:], ALU.mult))
        for c in range(NC):
            mm = nc.tensor.transpose(k.ps[:, 2 + c // 4, (c % 4) * P:(c % 4 + 1) * P], val[:, c * P:(c + 1) * P], k.ident)
        t = pe.go(mm)
        act.wait(t)
        t_vp = act.go(nc.scalar.copy(VP[:, :, :, 64:128],
                                     flat_ps(k, 2, TA).rearrange("p (c h i) -> p c h i", c=NC, h=2)))
        read = [t_vp] * 8
        read[0] = read[1] = (dve.sem, dve.n)
        t_yf = None
        for d in range(2):
            rows = slice(64 * d, 64 * d + 64)
            pe.wait(t_ws, read[4], read[5], read[6], read[7])
            two_mm(k, 4, ws[rows, 0, :], WL[rows, :])
            t_w = pe.go(k.last_mm)
            two_mm(k, 6, ws[rows, 1, :], AL[rows, :])
            t_a = pe.go(k.last_mm)
            act.wait(t_w, (dve.sem, dve.n))
            t_lw = act.go(nc.scalar.activation(LW[:], flat_ps(k, 4, TA), ACT.Sigmoid, bias=rw(d)))
            act.wait(t_a)
            t_av = act.go(nc.scalar.activation(A[:], flat_ps(k, 6, TA), ACT.Sigmoid, bias=rw(2 + d)))
            read[4] = read[5] = read[6] = read[7] = t_av
            dve.wait(t_lw)
            step(v.tensor_scalar(LW[:], LW[:], -math.exp(-0.5), None, ALU.mult))
            step(v.tensor_tensor_scan(F[:], k.c("scan_reset"), LW[:], 0.0, ALU.mult, ALU.add))
            fmid = ch(F[:])[:, :, 63:64]
            fend = ch(F[:])[:, :, CH - 1:CH]
            fm = fmid.broadcast_to([P, NC, CH])
            if d == 0:
                step(v.tensor_tensor(ch(X2[:]), ch(F[:]), fm, ALU.subtract))
                t_x = step(v.tensor_tensor(X1[:], X2[:], LW[:], ALU.subtract))
            else:
                step(v.tensor_tensor(ch(X1[:]), fm, ch(F[:]), ALU.subtract))
                t_x = step(v.tensor_tensor(X2[:], X1[:], LW[:], ALU.add))
            g1, g2 = HAT[:], LW[:, 0:NC]
            t_g = step(v.tensor_tensor(LW[:, NC:2 * NC], fend, fmid, ALU.subtract))
            act.wait(t_g)
            act.go(nc.scalar.activation(E3[:], X2[:], ACT.Exp, scale=-1.0))
            act.go(nc.scalar.activation(X1[:], X1[:], ACT.Exp))
            act.go(nc.scalar.activation(X2[:], X2[:], ACT.Exp))
            act.go(nc.scalar.activation(LW[:, 2 * NC:3 * NC], fmid, ACT.Exp))
            t_e = act.go(nc.scalar.activation(LW[:, 3 * NC:4 * NC], LW[:, NC:2 * NC], ACT.Exp))
            dve.wait(t_e, t_av)
            g_mid, g_end = LW[:, 2 * NC:3 * NC], LW[:, 3 * NC:4 * NC]
            if d:
                g_mid, g_end = g_end, g_mid
            dve.go(v.tensor_copy(EV[0:64, 0, :], g_mid[0:64, :]))
            dve.go(v.tensor_copy(EV[0:64, 1, :], g_mid[64:128, :]))
            hat = g_end
            step(v.tensor_scalar(KD[:], A[:], rw(5), rw(9), ALU.mult, ALU.add))
            step(v.tensor_tensor(KD[:], KD[:], k0, ALU.mult))
            if d == 0:
                dve.go(v.tensor_copy(KS[:], KD[:]))
            else:
                dve.go(v.tensor_tensor(KS[:], KS[:], KD[:], ALU.add))
            step(v.scalar_tensor_tensor(A[:], A[:], -1.0, KK[:], ALU.mult, ALU.mult))
            dve.go(v.tensor_tensor(AR[:, :, 0:CH], ch(KK[:]), ch(X1[:]), ALU.mult))
            dve.go(v.tensor_tensor(AR[:, :, CH:2 * CH], ch(r), ch(X2[:]), ALU.mult))
            dve.go(v.tensor_tensor(AR[:, :, 2 * CH:320], k.c("ident64").unsqueeze(1).broadcast_to([P, NC, 64]),
                                   hat.unsqueeze(2).broadcast_to([P, NC, 64]), ALU.mult))
            dve.go(v.tensor_tensor(BP[:], A[:], E3[:], ALU.mult))
            t_ar = step(v.tensor_tensor(KP[:], KD[:], E3[:], ALU.mult))
            hb = hat.unsqueeze(2).broadcast_to([P, NC, CH])
            dve.go(v.tensor_tensor(ch(X1[:]), ch(BP[:]), hb, ALU.mult))
            t_hat = step(v.tensor_tensor(ch(X2[:]), ch(KP[:]), hb, ALU.mult))
            lo, up = (k.c("low"), k.c("up")) if d == 0 else (k.c("up"), k.c("low"))
            s_lo, s_up = (k.c("strict_low"), k.c("strict_up"))[::1 if d == 0 else -1]
            i_up = k.c("incl_up") if d == 0 else k.c("incl_low")
            b4 = lambda m: m.unsqueeze(1).broadcast_to([P, 4, P])
            for q in range(NC // 2):
                cs = (2 * q, 2 * q + 1)
                pe.wait(t_ar, *read)
                for h in range(2):
                    hr = slice(64 * h, 64 * h + 64)
                    for j, c in enumerate(cs):
                        a = slice(c * CH, (c + 1) * CH)
                        nc.tensor.matmul(k.ps[:, h, j * 256:(j + 1) * 256], BP[hr, a], AR[hr, c, 0:256], start=True, stop=True)
                        nc.tensor.matmul(k.ps[:, 2 + h, j * 256:(j + 1) * 256], KP[hr, a], AR[hr, c, 0:256], start=True, stop=True)
                        mm = nc.tensor.matmul(k.ps[:, 4 + h, j * 256:j * 256 + CH], AR[hr, c, 0:CH], BP[hr, a], start=True, stop=True)
                t_sc = pe.go(mm)
                pe.wait(t_hat)
                for j, c in enumerate(cs):
                    a = slice(c * CH, (c + 1) * CH)
                    nc.tensor.transpose(k.ps[:, 6, j * P:(j + 1) * P], AR[:, c, 0:CH], k.ident)
                    nc.tensor.transpose(k.ps[:, 6, (2 + j) * P:(3 + j) * P], X1[:, a], k.ident)
                    mm = nc.tensor.transpose(k.ps[:, 7, j * P:(j + 1) * P], X2[:, a], k.ident)
                t_tr = pe.go(mm)
                u4 = lambda b: k.ps[:, b:b + 2, :].rearrange("p h (j n) -> p (h j) n", j=2)
                dve.wait(t_sc)
                act.wait(t_sc, (dve.sem, dve.n))
                act.go(nc.scalar.copy(X[:], b4(k.ident)))
                t_i = act.go(nc.scalar.copy(Y[:], b4(k.ident)))
                dve.go(v.tensor_tensor(NLT[:], u4(0)[:, :, 0:CH], b4(s_up), ALU.mult))
                dve.go(v.tensor_tensor(BB[:, :, 0:CH], u4(0)[:, :, CH:256], b4(i_up), ALU.mult))
                t_mt = dve.go(v.tensor_tensor(MT[:], u4(2)[:, :, 0:CH], b4(s_up), ALU.mult))
                dve.go(v.tensor_tensor(KB[:, :, 0:CH], u4(2)[:, :, CH:256], b4(i_up), ALU.mult))
                dve.wait(t_i)
                dve.go(v.copy_predicated(X[:], b4(lo[:, 0:P]).bitcast(I32), u4(4)[:, :, 0:CH]))
                t_x0 = dve.go(v.copy_predicated(Y[:], b4(up[:, 0:P]).bitcast(I32), u4(0)[:, :, 0:CH]))
                act.wait(t_tr)
                tm = lambda b, o: k.ps[:, b, o:o + 2 * P].rearrange("p (j h i) -> p h j i", j=2, h=2)
                hj = lambda a: a.rearrange("p (h j) i -> p h j i", h=2)
                act.go(nc.scalar.copy(hj(AMV[:, :, 0:64]), tm(6, 0)))
                act.go(nc.scalar.copy(hj(BB[:, :, CH:192]), tm(6, 2 * P)))
                t_tm = act.go(nc.scalar.copy(hj(KB[:, :, CH:192]), tm(7, 0)))
                pe.wait(t_mt, t_x0, t_tm)
                for u in range(4):
                    mm = nc.tensor.matmul(k.ps[:, 6, u * 64:(u + 1) * 64], MT[:, u, :], VP[:, cs[u % 2], u // 2, 64:128], start=True, stop=True)
                t_mv = pe.go(mm)
                act.wait(t_mv)
                t_amv = act.go(nc.scalar.copy(AMV[:, :, 64:128], k.ps[:, 6, 0:256].rearrange("p (u i) -> p u i", u=4)))
                for m in range(1, LEVELS):
                    bk = 3 * (m % 2)
                    for u in range(4):
                        mm = nc.tensor.matmul(k.ps[:, bk, u * P:(u + 1) * P], NLT[:, u, :], X[:, u, :], start=True, stop=True)
                    t = pe.go(mm)
                    act.wait(t)
                    t_t1 = act.go(nc.scalar.copy(T1[:], k.ps[:, bk, :].rearrange("p (u t) -> p u t", u=4)))
                    pe.wait(t_t1)
                    if m < LEVELS - 1:
                        for u in range(4):
                            mm = nc.tensor.matmul(k.ps[:, bk + 1, u * P:(u + 1) * P], Y[:, u, :], T1[:, u, :], start=True, stop=True)
                        t_xm = pe.go(mm)
                    for u in range(4):
                        mm = nc.tensor.matmul(k.ps[:, bk + 2, u * P:(u + 1) * P], T1[:, u, :], Y[:, u, :], start=True, stop=True)
                    t_ym = pe.go(mm)
                    u3 = lambda b: k.ps[:, b, :].rearrange("p (u t) -> p u t", u=4)
                    dve.wait(t_ym)
                    if m < LEVELS - 1:
                        dve.go(v.copy_predicated(X[:], b4(lo[:, m * P:(m + 1) * P]).bitcast(I32), u3(bk + 1)))
                    t_y = dve.go(v.copy_predicated(Y[:], b4(up[:, m * P:(m + 1) * P]).bitcast(I32), u3(bk + 2)))
                    pe.wait(t_y)
                pe.wait(t_amv)
                for u in range(4):
                    mm = nc.tensor.matmul(k.ps[:, 7, u * P:(u + 1) * P], Y[:, u, :], AMV[:, u, :], start=True, stop=True)
                t = pe.go(mm)
                act.wait(t)
                t_wu = act.go(nc.scalar.copy(T1[:], k.ps[:, 7, :].rearrange("p (u t) -> p u t", u=4)))
                pe.wait(t_wu)
                for u in range(4):
                    h, c = u // 2, cs[u % 2]
                    hr = slice(64 * h, 64 * h + 64)
                    o = k.ps[:, 4 + h, (u % 2) * 192:(u % 2 + 1) * 192]
                    nc.tensor.matmul(o, T1[:, u, :], BB[:, u, :], start=True, stop=False)
                    nc.tensor.matmul(o, VP[:, c, h, :], KB[:, u, :], start=False, stop=False)
                    mm = nc.tensor.matmul(o, k.c("top_ident")[hr, :], AR[hr, c, CH:320], start=False, stop=True)
                t_qg = pe.go(mm)
                act.wait(t_qg)
                for u in range(4):
                    h, c = u // 2, cs[u % 2]
                    t = act.go(nc.scalar.mul(QG[:, c, h, :], k.ps[:, 4 + h, (u % 2) * 192:(u % 2 + 1) * 192], EV[:, h, c:c + 1]))
                read = [t, (dve.sem, dve.n)]
            t_st = step(v.memset(TI[0:64, 0, :, :], 0.0))
            order = [0, 1, 2, 3, 4, 5] if d == 0 else [1, 0, 5, 4, 3, 2]
            pe.wait(*read)
            for n, c in enumerate(order):
                pe.wait(t_st)
                cur, nxt = TI[:, n % 2, :, :], TI[:, (n + 1) % 2, :, :]
                if n < NC - 1:
                    for h in range(2):
                        mm = nc.tensor.matmul(k.ps[0:64, 2 + n % 2, h * 64:(h + 1) * 64], QG[:, c, h, CH:192], cur[:, h, :], start=True, stop=True)
                    t = pe.go(mm)
                    dve.wait(t)
                    if n:
                        dve.wait(t_out)
                    t_st = dve.go(v.tensor_copy(nxt[0:64, :, :], k.ps[0:64, 2 + n % 2, 0:P].rearrange("p (h i) -> p h i", h=2)))
                for h in range(2):
                    mm = nc.tensor.matmul(k.ps[64 * h:64 * h + 64, c // 4, (c % 4) * P:(c % 4 + 1) * P], cur[:, h, :],
                                          QG[:, c, h, 0:CH], start=True, stop=True)
                t_out = pe.go(mm)
            dve.wait(t_out)
            if d == 0:
                t = step(v.tensor_copy(tile_of(O, p), flat_ps(k, 0, TA)))
            else:
                t = step(v.tensor_tensor(F[:], tile_of(O, p), flat_ps(k, 0, TA), ALU.add))
            read = [t] * 8
        t = step(v.scalar_tensor_tensor(KS[:], r, rw(6), KS[:], ALU.mult, ALU.mult))
        pe.wait(t)
        two_mm(k, 0, k.c("blk64"), KS)
        t = pe.go(k.last_mm)
        dve.wait(t)
        step(v.tensor_tensor(X1[:], flat_ps(k, 0, TA), val, ALU.mult))
        t = step(v.tensor_tensor(F[:], F[:], X1[:], ALU.add))
        pe.wait(t)
        two_mm(k, 2, k.c("blk64"), F)
        t = pe.go(k.last_mm)
        dve.wait(t)
        t = step(v.scalar_tensor_tensor(F[:], flat_ps(k, 2, TA), -1.0 / 64, F[:], ALU.mult, ALU.add))
        act.wait(t)
        t = act.go(nc.scalar.activation(X1[:], F[:], ACT.Square))
        pe.wait(t)
        two_mm(k, 4, k.c("blk64"), X1)
        t = pe.go(k.last_mm)
        rstd(k, X2[:], flat_ps(k, 4, TA), 1.0 / 64, GN_EPS, t)
        step(v.tensor_tensor(F[:], F[:], X2[:], ALU.mult))
        step(v.tensor_scalar(F[:], F[:], rw(7), rw(8), ALU.mult, ALU.add))
        dve.wait(t_gr)
        dve.go(v.tensor_tensor(tile_of(O, p), F[:], GR[:], ALU.mult))
        k.phase_end()
    k.slab_loop(RT)


def two_mm(k, bank, lhsT, rhs):
    for n, (t0, tn) in enumerate(((0, T), (T, TC))):
        k.last_mm = k.nc.tensor.matmul(k.ps[:, bank + n, 0:tn], lhsT, rhs[:, t0:t0 + tn], start=True, stop=True)


def log_sigmoid(k, ctx, out, x):
    nc, dve, act = k.nc, k.dve, k.act
    v = nc.vector
    n = x.shape[1]
    b = k.sb("ls_tmp", [P, 4, n], ctx)
    y, z, z2, acc = (b[:, j, :] for j in range(4))

    def step(ins):
        t = dve.go(ins)
        dve.wait(t)
        return t
    step(v.tensor_scalar(z, x, -1.0, None, ALU.mult))
    t = step(v.tensor_tensor(z, z, x, ALU.max))
    act.wait(t)
    t = act.go(nc.scalar.activation(y, z, ACT.Exp, scale=-1.0))
    dve.wait(t)
    step(v.tensor_scalar(z, y, 2.0, None, ALU.add))
    step(v.reciprocal(z, z))
    step(v.tensor_tensor(z, z, y, ALU.mult))
    step(v.tensor_tensor(z2, z, z, ALU.mult))
    step(v.tensor_scalar(acc, z2, 1.0 / 17, 1.0 / 15, ALU.mult, ALU.add))
    for c in (13, 11, 9, 7, 5, 3, 1):
        step(v.tensor_tensor(acc, acc, z2, ALU.mult))
        step(v.tensor_scalar(acc, acc, 1.0 / c, None, ALU.add))
    step(v.tensor_tensor(acc, acc, z, ALU.mult))
    step(v.tensor_scalar(z, x, 0.0, None, ALU.min))
    return step(v.scalar_tensor_tensor(out, acc, -2.0, z, ALU.mult, ALU.add))


def rope_loop(k, ctx, X, t0, cos, sin, what):
    nc, pe, dve = k.nc, k.pe, k.dve
    v = nc.vector
    ROT = k.sb("ROT" + what, [P, 4, T], ctx)
    with nc.Fori(0, RH // 4) as i:
        for j in range(4):
            x = tile_of(X, i * 4 + j)[:, t0:t0 + T]
            t = pe.go(nc.tensor.matmul(k.ps[:, j, :], k.c("swap64"), x, start=True, stop=True))
            dve.wait(t)
            ta = dve.go(v.tensor_tensor(ROT[:, j, :], k.ps[:, j, :], sin, ALU.mult))
            tb = dve.go(v.tensor_tensor(x, x, cos, ALU.mult))
            dve.wait(ta, tb)
            dve.go(v.tensor_tensor(x, x, ROT[:, j, :], ALU.add))
        k.phase_end()


def odd_mixer2(k, OUT):
    nc, pe, dve, act = k.nc, k.pe, k.dve, k.act
    v = nc.vector
    NC, NL = TA // CH, T // CH
    with ExitStack() as ctx:
        Q = k.sb("Q", [P, RH, T], ctx)
        K = k.sb("Kr", [P, RH, TA], ctx)
        V = k.sb("V", [P, NC, D], ctx)
        G = k.sb("Gr", [P, RH, T], ctx)
        lat = [(TC, T)]
        dense_fm(k, "od_in", 4, k.H, lat, lambda n, b: v.tensor_copy(tile_of(Q, n), b[0]))

        def scaled(n, banks):
            o = tile_of(K, n)
            v.tensor_scalar(o[:, 0:TC], banks[0], P ** -0.5, None, ALU.mult)
            return v.tensor_scalar(o[:, TC:TA], banks[1], P ** -0.5, None, ALU.mult)
        dense_fm(k, "od_in", 4, k.H, [(0, TC), (TC, T)], scaled, first=4)
        values(k, "od_in", 8, V)
        dense_fm(k, "od_in", 4, k.H, lat, lambda n, b: v.tensor_copy(tile_of(G, n), b[0]), first=12)
        O = k.H[:, :, 0:T]
        with ExitStack() as c2:
            C2 = k.sb("consts2_sb", [P, C2_N], c2)
            t = k.load(C2[:], k.dram["consts2"])
            for q in (pe, dve, act):
                k.loaded(q, t)
            k.n_loads = 0
            c = lambda name, a=0, n=None: C2[:, C2_AT[name][0] + a:C2_AT[name][0] + a + (n or C2_AT[name][1])]
            act.go(nc.scalar.activation(G[:], G[:], ACT.Silu))
            LG, GC, ZT = k.sb("LG", [P, 16], c2), k.sb("GC", [P, 16], c2), k.sb("ZT", [P, 16], c2)
            DD = k.sb("DD", [P, RH, P], c2)
            XI = k.sb("XI", [P, 2, RH, P], c2)
            tmp = k.H[:, :, T:T + P]
            t = log_sigmoid(k, c2, LG[:], k.p("decay"))
            act.wait(t)
            act.go(nc.scalar.activation(GC[:], LG[:], ACT.Exp, scale=float(CH)))
            act.go(nc.scalar.activation(ZT[:, 0:8], LG[:, 0:8], ACT.Exp, scale=c("zpos", 0, 1)))
            act.go(nc.scalar.activation(ZT[:, 8:16], LG[:, 8:16], ACT.Exp, scale=c("zpos", 1, 1)))
            for h in range(RH):
                f, b = LG[:, h:h + 1], LG[:, 8 + h:9 + h]
                act.go(nc.scalar.activation(XI[:, 0, h, :], c("pos1"), ACT.Exp, scale=f))
                act.go(nc.scalar.activation(XI[:, 1, h, :], c("pos1r"), ACT.Exp, scale=b))
                act.go(nc.scalar.activation(DD[:, h, :], c("dist_f"), ACT.Exp, scale=f))
                t = act.go(nc.scalar.activation(tmp[:, h, :], c("dist_b"), ACT.Exp, scale=b))
            dve.wait(t)
            bc = lambda m: m.unsqueeze(1).broadcast_to([P, RH, P])
            ta = dve.go(v.tensor_tensor(DD[:], DD[:], bc(k.c("incl_up")), ALU.mult))
            tb = dve.go(v.tensor_tensor(tmp, tmp, bc(k.c("strict_low")), ALU.mult))
            dve.wait(ta, tb)
            dve.go(v.tensor_tensor(DD[:], DD[:], tmp, ALU.add))
            k.phase_end()
            with ExitStack() as c3:
                rope_loop(k, c3, Q, 0, c("ax_cos"), c("ax_sin"), "q")
            with ExitStack() as c3:
                rope_loop(k, c3, K, TC, c("ax_cos"), c("ax_sin"), "k")
            KS, VS = k.sb("KS1", [P, TA], c2), k.sb("VS", [P, NC, P], c2)
            KZ = k.sb("KZ", [P, 2, NC, P], c2)
            ATT = k.sb("ATT1", [P, NL, P], c2)
            QX = k.sb("QX", [P, 2, T], c2)
            R = k.sb("Rst", [P, 2, NL, P], c2)
            SQ, OS = QX[:, 0, :], QX[:, 1, :]
            RS = k.sb("RS1", [P, T], c2)
            sc = k.sb("ret_scal", [P, 4], c2)
            with nc.Fori(0, RH) as h:
                ds = bass.ds
                t_k = act.go(nc.scalar.copy(KS[:], tile_of(K, h)))
                t_v = act.go(nc.scalar.copy(VS[:], V[:, :, ds(h * P, P)]))
                for d in range(2):
                    dve.go(v.tensor_copy(sc[:, d:d + 1], ZT[:, ds(h + 8 * d, 1)]))
                    t = dve.go(v.tensor_copy(sc[:, 2 + d:3 + d], GC[:, ds(h + 8 * d, 1)]))
                dve.wait(t)
                pe.wait(t_k)
                for c_ in range(NL):
                    mm = nc.tensor.matmul(k.ps[:, 2, c_ * P:(c_ + 1) * P], KS[:, TC + c_ * P:TC + (c_ + 1) * P],
                                          Q[:, ds(h, 1), c_ * P:(c_ + 1) * P].rearrange("p a t -> p (a t)"), start=True, stop=True)
                t_s = pe.go(mm)
                for c_ in range(NC):
                    mm = nc.tensor.transpose(k.ps[:, c_ // 4, (c_ % 4) * P:(c_ % 4 + 1) * P], KS[:, c_ * P:(c_ + 1) * P], k.ident)
                t_t = pe.go(mm)
                dve.wait(t_s)
                dd = DD[:, ds(h, 1), :].broadcast_to([P, NL, P])
                t_att = dve.go(v.tensor_tensor(ATT[:], k.ps[:, 2, :].rearrange("p (c t) -> p c t", c=NL), dd, ALU.mult))
                dve.wait(t_t)
                kt = flat_ps(k, 0, TA)
                for d in range(2):
                    t_kz = dve.go(v.tensor_scalar(KZ[:, d, :, :].rearrange("p c t -> p (c t)"), kt, sc[:, d:d + 1], None, ALU.mult))
                pe.wait(t_kz, t_v)
                ordf, ordb = (0, 1, 2, 3, 4), (1, 0, 5, 4, 3)
                kv = lambda d, n: k.ps[:, 3 + (5 * d + n) // 4, ((5 * d + n) % 4) * P:((5 * d + n) % 4 + 1) * P]
                for d, order in enumerate((ordf, ordb)):
                    for n, c_ in enumerate(order):
                        mm = nc.tensor.matmul(kv(d, n), KZ[:, d, c_, :], VS[:, c_, :], start=True, stop=True)
                t_kv = pe.go(mm)
                for d in range(2):
                    xi = XI[:, d, ds(h, 1), :].broadcast_to([P, NL, P])
                    q = Q[:, ds(h, 1), :].rearrange("p a (c t) -> p (a c) t", t=CH)
                    t_qx = dve.go(v.tensor_tensor(QX[:, d, :].rearrange("p (c t) -> p c t", t=CH), q, xi, ALU.mult))
                dve.wait(t_kv)
                for d in range(2):
                    t0 = dve.go(v.tensor_copy(R[:, d, 0, :], kv(d, 0)))
                dve.wait(t0)
                for n in range(1, 5):
                    for d in range(2):
                        src, dst = R[:, d, max(n - 2, 0), :], R[:, d, n - 1, :]
                        t_r = dve.go(v.scalar_tensor_tensor(dst, src, sc[:, 2 + d:3 + d], kv(d, n), ALU.mult, ALU.add))
                    dve.wait(t_r)
                pe.wait(t_att, t_qx, t_r)
                for c_ in range(NL):
                    o = k.ps[:, 6, c_ * P:(c_ + 1) * P]
                    a = slice(c_ * P, (c_ + 1) * P)
                    nc.tensor.matmul(o, VS[:, 2 + c_, :], ATT[:, c_, :], start=True, stop=False)
                    nc.tensor.matmul(o, R[:, 0, c_, :], QX[:, 0, a], start=False, stop=False)
                    mm = nc.tensor.matmul(o, R[:, 1, NL - 1 - c_, :], QX[:, 1, a], start=False, stop=True)
                t_o = pe.go(mm)
                act.wait(t_o)
                t_sq = act.go(nc.scalar.activation(SQ, k.ps[:, 6, :], ACT.Square))
                pe.wait(t_sq)
                t = pe.go(nc.tensor.matmul(k.ps[:, 7, :], k.ones, SQ, start=True, stop=True))
                t_os = act.go(nc.scalar.copy(OS, k.ps[:, 6, :]))
                rstd(k, RS[:], k.ps[:, 7, :], 1.0 / P, EPS, t)
                dve.wait(t_os)
                t = dve.go(v.tensor_tensor(OS, OS, RS[:], ALU.mult))
                dve.wait(t)
                dve.go(v.tensor_tensor(tile_of(O, h), OS, tile_of(G, h), ALU.mult))
                k.phase_end()
        dense_fm(k, "od_out", 4, O, [(0, T)], lambda n, b: v.tensor_copy(tile_of(Q, n), b[0]))
        act.go(nc.scalar.copy(OUT[:, :, 0:T], Q[:]))
        k.phase_end()


def values(k, name, first, V):
    nc, pe = k.nc, k.pe
    w = k.dram[name]
    NC = TA // P
    nc.vector.sem_inc(k.free_a, NSLOT)
    with nc.Fori(0, 2) as i:
        for s in range(NSLOT):
            k.fetch(w[first + i * NSLOT + s], DT, 2 * P, i, 1)
            k.slab_wait(i, 1)
            wv = k.slab_view(DT, 2 * P)
            slot = k.slab_next()
            pe.wait_reg(k.free_a, i * NSLOT + s + 1)
            for t in range(NC):
                for kk in range(DT):
                    mm = nc.tensor.matmul(k.ps[:, 3 * s + t // 2, (t % 2) * 256:(t % 2 + 1) * 256],
                                          k.H[:, kk, t * P:(t + 1) * P], wv[:, kk, :], start=(kk == 0), stop=(kk == DT - 1))
            mm.then_inc(k.mm_a, 1)
            k.dve.wait_reg(k.mm_a, i * NSLOT + s + 1, slot)
            nc.vector.tensor_copy(V[:, :, bass.ds((i * NSLOT + s) * 256, 256)],
                                  k.ps[:, 3 * s:3 * s + 3, :].rearrange("p b (t n) -> p (b t) n", n=256)).then_inc(k.free_a, 1)
    k.slab_loop(2)
    k.phase_end()


def program(nc, dram, upto=99):
    with ExitStack() as ctx:
        k = Core(nc, ctx, dram)
        setup(k)
        ada(k, "ada0", 24, k.p("c").unsqueeze(2), 1, k.MOD[0], k.p("ada_b0"))
        if upto < 5 or upto > 90:
            ada(k, "ada1", 24, k.p("c").unsqueeze(2), 1, k.MOD[1], k.p("ada_b1"))
            block1_input(k, ctx, 0)
            with ExitStack() as c1:
                R = k.sb("R", [P, DT, T], c1)
                even_mixer1(k, R)
                if upto == 1:
                    return finish(k, R)
                residual_norm(k, R, 0, 0)
                if upto == 2:
                    return finish(k, k.XA)
                ffn(k, 0, R)
                residual_norm(k, R, 0, 1)
                if upto == 3:
                    return finish(k, k.XA)
                pool_mixer(k, R)
                residual_norm(k, R, 1, 0)
                ffn(k, 1, R)
                residual_norm(k, R, 1, 1)
                if upto == 4:
                    return finish(k, k.XA)
        MOD = k.sb("mod2", [P, 24, 2])
        c2 = k.p("c2").rearrange("p (a n) -> p a n", n=2)
        ada(k, "ada2_0", 12, c2, 2, MOD, k.p("ada_b2_0"))
        with ExitStack() as c1:
            XC = k.sb("XC", [P, DT, TC], c1)
            t = k.load(XC[:], dram["ctx"])
            k.loaded(k.act, t)
            k.loaded(k.dve, t)
            k.n_loads = 0
            pre_norm(k, c1, 0, MOD, XC)
        OUT = k.H
        even_mixer2(k, ctx, OUT)
        if upto == 5:
            return finish(k, OUT[:, :, TC:TA])
        with ExitStack() as c1:
            XC = k.sb("XC_b", [P, DT, TC], c1)
            t = k.load(XC[:], dram["ctx"])
            k.loaded(k.dve, t)
            k.n_loads = 0
            post_norm(k, c1, "l", 0, MOD, OUT, k.XA, 0, TC, T)
            post_norm(k, c1, "c", 0, MOD, OUT, XC, 1, 0, TC)
            if upto == 6:
                return finish(k, k.XA)
            ada(k, "ada2_1", 12, c2, 2, MOD, k.p("ada_b2_1"))
            pre_norm(k, c1, 1, MOD, XC)
        odd_mixer2(k, OUT)
        with ExitStack() as c1:
            post_norm(k, c1, "f", 1, MOD, OUT, k.XA, 0, 0, T)
        finish(k, k.XA)


def finish(k, X):
    nc = k.nc
    nc.scalar.dma_start(k.dram["out"], X[:]).then_inc(k.loads, 16)
    nc.scalar.wait_ge(k.loads, 16)


def columns(a):
    a = np.asarray(a)
    return np.ascontiguousarray(a.reshape(-1, P).T)


def slabs(w, cols, tiles=2):
    w = np.asarray(w)[:, cols] if cols is not None else np.asarray(w)
    K, N = w.shape
    n = tiles * P
    return np.ascontiguousarray(w.reshape(K // P, P, N // n, n).transpose(2, 1, 0, 3)).reshape(N // n, P, -1)


def lay_out(a):
    r = np.arange
    out = {}
    fm = lambda x: np.ascontiguousarray(np.asarray(x).T.reshape(DT, P, -1).transpose(1, 0, 2))
    out["x"] = fm(a["x"][0])
    out["ctx"] = fm(a["ctx_2"][0])
    out["positions"] = np.asarray(a["positions"])[0]
    heads = np.concatenate([np.concatenate([r(64) + 64 * j, r(64) + 64 * (j + 4)]) for j in range(4)])
    aq, af, ai, ag = (r(512) + 512 * i for i in range(4))
    bq, bk, bv = 2048 + heads, 2560 + r(128), 2688 + r(128)
    out["ab_in"] = slabs(a["ab_w_in"][0], np.concatenate([aq, af, ag, bq, bk, bv, ai]))
    rows = np.concatenate([r(512), 512 + heads])
    out["ab_out"] = slabs(np.asarray(a["ab_w_out"][0])[rows], None)
    for l in range(DEPTH):
        out[f"ada{l}"] = slabs(a["ada_w"][l], None)
        out[f"ada2_{l}"] = slabs(a["ada_w_2"][l], None)
        uv = np.concatenate([np.concatenate([n * P + r(P), FF + n * P + r(P)]) for n in range(FT)])
        out[f"w_up{l}"] = slabs(a["ffn_w_up"][l], uv)
        out[f"w_down{l}"] = slabs(a["ffn_w_down"][l], None, 1)
    out["pool_w"] = np.ascontiguousarray(np.asarray(a["pool_w"][0]).reshape(4, 2, P, 256).transpose(2, 0, 1, 3)).reshape(1, P, -1)
    tile = lambda n: n * P + r(P)
    order = [tile(n) for n in (18, 19, 26, 27, 28, 29)]
    for j in range(RT):
        order += [tile(j), tile(6 + j), tile(12 + j), tile(20 + j)]
    out["ev_in"] = slabs(a["ev_w_in_2"][0], np.concatenate(order))
    out["ev_out"] = slabs(a["ev_w_out_2"][0], None)
    out["w2"] = np.ascontiguousarray(np.asarray(a["ev_w2_2"][0]).reshape(P, RT * P))
    out["a2"] = np.ascontiguousarray(np.asarray(a["ev_a2_2"][0]).reshape(P, RT * P))
    out["od_in"] = slabs(a["od_w_in_2"][0], None)
    out["od_out"] = slabs(a["od_w_out_2"][0], None)
    p = {}
    p["c"] = columns(a["c"][0])
    p["c2"] = np.stack([columns(a["c_2"][0]), columns(a["c_ctx_2"])], 2).reshape(P, 16)
    for l in range(DEPTH):
        p[f"ada_b{l}"] = columns(a["ada_b"][l])
        p[f"ada_b2_{l}"] = columns(a["ada_b_2"][l])
        cw, cb = np.asarray(a["ffn_conv_w"][l]), np.asarray(a["ffn_conv_b"][l])
        p[f"conv{l}"] = np.stack([columns(cw[0]), columns(cw[1]), columns(cw[2]), columns(cb)], 2).reshape(P, -1)
    p["ln_g"], p["ln_b"] = columns(a["ln_g"]), columns(a["ln_b"])
    p["lb_raw"] = columns(a["hgrn_lb_raw"][0])
    p["norm_g"] = columns(a["hgrn_norm_g"][0])
    p["sinks"] = np.broadcast_to(np.asarray(a["attn_sinks"][0]).reshape(1, 8), (P, 8))
    p["pool_scale"] = columns(a["pool_scale"][0])
    p["norm_pre"], p["norm_post"] = columns(a["norm_pre_2"]), columns(a["norm_post_2"])
    p["mu"] = columns(a["ev_mu_2"][0])
    rw = [a["ev_w0_2"][0][0], a["ev_w0_2"][0][1], a["ev_a0_2"][0][0], a["ev_a0_2"][0][1], a["ev_k_k_2"][0],
          a["ev_k_a_2"][0], np.asarray(a["ev_r_k_2"][0]).reshape(-1), a["ev_lnx_g_2"][0], a["ev_lnx_b_2"][0]]
    p["rw"] = np.stack([columns(x) for x in rw], 2).reshape(P, -1)
    p["decay"] = np.broadcast_to(np.asarray(a["od_decay_logit_2"][0]).reshape(1, 16), (P, 16))
    out["params"] = np.concatenate([p[n] for n, _ in PARAMS], 1)
    out["consts"], out["consts2"], out["dft"] = constants()
    return out


def kernel(**inputs):
    import concourse.bacc as _bacc
    from concourse.bass_utils import run_bass_kernel_spmd as _run

    arrays = lay_out(inputs)
    nc = _bacc.Bacc("TRN2", target_bir_lowering=False, num_devices=1)
    dram = {n: nc.dram_tensor(n, x.shape, mybir.dt.from_np(x.dtype), kind="ExternalInput").ap()
            for n, x in arrays.items()}
    dram["out"] = nc.dram_tensor("out", (P, DT, T), F32, kind="ExternalOutput").ap()
    program(nc, dram)
    r = _run(nc, [arrays], core_ids=[0])
    y = np.asarray(r.results[0]["out"])
    return np.ascontiguousarray(y.transpose(2, 1, 0).reshape(1, T, D))
```

```python
from contextlib import ExitStack
import math

import numpy as np
import concourse.bass as bass
from concourse import mybir

F32 = mybir.dt.float32
I32 = mybir.dt.int32
ALU = mybir.AluOpType
ACT = mybir.ActivationFunctionType
AX = mybir.AxisListType

P = 128
D = 1024
DT = D // P
T = 512
TC = 256
TA = T + TC
DEPTH = 2
FF = 2816
FT = FF // P
ALPHA = (2.0 * DEPTH) ** 0.25
LN_EPS, RMS_EPS, EPS, GN_EPS = 1e-5, 1e-6, 1e-6, 64e-5
ROPE_THETA, ROPE_BASE = 500000.0, 10000.0
AH = 4
BH, BD = 8, 64
RT = 6
RH = 8
GRID_W = 64
POOL_WINDOWS = (2, 4, 8, 16)
NSLOT = 2
SLOT = FT * P
CH = 128
LEVELS = 7
LEAD = 2

PARAMS = [
    ("c", 8), ("c2", 16),
    ("ada_b0", 48), ("ada_b1", 48), ("ada_b2_0", 24), ("ada_b2_1", 24),
    ("ln_g", 32), ("ln_b", 32), ("lb_raw", 4), ("norm_g", 1), ("sinks", 8), ("pool_scale", 8),
    ("conv0", 4 * FT), ("conv1", 4 * FT),
    ("norm_pre", 16), ("norm_post", 16),
    ("mu", 20), ("rw", 9 * RT),
    ("decay", 16),
]
CONSTS = [
    ("ident", P), ("ones", P), ("blk64", P), ("rope_perm", P), ("swap64", P),
    ("inv_freq", 1), ("rope_sign", 1), ("type4", 4), ("type2", 2),
    ("low", LEVELS * P),
    ("up", LEVELS * P),
    ("band", 256), ("pool_cnt", 4 * 16), ("scan_reset", TA),
    ("strict_low", P), ("strict_up", P), ("incl_low", P), ("incl_up", P), ("ident64", 64), ("top_ident", P), ("eps", 3),
]
CONSTS2 = [
    ("dist_f", P), ("dist_b", P), ("pos1", P), ("pos1r", P), ("zpos", 2),
    ("ax_cos", T), ("ax_sin", T),
]
DFT = [("c512", 4 * T), ("s512", 4 * T), ("c256", 2 * TC), ("s256", 2 * TC), ("f64", 2 * P)]


def offsets(items):
    at, out = 0, {}
    for name, n in items:
        out[name] = (at, n)
        at += n
    return out, at


P_AT, P_N = offsets(PARAMS)
C_AT, C_N = offsets(CONSTS)
C2_AT, C2_N = offsets(CONSTS2)
F_AT, F_N = offsets(DFT)


def constants():
    p = np.arange(P)
    t = {}
    t["ident"] = np.eye(P)
    t["ones"] = np.ones((P, P))
    t["blk64"] = (p[:, None] // 64 == p[None] // 64)
    perm = np.zeros((P, P))
    for m in range(P):
        if m % 64 < 8:
            perm[m + 8, m] = 1
        elif m % 64 < 16:
            perm[m - 8, m] = 1
    t["rope_perm"] = perm
    t["swap64"] = (p[:, None] == (p[None] + 64) % P)
    inv = ROPE_THETA ** (-np.arange(0, 16, 2) / 16.0)
    t["inv_freq"] = np.where(p % 64 < 16, inv[p % 8], 0.0)[:, None]
    t["rope_sign"] = np.where(p % 64 < 8, -1.0, 1.0)[:, None]
    t["type4"] = (p[:, None] % 4 == np.arange(4)[None])
    t["type2"] = (p[:, None] % 2 == np.arange(2)[None])
    low = np.zeros((P, LEVELS, P))
    for m in range(LEVELS):
        n = 2 << m
        same = p[:, None] // n == p[None] // n
        low[:, m] = same & (p[:, None] % n >= n // 2) & (p[None] % n < n // 2)
    t["low"] = low.reshape(P, -1)
    t["up"] = low.transpose(2, 1, 0).reshape(P, -1)
    k = np.arange(256)
    rel = p[:, None] + 128 - k[None]
    t["band"] = np.where((rel >= 0) & (rel < 128), 0.0, -1e30)
    w = np.array(POOL_WINDOWS)[:, None]
    t["pool_cnt"] = np.broadcast_to((1.0 / np.minimum(np.arange(16)[None] + 1, w)).reshape(1, -1), (P, 64))
    t["scan_reset"] = np.broadcast_to((np.arange(TA) % CH != 0)[None], (P, TA))
    t["strict_low"] = p[:, None] > p[None]
    t["strict_up"] = p[:, None] < p[None]
    t["incl_low"] = p[:, None] >= p[None]
    t["incl_up"] = p[:, None] <= p[None]
    t["ident64"] = p[:, None] % 64 == np.arange(64)[None]
    t["top_ident"] = p[:, None] % 64 == p[None]
    t["eps"] = np.broadcast_to(np.array([[LN_EPS, EPS, GN_EPS]]), (P, 3))
    c1 = np.concatenate([np.asarray(t[n], np.float32) for n, _ in CONSTS], 1)
    q = {}
    q["dist_f"] = np.maximum(p[None] - p[:, None], 0)
    q["dist_b"] = np.maximum(p[:, None] - p[None], 0)
    q["pos1"] = np.broadcast_to(p[None] + 1, (P, P))
    q["pos1r"] = np.broadcast_to(P - p[None], (P, P))
    q["zpos"] = np.stack([P - 1 - p, p], 1)
    rope = ROPE_BASE ** (-np.arange(0, 64, 2) / 64.0)
    pos = np.arange(T)
    rc = np.stack([pos // GRID_W, pos % GRID_W], 1)
    ang = (rc[:, :, None] * rope.astype(np.float32)).reshape(T, 64).T
    q["ax_cos"] = np.concatenate([np.cos(ang), np.cos(ang)])
    q["ax_sin"] = np.concatenate([-np.sin(ang), np.sin(ang)])
    c2 = np.concatenate([np.asarray(q[n], np.float32) for n, _ in CONSTS2], 1)
    f = {}
    for n, L in ((512, T), (256, TC)):
        a = 2 * np.pi * np.outer(np.arange(L), np.arange(L)) / L
        s = 1.0 / math.sqrt(L * 64)
        f[f"c{n}"] = (s * np.cos(a)).reshape(L // P, P, L).transpose(1, 0, 2).reshape(P, -1)
        f[f"s{n}"] = (-s * np.sin(a)).reshape(L // P, P, L).transpose(1, 0, 2).reshape(P, -1)
    a = 2 * np.pi * np.outer(np.arange(64), np.arange(64)) / 64
    z = np.zeros((64, 64))
    f["f64"] = np.concatenate([np.block([[g, z], [z, g]]) for g in (np.cos(a), np.sin(a))], 1)
    c3 = np.concatenate([np.asarray(f[n], np.float32) for n, _ in DFT], 1)
    return c1, c2, c3


class Queue:

    def __init__(self, eng, sem):
        self.eng, self.sem, self.n, self.seen = eng, sem, 0, {}

    def wait(self, *tokens):
        for sem, value in tokens:
            if self.seen.get(sem.num, 0) < value:
                self.eng.wait_ge(sem, value)
                self.seen[sem.num] = value

    def go(self, ins):
        ins.then_inc(self.sem, 1)
        self.n += 1
        return (self.sem, self.n)

    def wait_reg(self, sem, value, frees=None):
        self.eng.wait_ge(sem, value)
        nop = self.eng.nop()
        if frees is not None:
            nop.then_inc(frees, 1)


class Core:
    def __init__(self, nc, ctx, dram):
        self.nc, self.ctx, self.dram = nc, ctx, dram
        sems = [ctx.enter_context(nc.semaphore(n)) for n in (
            "pe_done", "dve_done", "act_done", "pool_done",
            "mm_a", "mm_b", "free_a", "free_b", "loop_1", "loop_2", "loop_3", "loop_4", "chain", "loads")]
        self.cleared = range(sems[0].num, sems[-1].num + 1)
        assert [s.num for s in sems] == list(self.cleared)
        self.pe = Queue(nc.tensor, sems[0])
        self.dve = Queue(nc.vector, sems[1])
        self.act = Queue(nc.scalar, sems[2])
        self.pool = Queue(nc.gpsimd, sems[3])
        (self.mm_a, self.mm_b, self.free_a, self.free_b, self.l1, self.l2, self.l3, self.l4,
         self.chain, self.loads) = sems[4:]
        self.n_loads = 0
        self.full = [ctx.enter_context(nc.semaphore(f"slot_full{i}")) for i in range(NSLOT)]
        self.free = [ctx.enter_context(nc.semaphore(f"slot_free{i}")) for i in range(NSLOT)]
        self.ring = self.sb("ring", [P, NSLOT, SLOT])
        self.slab = 0
        self.ps = ctx.enter_context(nc.psum_tensor("ps", [P, 8, 512], F32))
        for s in self.free:
            nc.sync.sem_inc(s, 1)

    def sb(self, name, shape, ctx=None, dt=F32):
        return (ctx or self.ctx).enter_context(self.nc.sbuf_tensor(name, shape, dt))

    def phase_end(self):
        assert self.n_loads == 0
        self.nc.multi_engine_barrier([q.eng.engine for q in (self.pe, self.dve, self.act, self.pool)],
                                     sems_to_clear=self.cleared)
        for q in (self.pe, self.dve, self.act, self.pool):
            q.n, q.seen = 0, {}

    def load(self, out, in_, *after):
        self.act.wait(*after)
        self.nc.scalar.dma_start(out, in_).then_inc(self.loads, 16)
        self.n_loads += 16
        return (self.loads, self.n_loads)

    def loaded(self, q, token):
        q.wait((self.loads, self.n_loads))

    def fetch(self, src, kt, width, i=0, per=0):
        slot, use = self.slab % NSLOT, self.slab // NSLOT
        self.nc.sync.wait_ge(self.free[slot], use + 1 + i * per)
        self.nc.sync.dma_start(self.ring[:, slot, 0:kt * width], src).then_inc(self.full[slot], 16)

    def slab_view(self, kt, width):
        return self.ring[:, self.slab % NSLOT, 0:kt * width].rearrange("p (k n) -> p k n", k=kt)

    def slab_wait(self, i=0, per=0):
        slot, use = self.slab % NSLOT, self.slab // NSLOT
        self.nc.tensor.wait_ge(self.full[slot], 16 * (use + 1) + i * (16 * per))
        if per:
            self.nc.tensor.nop()

    def slab_next(self):
        self.slab += 1
        return self.free[(self.slab - 1) % NSLOT]

    def slab_loop(self, iters):
        self.slab += NSLOT * (iters - 1)


def dense_fm(k, name, slabs, rhs, splits, evac, kt=8, tiles=2, first=0, end=True):
    nc, pe = k.nc, k.pe
    w = k.dram[name]
    nb = len(splits)
    per_iter = NSLOT * tiles
    assert per_iter * nb <= 8
    nc.vector.sem_inc(k.free_a, per_iter)

    def body(i, n_slabs, per):
        k.chain_n = 0
        for s in range(n_slabs):
            k.fetch(w[first + i * NSLOT + s], kt, tiles * P, i * per, 1)
            k.slab_wait(i * per, 1)
            wv = k.slab_view(kt, tiles * P)
            slot = k.slab_next()
            for a in range(tiles):
                g = s * tiles + a
                pe.wait_reg(k.free_a, i * per_iter + g + 1)
                for b, (t0, tn) in enumerate(splits):
                    for kk in range(kt):
                        mm = nc.tensor.matmul(k.ps[:, g * nb + b, 0:tn], wv[:, kk, a * P:(a + 1) * P],
                                              rhs[:, kk, t0:t0 + tn], start=(kk == 0), stop=(kk == kt - 1))
                mm.then_inc(k.mm_a, 1)
                k.dve.wait_reg(k.mm_a, i * per_iter + g + 1, slot if a == tiles - 1 else None)
                evac(i * per_iter + g, [k.ps[:, g * nb + b, 0:tn] for b, (_, tn) in enumerate(splits)])\
                    .then_inc(k.free_a, 1)
        if k.chain_n:
            nc.vector.wait_ge(k.chain, k.chain_n)
            nc.vector.nop()
            nc.vector.sem_clear(k.chain)

    iters = slabs // NSLOT
    if iters:
        with nc.Fori(0, iters) as i:
            body(i, NSLOT, 1)
        k.slab_loop(iters)
    if slabs % NSLOT:
        body(iters, 1, 0)
    if end:
        k.phase_end()


def chained(k, ins):
    k.chain_n += 1
    ins.then_inc(k.chain, 1)
    k.nc.vector.wait_ge(k.chain, k.chain_n)
    k.nc.vector.nop()


def ada(k, name, slabs, c, n, out, bias):
    nc, pe, dve = k.nc, k.pe, k.dve
    width = 2 * P
    rows = k.H[:].rearrange("p a t -> p (a t)")
    nc.vector.sem_inc(k.free_a, NSLOT)
    with nc.Fori(0, slabs // NSLOT) as i:
        for s in range(NSLOT):
            k.fetch(k.dram[name][i * NSLOT + s], DT, width, i, 1)
            k.slab_wait(i, 1)
            wv = k.slab_view(DT, width)
            slot = k.slab_next()
            pe.wait_reg(k.free_a, i * NSLOT + s + 1)
            for kk in range(DT):
                mm = nc.tensor.matmul(k.ps[0:n, s, 0:width], c[:, kk, :], wv[:, kk, :], start=(kk == 0), stop=(kk == DT - 1))
            mm.then_inc(k.mm_a, 1)
            dve.wait_reg(k.mm_a, i * NSLOT + s + 1, slot)
            nc.vector.tensor_copy(rows[0:n, bass.ds((i * NSLOT + s) * width, width)], k.ps[0:n, s, 0:width]).then_inc(k.free_a, 1)
    k.slab_loop(slabs // NSLOT)
    k.phase_end()
    with ExitStack() as ctx:
        tiles = 2 * slabs
        by_tile = k.sb("by_tile_" + name, [n * tiles, P], ctx)
        for j in range(n):
            t = k.load(by_tile[j * tiles:(j + 1) * tiles, :], rows[j:j + 1, 0:tiles * P].rearrange("p (a m) -> p a m", m=P))
        k.loaded(pe, t)
        t = pe.go(nc.tensor.transpose(k.ps[:, 2, 0:n * tiles], by_tile[:], k.ident[0:n * tiles, 0:n * tiles]))
        dve.wait(t)
        for j in range(n):
            dve.go(nc.vector.tensor_tensor(out[:, :, j], k.ps[:, 2, j * tiles:(j + 1) * tiles], bias, ALU.add))
        k.n_loads = 0
        k.phase_end()


def layer_norm(k, ctx, R, eps, outs, what):
    nc, pe, dve, act = k.nc, k.pe, k.dve, k.act
    sq = k.sb("ln_sq_" + what, [P, DT, T], ctx)
    mu = k.sb("ln_mu_" + what, [P, T], ctx)
    rs = k.sb("ln_rs_" + what, [P, T], ctx)
    for kk in range(DT):
        mm = nc.tensor.matmul(k.ps[:, 0, :], k.ones, R[:, kk, :], start=(kk == 0), stop=(kk == DT - 1))
    t_sum = pe.go(mm)
    dve.wait(t_sum)
    dve.wait(dve.go(nc.vector.tensor_scalar(mu[:], k.ps[:, 0, :], 1.0 / D, None, ALU.mult)))
    part = DT // 4
    for j in range(4):
        r = R[:, j * part:(j + 1) * part, :]
        t_sub = dve.go(nc.vector.tensor_tensor(r, r, mu[:].unsqueeze(1).broadcast_to([P, part, T]), ALU.subtract))
        act.wait(t_sub)
        t_sq = act.go(nc.scalar.activation(sq[:, j * part:(j + 1) * part, :], r, ACT.Square))
        pe.wait(t_sq)
        for kk in range(j * part, (j + 1) * part):
            mm = nc.tensor.matmul(k.ps[:, 1, :], k.ones, sq[:, kk, :], start=(kk == 0), stop=(kk == DT - 1))
    t_var = pe.go(mm)
    rstd(k, rs[:], k.ps[:, 1, :], 1.0 / D, eps, t_var)
    for j in range(4):
        r = R[:, j * part:(j + 1) * part, :]
        t_n = dve.go(nc.vector.tensor_tensor(r, r, rs[:].unsqueeze(1).broadcast_to([P, part, T]), ALU.mult))
        for queues, dst, scale, bias in outs:
            for kk in range(j * part, (j + 1) * part):
                q = queues[kk % 2]
                q.wait(t_n)
                affine(q, dst[:, kk, :], R[:, kk, :], scale[:, kk:kk + 1], bias[:, kk:kk + 1])


def affine(q, out, x, scale, bias):
    if hasattr(q.eng, "activation"):
        return q.go(q.eng.activation(out, x, ACT.Identity, bias=bias, scale=scale))
    return q.go(q.eng.tensor_scalar(out, x, scale, bias, ALU.mult, ALU.add))


def rstd(k, out, x, scale, eps, token):
    nc, dve, act = k.nc, k.dve, k.act
    act.wait(token)
    bias = k.c("eps", {LN_EPS: 0, EPS: 1, GN_EPS: 2}[eps], 1)
    t = act.go(nc.scalar.activation(out, x, ACT.Ln, bias=bias, scale=scale))
    act.wait(t)
    t = act.go(nc.scalar.activation(out, out, ACT.Exp, scale=-0.5))
    dve.wait(t)
    return t


def transpose_fp32(k, out, x):
    return k.nc.tensor.transpose(out, x, k.ident)


def setup(k):
    nc, act, dve = k.nc, k.act, k.dve
    k.par = k.sb("params_sb", [P, P_N])
    k.cst = k.sb("consts_sb", [P, C_N])
    k.XA = k.sb("XA", [P, DT, T])
    k.H = k.sb("H", [P, DT, TA])
    k.MOD = [k.sb("mod0", [P, 48, 1]), k.sb("mod1", [P, 48, 1])]
    k.sc = k.sb("scalars", [P, 8, 8])
    k.p = lambda name, a=0, n=None: k.par[:, P_AT[name][0] + a:P_AT[name][0] + a + (P_AT[name][1] - a if n is None else n)]
    k.c = lambda name, a=0, n=None: k.cst[:, C_AT[name][0] + a:C_AT[name][0] + a + (C_AT[name][1] - a if n is None else n)]
    k.ident, k.ones = k.c("ident"), k.c("ones")
    k.load(k.par[:], k.dram["params"])
    k.load(k.cst[:], k.dram["consts"])
    t = k.load(k.XA[:], k.dram["x"])
    k.loaded(act, t)
    k.loaded(dve, t)
    k.loaded(k.pe, t)
    k.loaded(k.pool, t)
    for name in ("c", "c2"):
        act.go(nc.scalar.activation(k.p(name), k.p(name), ACT.Silu))
    k.n_loads = 0
    k.phase_end()


def block1_input(k, ctx, l, scale_only=False):
    nc, dve, act, pool = k.nc, k.dve, k.act, k.pool
    m = k.MOD[l]
    one_sc = k.sc[:, 0, :]
    t = dve.go(nc.vector.tensor_scalar(one_sc, m[:, 8:16, 0], 1.0, None, ALU.add))
    act.wait(t)
    for kk in range(DT):
        t = affine(act, k.H[:, kk, 0:T], k.XA[:, kk, :], one_sc[:, kk:kk + 1], m[:, kk, :])
        dve.wait(t)
        dve.go(nc.vector.tensor_scalar(k.XA[:, kk, :], k.XA[:, kk, :], ALPHA, None, ALU.mult))
    k.phase_end()


def ln_scalars(k, l, i, sh, sc, final=False):
    nc, dve = k.nc, k.dve
    g, b = k.p("ln_g", (2 * l + i) * 8, 8), k.p("ln_b", (2 * l + i) * 8, 8)
    if final:
        return g, b, None, None
    ga, ba, gh, bh = (k.sc[:, j, :] for j in range(1, 5))
    dve.go(nc.vector.tensor_scalar(ga, g, ALPHA, None, ALU.mult))
    dve.go(nc.vector.tensor_scalar(ba, b, ALPHA, None, ALU.mult))
    t = dve.go(nc.vector.tensor_scalar(bh, sc, 1.0, None, ALU.add))
    dve.wait(t)
    dve.wait(dve.go(nc.vector.tensor_tensor(gh, g, bh, ALU.mult)))
    dve.wait(dve.go(nc.vector.tensor_tensor(bh, b, bh, ALU.mult)))
    dve.wait(dve.go(nc.vector.tensor_tensor(bh, bh, sh, ALU.add)))
    return ga, ba, gh, bh


def residual_norm(k, R, l, i):
    m = k.MOD
    with ExitStack() as ctx:
        if i == 0:
            ga, ba, gh, bh = ln_scalars(k, l, 0, m[l][:, 24:32, 0], m[l][:, 32:40, 0])
        elif l + 1 < DEPTH:
            ga, ba, gh, bh = ln_scalars(k, l, 1, m[l + 1][:, 0:8, 0], m[l + 1][:, 8:16, 0])
        else:
            ga, ba, gh, bh = ln_scalars(k, l, 1, None, None, final=True)
        outs = [((k.act, k.act), k.H[:, :, 0:T], gh, bh), ((k.pool, k.dve), k.XA, ga, ba)]
        if gh is None:
            outs = [((k.act, k.dve), k.XA, ga, ba)]
        layer_norm(k, ctx, R, LN_EPS, outs, f"{l}{i}")
        k.phase_end()


def ffn(k, l, R):
    nc, pe, dve, act = k.nc, k.pe, k.dve, k.act
    with ExitStack() as ctx:
        G = k.sb(f"G{l}", [P, FT, T], ctx)
        U = k.sb(f"U{l}", [P, NSLOT, T + 2], ctx)
        C = k.sb(f"C{l}", [P, NSLOT, T], ctx)
        cw = k.p(f"conv{l}")
        dve.go(nc.vector.memset(U[:, :, 0:2], 0.0))
        for s in (k.free_a, k.free_b, k.l2):
            nc.vector.sem_inc(s, NSLOT)
        k.phase_end_keep()
        with nc.Fori(0, FT // NSLOT) as i:
            for s in range(NSLOT):
                n = i * NSLOT + s
                k.fetch(k.dram[f"w_up{l}"][i * NSLOT + s], DT, 2 * P, i, 1)
                k.slab_wait(i, 1)
                wv = k.slab_view(DT, 2 * P)
                slot = k.slab_next()
                pu, pv = k.ps[:, 2 * s, :], k.ps[:, 2 * s + 1, :]
                pe.wait_reg(k.free_a, n + 1)
                for kk in range(DT):
                    mm = nc.tensor.matmul(pu, wv[:, kk, 0:P], k.H[:, kk, 0:T], start=(kk == 0), stop=(kk == DT - 1))
                mm.then_inc(k.mm_a, 1)
                pe.wait_reg(k.free_b, n + 1)
                for kk in range(DT):
                    mm = nc.tensor.matmul(pv, wv[:, kk, P:2 * P], k.H[:, kk, 0:T], start=(kk == 0), stop=(kk == DT - 1))
                mm.then_inc(k.mm_b, 1)
                act.wait_reg(k.mm_a, n + 1)
                act.wait_reg(k.l2, n + 1)
                nc.scalar.copy(U[:, s, 2:T + 2], pu).then_inc(k.free_a, 1)
                dve.wait_reg(k.free_a, n + 1 + NSLOT)
                w = lambda j: cw[:, bass.ds(4 * n + j, 1)]
                dve.eng.tensor_scalar(C[:, s, :], U[:, s, 2:T + 2], w(2), w(3), ALU.mult, ALU.add).then_inc(k.chain, 1)
                dve.eng.wait_ge(k.chain, 2 * s + 1)
                dve.eng.nop()
                dve.eng.scalar_tensor_tensor(C[:, s, :], U[:, s, 1:T + 1], w(1), C[:, s, :], ALU.mult, ALU.add).then_inc(k.chain, 1)
                dve.eng.wait_ge(k.chain, 2 * s + 2)
                dve.eng.nop()
                dve.eng.scalar_tensor_tensor(C[:, s, :], U[:, s, 0:T], w(0), C[:, s, :], ALU.mult, ALU.add).then_inc(k.l2, 1)
                act.wait_reg(k.l2, n + 1 + NSLOT)
                nc.scalar.activation(C[:, s, :], C[:, s, :], ACT.Silu).then_inc(k.l3, 1)
                dve.wait_reg(k.l3, n + 1)
                dve.wait_reg(k.mm_b, n + 1, slot)
                dve.eng.tensor_tensor(G[:, bass.ds(n, 1), :].rearrange("p a t -> p (a t)"), C[:, s, :], pv, ALU.mult).then_inc(k.free_b, 1)
            nc.vector.sem_clear(k.chain)
        k.slab_loop(FT // NSLOT)
        k.phase_end()
        g2 = k.MOD[l][:, 40:48, 0]

        def evac(n, banks):
            return nc.vector.scalar_tensor_tensor(
                R[:, bass.ds(n, 1), :].rearrange("p a t -> p (a t)"), banks[0], g2[:, bass.ds(n, 1)],
                k.XA[:, bass.ds(n, 1), :].rearrange("p a t -> p (a t)"), ALU.mult, ALU.add)
        dense_fm(k, f"w_down{l}", 8, G, [(0, T)], evac, kt=FT, tiles=1)


def phase_end_keep(self):
    self.nc.multi_engine_barrier([q.eng.engine for q in (self.pe, self.dve, self.act, self.pool)],
                                 sems_to_clear=range(self.pe.sem.num, self.pool.sem.num + 1))
    for q in (self.pe, self.dve, self.act, self.pool):
        q.n, q.seen = 0, {}


Core.phase_end_keep = phase_end_keep


def tile_of(buf, n):
    return buf[:, bass.ds(n, 1), :].rearrange("p a t -> p (a t)")


def sincos(k, COS, SIN, pos, ang, n):
    nc, dve, act = k.nc, k.dve, k.act
    t = k.load(pos, k.dram["positions"].partition_broadcast(P))
    k.loaded(dve, t)
    v = nc.vector

    def step(ins):
        t = dve.go(ins)
        yield
        dve.wait(t)
        return t
    yield from step(v.tensor_copy(ang, pos))
    yield from step(v.tensor_scalar(ang, ang, k.c("inv_freq"), None, ALU.mult))
    magic = 1.5 * 2.0 ** 23
    yield from step(v.tensor_scalar(n, ang, 1.0 / (2 * math.pi), magic, ALU.mult, ALU.add))
    yield from step(v.tensor_scalar(n, n, magic, None, ALU.subtract))
    c1 = 6.28125
    c2 = math.floor((2 * math.pi - c1) * 2 ** 22) / 2 ** 22
    c3 = 2 * math.pi - c1 - c2
    for c in (c1, c2, c3):
        yield from step(v.scalar_tensor_tensor(ang, n, -c, ang, ALU.mult, ALU.add))
    top = 3.1415925
    yield from step(v.tensor_scalar(ang, ang, top, -top, ALU.min, ALU.max))
    yield from step(v.tensor_scalar(COS[:], ang, math.pi / 2, None, ALU.add))
    yield from step(v.tensor_scalar(n, COS[:], math.pi, -2 * math.pi, ALU.is_gt, ALU.mult))
    yield from step(v.tensor_tensor(COS[:], COS[:], n, ALU.add))
    t = yield from step(v.tensor_scalar(COS[:], COS[:], top, -top, ALU.min, ALU.max))
    act.wait(t)
    act.go(nc.scalar.activation(COS[:], COS[:], ACT.Sin))
    t = act.go(nc.scalar.activation(SIN[:], ang, ACT.Sin))
    dve.wait(t)
    yield
    return (yield from step(v.tensor_scalar(SIN[:], SIN[:], k.c("rope_sign"), None, ALU.mult)))


def even_mixer1(k, R):
    nc, pe, dve, act, pool = k.nc, k.pe, k.dve, k.act, k.pool
    v = nc.vector
    with ExitStack() as ctx:
        Z = k.sb("Z", [P, 17, T], ctx)
        VA = k.sb("VA", [P, 4, 512], ctx)
        VB = k.sb("VB", [P, 4, P], ctx)
        dense_fm(k, "ab_in", 8, k.H, [(0, T)], lambda n, banks: v.tensor_copy(tile_of(Z, n), banks[0]))
        PT = k.sb("probs_T", [P, 2 * BH, P], ctx)
        COS, SIN = k.sb("COS", [P, T], ctx), k.sb("SIN", [P, T], ctx)
        ROT = flat(PT[:]).rearrange("p (j t) -> p j t", t=T)
        angles = sincos(k, COS, SIN, ROT[:, 0, :].bitcast(I32), ROT[:, 1, :], ROT[:, 2, :])
        w = k.dram["ab_in"]
        for s in range(3):
            k.fetch(w[8 + s], DT, 2 * P)
            k.slab_wait()
            wv = k.slab_view(DT, 2 * P)
            slot = k.slab_next()
            if s == 0:
                for kk in range(DT):
                    mm = nc.tensor.matmul(k.ps[:, 0, :], wv[:, kk, 0:P], k.H[:, kk, 0:T], start=(kk == 0), stop=(kk == DT - 1))
                t_k = pe.go(mm)
                act.wait(t_k)
                t_copied = act.go(nc.scalar.copy(Z[:, 16, :], k.ps[:, 0, :]))
                t_read = []
            lo, hi = (P, 2 * P) if s == 0 else (0, 2 * P)
            for t in range(4):
                bank = k.ps[:, (4 * (s + 1) + t) % 8, 0:hi - lo]
                if s == 1 and t == 0:
                    pe.wait(t_copied)
                if s == 2:
                    pe.wait(t_read[t])
                for kk in range(DT):
                    mm = nc.tensor.matmul(bank, k.H[:, kk, t * P:(t + 1) * P], wv[:, kk, lo:hi], start=(kk == 0), stop=(kk == DT - 1))
                t_v = pe.go(mm)
                dve.wait(t_v)
                dst = VB[:, t, :] if s == 0 else VA[:, t, (s - 1) * 256:s * 256]
                t_read.append(dve.go(v.tensor_copy(dst, bank)))
                for _ in range(2):
                    next(angles, None)
            dve.eng.nop().then_inc(slot, 1)
        for _ in angles:
            pass
        k.n_loads = 0
        k.phase_end()
        OA = k.H[:, 0:4, 0:T]
        OB = k.H[:, 4:8, 0:T]
        hgrn(k, Z, VA, OA, lambda *place: attention(k, Z, VB, OB, COS, SIN, PT, ROT, *place))
    g1 = k.MOD[0][:, 16:24, 0]
    dense_fm(k, "ab_out", 4, k.H, [(0, T)], lambda n, banks: v.scalar_tensor_tensor(
        tile_of(R, n), banks[0], g1[:, bass.ds(n, 1)], tile_of(k.XA, n), ALU.mult, ALU.add))


def hgrn(k, Z, VA, OA, attention):
    nc, pe, dve, act, pool = k.nc, k.pe, k.dve, k.act, k.pool
    v = nc.vector
    NCH = T // CH
    with ExitStack() as ctx:
        B = k.sb("B", [P, AH, T], ctx)
        K = k.sb("K", [P, AH, T], ctx)
        E = k.sb("E", [P, AH, T], ctx)
        S = k.sb("S", [P, 2, AH, P], ctx)
        ATT = k.sb("ATT", [P, AH, T], ctx)
        KT = k.sb("KT", [P, AH, T], ctx)
        lbs = k.sb("lbs", [P, 3, AH], ctx)
        stream = attention(KT, k.sb("stats", [P, 4, BH], ctx))
        q, fz, ag = Z[:, 0:4, :], Z[:, 4:8, :], Z[:, 8:12, :]

        def step(ins):
            t = dve.go(ins)
            dve.wait(t)
            return t
        raw, lb, one = k.p("lb_raw"), lbs[:, 0, :], lbs[:, 1, :]
        step(v.tensor_tensor(lb, raw, raw, ALU.subtract))
        act.wait(dve.go(v.memset(lbs[:, 2, :], 0.0)))
        t = act.go(nc.scalar.activation(one, lb, ACT.Exp))
        dve.wait(t)
        step(v.reciprocal(lbs[:, 2, :], one))
        step(v.tensor_tensor(one, one, lbs[:, 2, :], ALU.mult))
        step(v.tensor_tensor(lb, one, one, ALU.subtract))
        step(v.tensor_scalar(one, lb, -1.0, 1.0, ALU.mult, ALU.add))
        def scores():
            act.go(nc.scalar.activation(K[:], fz, ACT.Sigmoid, scale=-1.0))
            t = act.go(nc.scalar.activation(B[:], fz, ACT.Sigmoid))
            yield
            dve.wait(t)
            for h in range(AH):
                dve.go(v.tensor_scalar(K[:, h, :], K[:, h, :], one[:, h:h + 1], None, ALU.mult))
                yield
                dve.go(v.tensor_scalar(B[:, h, :], B[:, h, :], one[:, h:h + 1], lb[:, h:h + 1], ALU.mult, ALU.add))
            dve.wait((dve.sem, dve.n))
            yield
            t = step(v.tensor_scalar(B[:], B[:], 2.0 ** -63, None, ALU.max))
            act.wait(t)
            t = act.go(nc.scalar.activation(E[:], B[:], ACT.Ln))
            yield
            dve.wait(t)
            for h in range(AH):
                t = dve.go(v.tensor_tensor_scan(B[:, h, :], k.c("scan_reset", 0, T), E[:, h, :], 0.0, ALU.mult, ALU.add))
            dve.wait(t)
            t_scores = None
            for m in range(LEVELS + 1):
                if m < LEVELS:
                    half = 1 << m
                    vw = lambda a: a.rearrange("p h (b s j) -> p (h b) s j", s=2, j=half)
                    nb = AH * T // (2 * half)
                    b4, e4 = vw(B[:]), vw(E[:])
                    mid = b4[:, :, 0, half - 1:half].broadcast_to([P, nb, half])
                    if t_scores is not None:
                        dve.wait(t_scores)
                    dve.go(v.tensor_tensor(e4[:, :, 1, :], b4[:, :, 1, :], mid, ALU.subtract))
                    t = dve.go(v.tensor_tensor(e4[:, :, 0, :], mid, b4[:, :, 0, :], ALU.subtract))
                    yield
                    act.wait(t)
                    t = act.go(nc.scalar.activation(E[:], E[:], ACT.Exp))
                    yield
                    dve.wait(t)
                    dve.go(v.tensor_tensor(e4[:, :, 1, :], e4[:, :, 1, :], vw(q)[:, :, 1, :], ALU.mult))
                    t = dve.go(v.tensor_tensor(e4[:, :, 0, :], e4[:, :, 0, :], vw(K[:])[:, :, 0, :], ALU.mult))
                    lhs, rhs = E, E
                else:
                    lhs, rhs = K, q
                yield
                pe.wait(t)
                if m:
                    pe.wait(tok)
                for h in range(AH):
                    for c in range(NCH):
                        a = slice(c * CH, (c + 1) * CH)
                        mm = nc.tensor.matmul(k.ps[:, h, a], lhs[:, h, a], rhs[:, h, a], start=True, stop=True)
                t_scores = pe.go(mm)
                yield
                dve.wait(t_scores)
                scores = k.ps[:, 0:AH, :].rearrange("p h (c t) -> p (h c) t", t=CH)
                out = ATT[:].rearrange("p h (c t) -> p (h c) t", t=CH)
                mask = (k.c("up", m * P, P) if m < LEVELS else k.ident).unsqueeze(1).broadcast_to([P, AH * NCH, CH])
                if m == 0:
                    tok = dve.go(v.tensor_tensor(out, scores, mask, ALU.mult))
                else:
                    dve.wait(tok)
                    tok = dve.go(v.copy_predicated(out, mask.bitcast(I32), scores))

        rounds(scores(), stream)
        k.phase_end()
        b4 = B[:].rearrange("p h (c t) -> p (h c) t", t=CH)
        e4 = E[:].rearrange("p h (c t) -> p (h c) t", t=CH)
        last = b4[:, :, CH - 1:CH].broadcast_to([P, AH * NCH, CH])
        t = dve.go(v.tensor_tensor(e4, last, b4, ALU.subtract))
        act.wait(t)
        t = act.go(nc.scalar.activation(E[:], E[:], ACT.Exp))
        dve.wait(t)
        t = step(v.tensor_tensor(E[:], E[:], K[:], ALU.mult))
        pe.wait(t)
        for h in range(AH):
            for c in range(NCH):
                a = slice(c * CH, (c + 1) * CH)
                mm = nc.tensor.transpose(k.ps[:, h, a], E[:, h, a], k.ident)
        t = pe.go(mm)
        act.wait(t)
        t_kt = act.go(nc.scalar.copy(KT[:], k.ps[:, 0:4, :]))
        t = act.go(nc.scalar.activation(B[:], B[:], ACT.Exp))
        dve.wait(t)
        t_q = dve.go(v.tensor_tensor(K[:], B[:], q, ALU.mult))
        pe.wait(t_kt)
        for c in range(NCH - 1):
            for h in range(AH):
                mm = nc.tensor.matmul(k.ps[:, 4 + c, h * P:(h + 1) * P], KT[:, h, c * CH:(c + 1) * CH],
                                      VA[:, c, h * P:(h + 1) * P], start=True, stop=True)
        t_kv = pe.go(mm)
        dve.wait(t_kv)
        pe.wait(t_q)
        t_o = None
        for c in range(NCH):
            for h in range(AH):
                o = k.ps[:, h, c * CH:(c + 1) * CH]
                mm = nc.tensor.matmul(o, VA[:, c, h * P:(h + 1) * P], ATT[:, h, c * CH:(c + 1) * CH], start=True, stop=(c == 0))
                if c > 0:
                    pe.wait(t_state)
                    mm = nc.tensor.matmul(o, S[:, c % 2, h, :], K[:, h, c * CH:(c + 1) * CH], start=False, stop=True)
            t_o = pe.go(mm)
            if c + 1 < NCH:
                if c == 0:
                    t_state = dve.go(v.tensor_copy(S[:, 1, :, :], k.ps[:, 4, :].rearrange("p (h d) -> p h d", h=AH)))
                else:
                    dve.wait(t_state, t_prev_o)
                    for h in range(AH):
                        end = B[:, h, (c + 1) * CH - 1:(c + 1) * CH]
                        t_state = dve.go(v.scalar_tensor_tensor(S[:, (c + 1) % 2, h, :], S[:, c % 2, h, :], end,
                                                                k.ps[:, 4 + c, h * P:(h + 1) * P], ALU.mult, ALU.add))
            t_prev_o = t_o
        act.wait(t_o)
        t = act.go(nc.scalar.copy(ATT[:], k.ps[:, 0:4, :]))
        t = act.go(nc.scalar.activation(E[:], k.ps[:, 0:4, :], ACT.Square))
        pe.wait(t)
        dve.wait(t)
        for h in range(AH):
            mm = nc.tensor.matmul(k.ps[:, 4 + h, :], k.ones, E[:, h, :], start=True, stop=True)
        t = pe.go(mm)
        t_n = rstd(k, B[:], k.ps[:, 4:8, :], 1.0 / CH, RMS_EPS, t)
        t_s = act.go(nc.scalar.activation(K[:], ag, ACT.Silu))
        step(v.scalar_tensor_tensor(flat(ATT[:]), flat(ATT[:]), k.p("norm_g"), flat(B[:]), ALU.mult, ALU.mult))
        dve.wait(t_s)
        dve.go(v.tensor_tensor(OA, ATT[:], K[:], ALU.mult))
        k.phase_end()


def flat(a):
    return a.rearrange("p a t -> p (a t)")


def attention(k, Z, VB, OB, COS, SIN, PT, ROT, tmp, st):
    nc, pe, dve, act = k.nc, k.pe, k.dve, k.act
    v = nc.vector
    tok = [None, None]
    for j in range(5):
        x = Z[:, 12 + j, :]
        if tok[j % 2]:
            pe.wait(tok[j % 2])
        t = pe.go(nc.tensor.matmul(k.ps[:, 4 + j % 2, :], k.c("rope_perm"), x, start=True, stop=True))
        yield
        dve.wait(t)
        tok[j % 2] = dve.go(v.tensor_tensor(ROT[:, j % 2, :], k.ps[:, 4 + j % 2, :], SIN[:], ALU.mult))
        t = dve.go(v.tensor_tensor(x, x, COS[:], ALU.mult))
        dve.wait(tok[j % 2], t)
        yield
        t_rope = dve.go(v.tensor_tensor(x, x, ROT[:, j % 2, :], ALU.add))
    pe.wait(t_rope)
    act.wait(t_rope)
    S = flat(tmp[:]).rearrange("p (g t) -> p g t", g=BH)

    yield from together(*(key_head(k, r, Z, VB, OB, S, PT, st) for r in range(2)))


def together(*streams):
    live = list(streams)
    while live:
        for s in list(live):
            if next(s, "end") == "end":
                live.remove(s)
        yield


def key_head(k, r, Z, VB, OB, S, PT, st):
    nc, pe, dve, act = k.nc, k.pe, k.dve, k.act
    v = nc.vector
    NB, HQ, bank = T // P, BH // 2, 4 + 2 * r
    rows = slice(64 * r, 64 * r + 64)
    heads = slice(HQ * r, HQ * r + HQ)
    S, PT = S[:, heads, :], PT[:, 2 * HQ * r:2 * HQ * (r + 1), :]
    sink = k.p("sinks")[:, heads]
    for b in range(NB):
        ks = 0 if b else P
        w = 256 - ks
        for g in range(HQ):
            mm = nc.tensor.matmul(k.ps[:, bank + g // 2, (g % 2) * 256 + ks:(g % 2 + 1) * 256],
                                  Z[rows, 12 + g, b * P:(b + 1) * P],
                                  Z[rows, 16, (b - 1) * P + ks:(b + 1) * P], start=True, stop=True)
        t_s = pe.go(mm)
        sc = k.ps[:, bank:bank + 2, :].rearrange("p j (r k) -> p (j r) k", r=2)[:, :, ks:256]
        s = S[:, :, ks:256]
        band = k.c("band")[:, ks:256].unsqueeze(1).broadcast_to([P, HQ, w])
        m, neg, den = (st[:, i, heads] for i in range(3))

        def step(ins):
            t = dve.go(ins)
            yield
            dve.wait(t)
            return t
        dve.wait(t_s)
        yield from step(v.scalar_tensor_tensor(s, sc, BD ** -0.5, band, ALU.mult, ALU.add))
        yield from step(v.tensor_reduce(m, s, AX.X, ALU.max))
        yield from step(v.tensor_tensor(m, m, sink, ALU.max))
        t_d = yield from step(v.tensor_tensor(neg, sink, m, ALU.subtract))
        t_m = yield from step(v.tensor_tensor(s, s, m.unsqueeze(2).broadcast_to([P, HQ, w]), ALU.subtract))
        act.wait(t_m)
        act.go(nc.scalar.activation(neg, neg, ACT.Exp))
        t_e = act.go(nc.scalar.activation(s, s, ACT.Exp))
        yield
        dve.wait(t_e)
        yield from step(v.tensor_reduce(den, s, AX.X, ALU.add))
        yield from step(v.tensor_tensor(den, den, neg, ALU.add))
        yield from step(v.reciprocal(den, den))
        t_p = yield from step(v.tensor_tensor(s, s, den.unsqueeze(2).broadcast_to([P, HQ, w]), ALU.mult))
        pe.wait(t_p)
        for g in range(HQ):
            for e in range(2 if b else 1):
                e = e if b else 1
                mm = nc.tensor.transpose(k.ps[:, bank + g // 2, ((g % 2) * 2 + e) * P:((g % 2) * 2 + e + 1) * P],
                                         S[:, g, e * P:(e + 1) * P], k.ident)
        t_t = pe.go(mm)
        yield
        act.wait(t_t)
        e0 = 0 if b else 1
        src = k.ps[:, bank:bank + 2, :].rearrange("p a (g e k) -> p (a g) e k", g=2, e=2)[:, :, e0:2, :]
        dst = PT.rearrange("p (g e) k -> p g e k", e=2)[:, :, e0:2, :]
        t_pt = act.go(nc.scalar.copy(dst, src))
        yield
        pe.wait(t_pt)
        for g in range(HQ):
            for e in range(e0, 2):
                mm = nc.tensor.matmul(k.ps[rows, bank, g * P:(g + 1) * P], VB[:, b - 1 + e, rows], PT[:, 2 * g + e, :],
                                      start=(e == e0), stop=(e == 1))
        t_o = pe.go(mm)
        yield
        act.wait(t_o)
        t_oc = act.go(nc.scalar.copy(OB[rows, :, b * P:(b + 1) * P], k.ps[rows, bank, :].rearrange("p (j t) -> p j t", j=4)))
        pe.wait(t_oc)
        yield


def pool_mixer(k, R):
    nc, pe, dve, act = k.nc, k.pe, k.dve, k.act
    v = nc.vector
    PAD = 16
    with ExitStack() as ctx:
        A = k.sb("pool_a", [P, 2, T + PAD], ctx)
        Bf = k.sb("pool_b", [P, 2, T + PAD], ctx)
        Y = k.sb("pooled", [P, DT, T], ctx)

        def step(ins):
            t = dve.go(ins)
            dve.wait(t)
            return t
        dve.go(v.memset(A[:, :, 0:PAD], 0.0))
        step(v.memset(Bf[:, :, 0:PAD], 0.0))
        t_y = []
        for g, w in enumerate(POOL_WINDOWS):
            h = k.H[:, 2 * g:2 * g + 2, 0:T]
            step(v.tensor_copy(A[:, :, PAD:], h))
            src, dst = A, Bf
            n = 1
            while n < w:
                step(v.tensor_tensor(dst[:, :, PAD:], src[:, :, PAD:], src[:, :, PAD - n:PAD - n + T], ALU.add))
                src, dst = dst, src
                n *= 2
            y = Y[:, 2 * g:2 * g + 2, :]
            cnt = k.c("pool_cnt", g * 16, 16).unsqueeze(1).broadcast_to([P, 2, 16])
            step(v.tensor_tensor(src[:, :, PAD:PAD + 16], src[:, :, PAD:PAD + 16], cnt, ALU.mult))
            step(v.tensor_scalar(src[:, :, PAD + 16:], src[:, :, PAD + 16:], 1.0 / w, None, ALU.mult))
            t_y.append(step(v.tensor_tensor(y, src[:, :, PAD:], h, ALU.subtract)))
        pg = k.sc[:, 5, :]
        step(v.tensor_tensor(pg, k.p("pool_scale"), k.MOD[1][:, 16:24, 0], ALU.mult))
        k.fetch(k.dram["pool_w"][0], DT, 2 * P)
        k.slab_wait()
        wv = k.slab_view(DT, 2 * P)
        slot = k.slab_next()
        for n in range(DT):
            g, a = n // 2, n % 2
            pe.wait(t_y[g])
            for kk in range(2):
                mm = nc.tensor.matmul(k.ps[:, n, :], wv[:, 2 * g + kk, a * P:(a + 1) * P], Y[:, 2 * g + kk, :],
                                      start=(kk == 0), stop=(kk == 1))
            t = pe.go(mm)
            dve.wait(t)
            if n == DT - 1:
                dve.eng.nop().then_inc(slot, 1)
            dve.go(v.scalar_tensor_tensor(R[:, n, :], k.ps[:, n, :], pg[:, n:n + 1], k.XA[:, n, :], ALU.mult, ALU.add))
        k.phase_end()


def pre_norm(k, ctx, layer, MOD, XC, all_tokens=True):
    nc, pe, dve, act = k.nc, k.pe, k.dve, k.act
    v = nc.vector
    sq = k.sb(f"sq{layer}", [P, DT, T], ctx)
    rs = k.sb(f"rs{layer}", [P, T], ctx)
    g = k.p("norm_pre", layer * 8, 8)
    for n, (X, t0, tn) in enumerate(((k.XA, TC, T), (XC, 0, TC))):
        sc = k.sc[:, 6 + n, :]
        t = dve.go(v.tensor_scalar(sc, MOD[:, 8:16, n], 1.0, None, ALU.add))
        dve.wait(t)
        dve.go(v.tensor_tensor(sc, sc, g, ALU.mult))
        if n:
            act.wait(t_mm)
        part = DT // 4
        for j in range(4):
            hs = slice(j * part, (j + 1) * part)
            t = act.go(nc.scalar.activation(sq[:, hs, 0:tn], X[:, hs, :], ACT.Square))
            pe.wait(t)
            for kk in range(j * part, (j + 1) * part):
                mm = nc.tensor.matmul(k.ps[:, n, 0:tn], k.ones, sq[:, kk, 0:tn], start=(kk == 0), stop=(kk == DT - 1))
        t_mm = pe.go(mm)
        if n:
            dve.wait(t_h)
        rstd(k, rs[:, 0:tn], k.ps[:, n, 0:tn], 1.0 / D, EPS, t_mm)
        H = k.H[:, :, t0:t0 + tn]
        for kk in range(DT):
            if kk % part == 0:
                hs = slice(kk, kk + part)
                t_h = dve.go(v.tensor_tensor(H[:, hs, :], X[:, hs, :], rs[:, 0:tn].unsqueeze(1).broadcast_to([P, part, tn]), ALU.mult))
                act.wait(t_h)
            affine(act, H[:, kk, :], H[:, kk, :], sc[:, kk:kk + 1], MOD[:, kk, n:n + 1])
    k.phase_end()


def post_norm(k, ctx, name, layer, MOD, OUT, X, n, t0, tn):
    nc, pe, dve, act = k.nc, k.pe, k.dve, k.act
    v = nc.vector
    sq = k.sb("psq" + name, [P, DT, T], ctx)
    rs = k.sb("prs" + name, [P, T], ctx)
    gg = k.sc[:, 5, :]
    dve.go(v.tensor_tensor(gg, MOD[:, 16:24, n], k.p("norm_post", layer * 8, 8), ALU.mult))
    O = OUT[:, :, t0:t0 + tn]
    for kk in range(DT):
        if kk % 2 == 0:
            t = act.go(nc.scalar.activation(sq[:, kk:kk + 2, 0:tn], O[:, kk:kk + 2, :], ACT.Square))
            pe.wait(t)
        mm = nc.tensor.matmul(k.ps[:, 0, 0:tn], k.ones, sq[:, kk, 0:tn], start=(kk == 0), stop=(kk == DT - 1))
    t = pe.go(mm)
    rstd(k, rs[:, 0:tn], k.ps[:, 0, 0:tn], 1.0 / D, EPS, t)
    pool = k.pool
    pool.wait((act.sem, act.n))
    for kk in (3, 7):
        t_p = pool.go(nc.gpsimd.tensor_tensor(O[:, kk, :], O[:, kk, :], rs[:, 0:tn], ALU.mult))
    for j in range(2):
        t = dve.go(v.tensor_tensor(O[:, 4 * j:4 * j + 3, :], O[:, 4 * j:4 * j + 3, :],
                                   rs[:, 0:tn].unsqueeze(1).broadcast_to([P, 3, tn]), ALU.mult))
    dve.wait(t, t_p)
    for kk in range(DT):
        dve.go(v.scalar_tensor_tensor(X[:, kk, :], O[:, kk, :], gg[:, kk:kk + 1], X[:, kk, :], ALU.mult, ALU.add))
    k.phase_end()


def mix(k, step, out, pc, pl, s):
    v = k.nc.vector
    oc, ol = out[:, 0:TC], out[:, TC:TA]
    g = lambda a: a.rearrange("p (r w) -> p r w", w=GRID_W)
    step(v.tensor_scalar(oc, pc, s[:, 0:1], None, ALU.mult))
    step(v.tensor_scalar(ol, pl, s[:, 0:1], None, ALU.mult))

    def add(o, i, j):
        return v.scalar_tensor_tensor(o, i, s[:, j:j + 1], o, ALU.mult, ALU.add)
    step(add(oc[:, 1:TC], pc[:, 0:TC - 1], 5))
    step(add(g(ol)[:, :, 1:], g(pl)[:, :, :-1], 1))
    step(add(oc[:, 0:TC - 1], pc[:, 1:TC], 6))
    step(add(g(ol)[:, :, :-1], g(pl)[:, :, 1:], 2))
    step(add(ol[:, GRID_W:], pl[:, :-GRID_W], 3))
    return step(add(ol[:, :-GRID_W], pl[:, GRID_W:], 4))


def flat_ps(k, bank, n):
    return k.ps[:, bank:bank + 2, :].rearrange("p a b -> p (a b)")[:, 0:n]


def tile_products(k, wv, a, bank):
    for b, (t0, tn) in enumerate(((0, TC), (TC, T))):
        for kk in range(DT):
            mm = k.nc.tensor.matmul(k.ps[:, bank + b, 0:tn], wv[:, kk, a * P:(a + 1) * P],
                                    k.H[:, kk, t0:t0 + tn], start=(kk == 0), stop=(kk == DT - 1))
    return k.pe.go(mm)


def slab_tiles(k, w, idx, banks, waits, i=0, per=0, order=(0, 1)):
    k.fetch(w[idx], DT, 2 * P, i, per)
    k.slab_wait(i, per)
    wv = k.slab_view(DT, 2 * P)
    slot = k.slab_next()
    out = [None, None]
    for a in order:
        k.pe.wait(*waits[a])
        out[a] = tile_products(k, wv, a, banks[a])
    return out, slot


def even_mixer2(k, ctx, OUT):
    nc, pe, dve, act, pool = k.nc, k.pe, k.dve, k.act, k.pool
    v = nc.vector
    w = k.dram["ev_in"]
    with ExitStack() as ctx:
        O = k.sb("O", [P, DT, TA], ctx)
        with ExitStack() as c2:
            WL = k.sb("WL", [P, TA], c2)
            AL = k.sb("AL", [P, TA], c2)
            MUX = k.sb("MUX", [P, 20, 7], c2)
            with ExitStack() as c3:
                FOUR = k.sb("FOUR", [P, 2, TA], c3)
                GF = k.sb("GF", [P, 2, TA], c3)

                def step(ins):
                    t = dve.go(ins)
                    dve.wait(t)
                    return t
                mu = k.p("mu")
                step(v.tensor_scalar(MUX[:, :, 0], mu, -1.0, 1.0, ALU.mult, ALU.add))
                for j in range(6):
                    m = k.c("type4", j, 1) if j < 4 else k.c("type2", j - 4, 1)
                    step(v.tensor_scalar(MUX[:, :, 1 + j], mu, m, None, ALU.mult))
                (ta, tb), slot = slab_tiles(k, w, 0, (0, 2), ((), ()))
                dve.wait(ta)
                mix(k, step, WL, k.ps[:, 0, 0:TC], k.ps[:, 1, :], MUX[:, 18, :])
                dve.wait(tb)
                dve.eng.nop().then_inc(slot, 1)
                t_al = mix(k, step, AL, k.ps[:, 2, 0:TC], k.ps[:, 3, :], MUX[:, 19, :])
                act.wait(t_al)
                act.go(nc.scalar.activation(WL[:], WL[:], ACT.Tanh))
                (ta, tb), slot = slab_tiles(k, w, 1, (4, 6), ((), ()))
                act.wait(ta)
                for a, t in ((0, ta), (1, tb)):
                    act.wait(t)
                    act.go(nc.scalar.copy(FOUR[:, a, 0:TC], k.ps[:, 4 + 2 * a, 0:TC]))
                    act.go(nc.scalar.copy(FOUR[:, a, TC:TA], k.ps[:, 5 + 2 * a, :]))
                act.eng.nop().then_inc(slot, 1)
                (ta, tb), slot = slab_tiles(k, w, 2, (0, 2), ((t_al,), ()))
                for a, t in ((0, ta), (1, tb)):
                    act.wait(t)
                    act.go(nc.scalar.activation(GF[:, a, 0:TC], k.ps[:, 2 * a, 0:TC], ACT.Silu))
                    act.go(nc.scalar.activation(GF[:, a, TC:TA], k.ps[:, 1 + 2 * a, :], ACT.Silu))
                act.eng.nop().then_inc(slot, 1)
                k.phase_end()
                fourier(k, FOUR, GF, O)
            rwkv(k, c2, WL, AL, MUX, O)
        dense_fm(k, "ev_out", 4, O, [(0, TC), (TC, T)], lambda n, banks: two_copies(k, OUT, n, banks))


def two_copies(k, OUT, n, banks):
    v = k.nc.vector
    o = tile_of(OUT, n)
    v.tensor_copy(o[:, 0:TC], banks[0])
    return v.tensor_copy(o[:, TC:TA], banks[1])


def fourier(k, FOUR, GF, O):
    nc, pe, dve, act = k.nc, k.pe, k.dve, k.act
    v = nc.vector
    with ExitStack() as ctx:
        dft = k.sb("dft_sb", [P, F_N], ctx)
        t_ld = k.load(dft[:], k.dram["dft"])
        k.loaded(pe, t_ld)
        f = lambda name: dft[:, F_AT[name][0]:F_AT[name][0] + F_AT[name][1]]
        PQ = k.sb("PQ", [P, TA // P, 2, 2 * P], ctx)
        for t in range(TA // P):
            for a in range(2):
                mm = nc.tensor.matmul(k.ps[:, t, a * 256:(a + 1) * 256], FOUR[:, a, t * P:(t + 1) * P], f("f64"),
                                      start=True, stop=True)
            tok = pe.go(mm)
            act.wait(tok)
            t_pq = act.go(nc.scalar.copy(PQ[:, t, :, :], k.ps[:, t, :].rearrange("p (a n) -> p a n", a=2)))
        pe.wait(t_pq)
        for a in range(2):
            for b, (c, s, t0, tn, u0) in enumerate((("c256", "s256", 0, TC, 0), ("c512", "s512", TC, T, 2))):
                n = tn // P
                out = k.ps[:, 2 * a + b, 0:tn]
                cw = f(c).rearrange("p (u t) -> p u t", u=n)
                sw = f(s).rearrange("p (u t) -> p u t", u=n)
                for u in range(n):
                    nc.tensor.matmul(out, PQ[:, u0 + u, a, 0:P], cw[:, u, :], start=(u == 0), stop=False)
                    mm = nc.tensor.matmul(out, PQ[:, u0 + u, a, P:2 * P], sw[:, u, :], start=False, stop=(u == n - 1))
                tok = pe.go(mm)
                dve.wait(tok)
                dve.go(v.tensor_tensor(O[:, RT + a, t0:t0 + tn], out, GF[:, a, t0:t0 + tn], ALU.mult))
        k.n_loads = 0
        k.phase_end()


def rounds(*streams):
    for _ in together(*streams):
        pass


def rwkv(k, ctx, WL, AL, MUX, O):
    nc, pe, dve, act, pool = k.nc, k.pe, k.dve, k.act, k.pool
    v = nc.vector
    w = k.dram["ev_in"]
    NC = TA // CH
    ws = k.sb("w2a2_sb", [P, 2, P], ctx)
    MS = k.sb("mix_scal", [P, 3, 7], ctx)
    RW = k.sb("rw_scal", [P, 10], ctx)
    SRC = k.sb("rkv", [P, 3, TA], ctx)
    GR = k.sb("gate_r", [P, TA], ctx)
    KK = k.sb("KK", [P, TA], ctx)
    KS = k.sb("KS", [P, TA], ctx)
    VP = k.sb("VP", [P, NC, 2, P], ctx)
    r, k0, val = SRC[:, 0, :], SRC[:, 1, :], SRC[:, 2, :]
    ch = lambda a: a.rearrange("p (c t) -> p c t", t=CH)
    xa = k.XA[:].rearrange("p a t -> p (a t)")
    slot_end = DT * 2 * P
    u4 = lambda a: a.rearrange("p (u t) -> p u t", u=4)

    class Direction:
        def __init__(b, d):
            if d == 0:
                b.LW, b.F, b.X1, b.X2, b.A = (k.sb(n, [P, TA], ctx)[:] for n in ("LW", "F", "X1", "X2", "A"))
                b.BB, b.KB = (k.sb(n, [P, 4, 192], ctx)[:] for n in ("BB", "KB"))
            else:
                b.LW, b.F, b.X1, b.X2, b.A = (xa[:, j * TA:(j + 1) * TA] for j in range(5))
                b.BB, b.KB = (u4(k.ring[:, j, slot_end:slot_end + 768]) for j in range(2))
            b.G = k.sb(f"G_{d}", [P, 4, NC], ctx)
            b.AR = k.sb(f"AR{d}", [P, NC, 320], ctx)
            b.AMV, b.NLT, b.X, b.Y, b.T1 = (k.sb(f"{n}_{d}", [P, 4, P], ctx) for n in ("AMV", "NLT", "X", "Y", "T1"))
            b.QG = k.sb(f"QG{d}", [P, 2, 2, 192], ctx)
            b.EV = k.sb(f"EV{d}", [P, 2, NC], ctx)
            b.TI = k.sb(f"TI{d}", [P, 2, 2, 64], ctx)
            b.bank = 4 * d
            dve.go(v.memset(b.EV[:], 1.0))
            for j in range(2):
                for h in range(2):
                    dve.go(v.tensor_copy(b.TI[64:128, j, h, :], k.c("ident64")[64:128, :]))

    dirs = [Direction(0), Direction(1)]
    dve.go(v.memset(VP[:], 0.0))
    k.phase_end()
    with nc.Fori(0, RT) as p:
        def step(ins):
            t = dve.go(ins)
            dve.wait(t)
            return t

        def stage(ins):
            t = dve.go(ins)
            yield
            dve.wait(t)
            return t
        D0 = dirs[0]
        dve.go(v.tensor_copy(MS[:].unsqueeze(2), MUX[:, 0:18, :].rearrange("p (a q) s -> p a q s", q=RT)[:, :, bass.ds(p, 1), :]))
        t_ws = k.load(ws[:].rearrange("p a n -> p (a n)"), k.dram["w2a2"][p])
        step(v.tensor_copy(RW[:, 0:9], k.p("rw")[:, bass.ds(p * 9, 9)]))
        t_rw = step(v.tensor_scalar(RW[:, 9:10], RW[:, 5:6], -1.0, 1.0, ALU.mult, ALU.add))
        rw = lambda j: RW[:, j:j + 1]
        shared = {}

        def decays(d):
            b = dirs[d]
            LW, F, X1, X2, A, G = b.LW, b.F, b.X1, b.X2, b.A, b.G
            act.wait(b.t_w)
            t_lw = act.go(nc.scalar.activation(LW, flat_ps(k, b.bank, TA), ACT.Sigmoid, bias=rw(d)))
            act.wait(b.t_a)
            b.t_av = act.go(nc.scalar.activation(A, flat_ps(k, b.bank + 2, TA), ACT.Sigmoid, bias=rw(2 + d)))
            yield
            dve.wait(t_lw)
            yield from stage(v.tensor_scalar(LW, LW, -math.exp(-0.5), None, ALU.mult))
            yield from stage(v.tensor_tensor_scan(F, k.c("scan_reset"), LW, 0.0, ALU.mult, ALU.add))
            fmid = ch(F)[:, :, 63:64]
            fend = ch(F)[:, :, CH - 1:CH]
            fm = fmid.broadcast_to([P, NC, CH])
            if d == 0:
                yield from stage(v.tensor_tensor(ch(X2), ch(F), fm, ALU.subtract))
                dve.go(v.tensor_tensor(X1, X2, LW, ALU.subtract))
            else:
                yield from stage(v.tensor_tensor(ch(X1), fm, ch(F), ALU.subtract))
                dve.go(v.tensor_tensor(X2, X1, LW, ALU.add))
            t_g = dve.go(v.tensor_tensor(G[:, 0, :].unsqueeze(2), fend, fmid, ALU.subtract))
            yield
            act.wait(t_g)
            act.go(nc.scalar.activation(G[:, 1, :].unsqueeze(2), fmid, ACT.Exp))
            b.t_g = act.go(nc.scalar.activation(G[:, 2, :], G[:, 0, :], ACT.Exp))
            act.go(nc.scalar.activation(LW, X2, ACT.Exp, scale=-1.0))
            act.go(nc.scalar.activation(X1, X1, ACT.Exp))
            b.t_x = act.go(nc.scalar.activation(X2, X2, ACT.Exp))
            yield
            dve.wait(b.t_av, b.t_g)
            b.t_kf = dve.go(v.tensor_scalar(F, A, rw(5), rw(9), ALU.mult, ALU.add))
            g_mid, b.g_end = (G[:, 1, :], G[:, 2, :])[::-1 if d else 1]
            dve.go(v.tensor_copy(b.EV[0:64, 0, :], g_mid[0:64, :]))
            t = dve.go(v.tensor_copy(b.EV[0:64, 1, :], g_mid[64:128, :]))
            dve.wait(t)
            b.t_kf = dve.go(v.tensor_scalar(A, A, -1.0, None, ALU.mult))
            yield

        pe.wait(t_ws)
        act.wait(t_rw)
        for d, b in enumerate(dirs):
            rows = slice(64 * d, 64 * d + 64)
            two_mm(k, b.bank, ws[rows, 0, :], WL[rows, :])
            b.t_w = pe.go(k.last_mm)
            two_mm(k, b.bank + 2, ws[rows, 1, :], AL[rows, :])
            b.t_a = pe.go(k.last_mm)
        early = [decays(0), decays(1)]
        for g in early:
            next(g)
        D1 = dirs[1]
        (tr, tk), slot = slab_tiles(k, w, 3 + p * 2, (0, 2), ((D0.t_av,), (D0.t_av,)), p, 1, order=(1, 0))
        rounds(*early)
        dve.wait(tk)
        t_k0 = mix(k, step, k0, k.ps[:, 2, 0:TC], k.ps[:, 3, :], MS[:, 1, :])
        t = step(v.tensor_scalar(KK[:], k0, rw(4), None, ALU.mult))
        act.wait(t)
        t_sq = act.go(nc.scalar.activation(KS[:], KK[:], ACT.Square))
        pe.wait(t_sq, t_k0)
        two_mm(k, 2, k.c("blk64"), KS)
        t_n = pe.go(k.last_mm)
        dve.wait(tr)
        dve.eng.nop().then_inc(slot, 1)
        t_r = mix(k, step, r, k.ps[:, 0, 0:TC], k.ps[:, 1, :], MS[:, 0, :])
        k.fetch(w[4 + p * 2], DT, 2 * P, p, 1)
        k.slab_wait(p, 1)
        wv = k.slab_view(DT, 2 * P)
        v_slot = k.slab_next()
        pe.wait(D1.t_av)
        tv = tile_products(k, wv, 0, 4)
        dve.wait(t_n)
        t = step(v.tensor_scalar(KS[:], flat_ps(k, 2, TA), 1e-24, None, ALU.max))
        act.wait(t)
        act.wait(act.go(nc.scalar.activation(KS[:], KS[:], ACT.Sqrt)))
        act.wait(act.go(nc.scalar.activation(KS[:], KS[:], ACT.Ln)))
        t_in = act.go(nc.scalar.activation(KS[:], KS[:], ACT.Exp, scale=-1.0))
        dve.wait(t_in)
        t_kk = step(v.tensor_tensor(KK[:], KK[:], KS[:], ALU.mult))

        def prepare(d):
            b = dirs[d]
            LW, F, X1, X2, A, AR = b.LW, b.F, b.X1, b.X2, b.A, b.AR
            q = dve
            mul = lambda out, x, y: q.go(q.eng.tensor_tensor(out, x, y, ALU.mult))
            q.wait(b.t_kf, b.t_x, t_kk, t_r)
            t_k = mul(F, F, k0)
            t_a = mul(A, A, KK[:])
            yield
            if d == 0:
                act.wait(t_k, t_kk)
                t_ks = shared["ks"] = act.go(nc.scalar.copy(KS[:], F))
            else:
                q.wait(t_k, shared["ks"])
                t_ks = shared["ks"] = q.go(q.eng.tensor_tensor(KS[:], KS[:], F, ALU.add))
            q.wait(t_a)
            t_a = mul(A, A, LW)
            yield
            mul(AR[:, :, 0:CH], ch(KK[:]), ch(X1))
            yield
            mul(AR[:, :, CH:2 * CH], ch(r), ch(X2))
            yield
            q.wait(t_ks, t_a)
            t_k = mul(F, F, LW)
            b.t_ar = mul(AR[:, :, 2 * CH:320], k.c("ident64").unsqueeze(1).broadcast_to([P, NC, 64]),
                         b.g_end.unsqueeze(2).broadcast_to([P, NC, 64]))
            yield
            q.wait(b.t_ar)
            hb = b.g_end.unsqueeze(2).broadcast_to([P, NC, CH])
            mul(ch(X1), ch(A), hb)
            yield
            b.t_hat = mul(ch(X2), ch(F), hb)
            b.read = b.t_ar
            yield

        def values_by_token():
            dve.wait(tv)
            t_v = mix(k, step, val, k.ps[:, 4, 0:TC], k.ps[:, 5, :], MS[:, 2, :])
            pe.wait(t_v)
            for c in range(NC):
                mm = nc.tensor.transpose(k.ps[:, 4 + c // 4, (c % 4) * P:(c % 4 + 1) * P], val[:, c * P:(c + 1) * P], k.ident)
            t = pe.go(mm)
            act.wait(t)
            return act.go(nc.scalar.copy(VP[:, :, :, 64:128],
                                         flat_ps(k, 4, TA).rearrange("p (c h i) -> p c h i", c=NC, h=2)))

        def bonus():
            dve.wait(shared["ks"])
            shared["rk"] = yield from stage(v.scalar_tensor_tensor(KS[:], r, rw(6), KS[:], ALU.mult, ALU.mult))
            pe.wait(shared["rk"], t_vp)
            two_mm(k, 4, k.c("blk64"), KS)
            t = pe.go(k.last_mm)
            yield
            dve.wait(t)
            shared["bonus"] = D1.read = dve.go(v.tensor_tensor(KS[:], flat_ps(k, 4, TA), val, ALU.mult))
            yield

        def batches(d):
            b = dirs[d]
            b.at, b.t_state = 0, dve.go(v.memset(b.TI[0:64, 0, :, :], 0.0))
            BP, KP, BX, KX, AR = b.A, b.F, b.X1, b.X2, b.AR
            BB, KB, AMV, NLT, X, Y, T1, QG = b.BB, b.KB, b.AMV, b.NLT, b.X, b.Y, b.T1, b.QG
            MT = T1
            lo, up = (k.c("low"), k.c("up")) if d == 0 else (k.c("up"), k.c("low"))
            s_up = k.c("strict_up") if d == 0 else k.c("strict_low")
            i_up = k.c("incl_up") if d == 0 else k.c("incl_low")
            b4 = lambda m: m.unsqueeze(1).broadcast_to([P, 4, P])
            bank = lambda j, n=512: k.ps[:, b.bank + j, 0:n]
            hjn = lambda j: k.ps[:, b.bank + j:b.bank + j + 2, :].rearrange("p h (j n) -> p (h j) n", j=2)
            hd = lambda j: k.ps[:, b.bank + j:b.bank + j + 2, 0:256].rearrange("p h (j n) -> p h j n", j=2)
            hj = lambda a: a.rearrange("p (h j) i -> p h j i", h=2)
            for q in ((0, 1, 2), (0, 2, 1))[d]:
                cs = (2 * q, 2 * q + 1)
                pe.wait(b.t_ar, b.read)
                for h in range(2):
                    hr = slice(64 * h, 64 * h + 64)
                    for j, c in enumerate(cs):
                        a = slice(c * CH, (c + 1) * CH)
                        nc.tensor.matmul(k.ps[:, b.bank + h, j * 256:(j + 1) * 256], BP[hr, a], AR[hr, c, 0:256], start=True, stop=True)
                        mm = nc.tensor.matmul(k.ps[:, b.bank + 2 + h, j * P:(j + 1) * P], AR[hr, c, 0:CH], BP[hr, a], start=True, stop=True)
                t_sc = pe.go(mm)
                act.wait(b.t_ar, b.read)
                act.go(nc.scalar.copy(X[:], b4(k.ident)))
                t_i = act.go(nc.scalar.copy(Y[:], b4(k.ident)))
                yield
                dve.wait(t_sc, t_i)
                t_nl = dve.go(v.tensor_tensor(NLT[:], hjn(0)[:, :, 0:CH], b4(s_up), ALU.mult))
                dve.go(v.tensor_tensor(BB[:, :, 0:CH], hjn(0)[:, :, CH:256], b4(i_up), ALU.mult))
                dve.go(v.copy_predicated(Y[:], b4(up[:, 0:P]).bitcast(I32), hjn(0)[:, :, 0:CH]))
                t_x0 = dve.go(v.copy_predicated(hj(X[:]), lo[:, 0:P].unsqueeze(1).unsqueeze(1).broadcast_to([P, 2, 2, P]).bitcast(I32), hd(2)))
                yield
                pe.wait(t_x0, b.t_hat)
                for h in range(2):
                    hr = slice(64 * h, 64 * h + 64)
                    for j, c in enumerate(cs):
                        a = slice(c * CH, (c + 1) * CH)
                        mm = nc.tensor.matmul(k.ps[:, b.bank + h, j * 256:(j + 1) * 256], KP[hr, a], AR[hr, c, 0:256], start=True, stop=True)
                t_sc = pe.go(mm)
                for j, c in enumerate(cs):
                    a = slice(c * CH, (c + 1) * CH)
                    nc.tensor.transpose(k.ps[:, b.bank + 2, j * P:(j + 1) * P], AR[:, c, 0:CH], k.ident)
                    nc.tensor.transpose(k.ps[:, b.bank + 2, (2 + j) * P:(3 + j) * P], BX[:, a], k.ident)
                    mm = nc.tensor.transpose(k.ps[:, b.bank + 3, j * P:(j + 1) * P], KX[:, a], k.ident)
                t_tr = pe.go(mm)
                yield
                dve.wait(t_sc)
                t_mt = dve.go(v.tensor_tensor(MT[:], hjn(0)[:, :, 0:CH], b4(s_up), ALU.mult))
                t_kb = dve.go(v.tensor_tensor(KB[:, :, 0:CH], hjn(0)[:, :, CH:256], b4(i_up), ALU.mult))
                act.wait(t_tr)
                tm = lambda j, o: k.ps[:, b.bank + j, o:o + 2 * P].rearrange("p (j h i) -> p h j i", j=2, h=2)
                t_k = act.go(nc.scalar.copy(hj(KB[:, :, CH:192]), tm(3, 0)))
                act.go(nc.scalar.copy(hj(AMV[:, :, 0:64]), tm(2, 0)))
                t_tm = act.go(nc.scalar.copy(hj(BB[:, :, CH:192]), tm(2, 2 * P)))
                yield
                pe.wait(t_mt, t_k)
                for u in range(4):
                    mm = nc.tensor.matmul(bank(3)[:, u * P:(u + 1) * P], MT[:, u, :], VP[:, cs[u % 2], u // 2, :], start=True, stop=True)
                t_mv = pe.go(mm)
                t_y = t_kb
                t_x = t_x0
                for m in range(1, LEVELS):
                    pe.wait(t_x, t_kb)
                    for u in range(4):
                        mm = nc.tensor.matmul(bank(0)[:, u * P:(u + 1) * P], NLT[:, u, :], X[:, u, :], start=True, stop=True)
                    t = pe.go(mm)
                    yield
                    act.wait(t)
                    t_t1 = act.go(nc.scalar.copy(T1[:], u4(bank(0))))
                    if m == 1:
                        act.wait(t_mv)
                        t_amv = act.go(nc.scalar.copy(AMV[:, :, 64:128], u4(bank(3))[:, :, 64:128]))
                    yield
                    pe.wait(t_t1, t_y, t_tm)
                    if m < LEVELS - 1:
                        for u in range(4):
                            mm = nc.tensor.matmul(bank(1)[:, u * P:(u + 1) * P], Y[:, u, :], T1[:, u, :], start=True, stop=True)
                        t_xm = pe.go(mm)
                    for u in range(4):
                        mm = nc.tensor.matmul(bank(2)[:, u * P:(u + 1) * P], T1[:, u, :], Y[:, u, :], start=True, stop=True)
                    t_ym = pe.go(mm)
                    yield
                    if m < LEVELS - 1:
                        dve.wait(t_xm)
                        t_x = dve.go(v.copy_predicated(X[:], b4(lo[:, m * P:(m + 1) * P]).bitcast(I32), u4(bank(1))))
                    dve.wait(t_ym)
                    t_y = dve.go(v.copy_predicated(Y[:], b4(up[:, m * P:(m + 1) * P]).bitcast(I32), u4(bank(2))))
                    yield
                pe.wait(t_y, t_amv)
                for u in range(4):
                    mm = nc.tensor.matmul(bank(3)[:, u * P:(u + 1) * P], Y[:, u, :], AMV[:, u, :], start=True, stop=True)
                t = pe.go(mm)
                yield
                act.wait(t)
                t_wu = act.go(nc.scalar.copy(T1[:], u4(bank(3))))
                yield
                pe.wait(t_wu)
                for u in range(4):
                    h, c = u // 2, cs[u % 2]
                    hr = slice(64 * h, 64 * h + 64)
                    o = k.ps[:, b.bank + h, (u % 2) * 192:(u % 2 + 1) * 192]
                    nc.tensor.matmul(o, T1[:, u, :], BB[:, u, :], start=True, stop=False)
                    nc.tensor.matmul(o, VP[:, c, h, :], KB[:, u, :], start=False, stop=False)
                    mm = nc.tensor.matmul(o, k.c("top_ident")[hr, :], AR[hr, c, CH:320], start=False, stop=True)
                t_qg = pe.go(mm)
                yield
                act.wait(t_qg)
                for u in range(4):
                    h, c = u // 2, cs[u % 2]
                    b.read = act.go(nc.scalar.mul(QG[:, u % 2, h, :], k.ps[:, b.bank + h, (u % 2) * 192:(u % 2 + 1) * 192], b.EV[:, h, c:c + 1]))
                yield
                yield from walk(b, d, q)

        def walk(b, d, q):
            QG, TI = b.QG, b.TI
            pe.wait(b.read)
            for j in ((0, 1), (1, 0))[d]:
                pe.wait(b.t_state)
                cur, nxt = TI[:, b.at % 2, :, :], TI[:, (b.at + 1) % 2, :, :]
                st = k.ps[0:64, b.bank + 2, 0:P]
                for h in range(2):
                    mm = nc.tensor.matmul(st[:, h * 64:(h + 1) * 64], QG[:, j, h, CH:192], cur[:, h, :], start=True, stop=True)
                t = pe.go(mm)
                for h in range(2):
                    mm = nc.tensor.matmul(k.ps[64 * h:64 * h + 64, b.bank + 3, j * P:(j + 1) * P], cur[:, h, :],
                                          QG[:, j, h, 0:CH], start=True, stop=True)
                t_out = pe.go(mm)
                yield
                dve.wait(t)
                b.t_state = dve.go(v.tensor_copy(nxt[0:64, :, :], st.rearrange("p (h i) -> p h i", h=2)))
                b.at += 1
                yield
            dve.wait(t_out)
            o, out = tile_of(O, p)[:, q * 256:(q + 1) * 256], k.ps[:, b.bank + 3, 0:256]
            if q in shared:
                dve.wait(shared[q])
                b.read = dve.go(v.tensor_tensor(o, o, out, ALU.add))
            else:
                b.read = dve.go(v.tensor_copy(o, out))
            shared[q] = b.read
            yield

        def stream(d):
            yield from prepare(d)
            if d:
                yield from bonus()
            yield from batches(d)
        first = stream(0)
        for n in range(7 + LEAD):
            if n == 7:
                t_vp = values_by_token()
            next(first)
        rounds(first, stream(1))
        pe.wait(D1.read)
        tg = tile_products(k, wv, 1, 6)
        F, X1, X2 = D0.LW, D0.X1, D0.X2
        dve.wait(shared["bonus"], *(shared[q] for q in range(NC // 2)))
        t = step(v.tensor_tensor(F, tile_of(O, p), KS[:], ALU.add))
        pe.wait(t)
        two_mm(k, 2, k.c("blk64"), F)
        t = pe.go(k.last_mm)
        dve.wait(t)
        t = step(v.scalar_tensor_tensor(F, flat_ps(k, 2, TA), -1.0 / 64, F, ALU.mult, ALU.add))
        act.wait(t)
        t = act.go(nc.scalar.activation(X1, F, ACT.Square))
        pe.wait(t)
        two_mm(k, 4, k.c("blk64"), X1)
        t = pe.go(k.last_mm)
        act.wait(tg)
        act.eng.nop().then_inc(v_slot, 1)
        act.go(nc.scalar.activation(GR[:, 0:TC], k.ps[:, 6, 0:TC], ACT.Silu))
        t_gr = act.go(nc.scalar.activation(GR[:, TC:TA], k.ps[:, 7, :], ACT.Silu))
        rstd(k, X2, flat_ps(k, 4, TA), 1.0 / 64, GN_EPS, t)
        step(v.tensor_tensor(F, F, X2, ALU.mult))
        step(v.tensor_scalar(F, F, rw(7), rw(8), ALU.mult, ALU.add))
        dve.wait(t_gr)
        dve.go(v.tensor_tensor(tile_of(O, p), F, GR[:], ALU.mult))
        k.n_loads = 0
        k.phase_end()
    k.slab_loop(RT)


def two_mm(k, bank, lhsT, rhs):
    for n, (t0, tn) in enumerate(((0, T), (T, TC))):
        k.last_mm = k.nc.tensor.matmul(k.ps[:, bank + n, 0:tn], lhsT, rhs[:, t0:t0 + tn], start=True, stop=True)


def log_sigmoid(k, ctx, out, x):
    nc, dve, act = k.nc, k.dve, k.act
    v = nc.vector
    n = x.shape[1]
    b = k.sb("ls_tmp", [P, 4, n], ctx)
    y, z, z2, acc = (b[:, j, :] for j in range(4))

    def step(ins):
        t = dve.go(ins)
        dve.wait(t)
        return t
    step(v.tensor_scalar(z, x, -1.0, None, ALU.mult))
    t = step(v.tensor_tensor(z, z, x, ALU.max))
    act.wait(t)
    t = act.go(nc.scalar.activation(y, z, ACT.Exp, scale=-1.0))
    dve.wait(t)
    step(v.tensor_scalar(z, y, 2.0, None, ALU.add))
    step(v.reciprocal(z, z))
    step(v.tensor_tensor(z, z, y, ALU.mult))
    step(v.tensor_tensor(z2, z, z, ALU.mult))
    step(v.tensor_scalar(acc, z2, 1.0 / 17, 1.0 / 15, ALU.mult, ALU.add))
    for c in (13, 11, 9, 7, 5, 3, 1):
        step(v.tensor_tensor(acc, acc, z2, ALU.mult))
        step(v.tensor_scalar(acc, acc, 1.0 / c, None, ALU.add))
    step(v.tensor_tensor(acc, acc, z, ALU.mult))
    step(v.tensor_scalar(z, x, 0.0, None, ALU.min))
    return step(v.scalar_tensor_tensor(out, acc, -2.0, z, ALU.mult, ALU.add))


def rope_loop(k, ctx, X, t0, cos, sin, what):
    nc, pe, dve = k.nc, k.pe, k.dve
    v = nc.vector
    ROT = k.sb("ROT" + what, [P, 4, T], ctx)
    with nc.Fori(0, RH // 4) as i:
        for j in range(4):
            x = tile_of(X, i * 4 + j)[:, t0:t0 + T]
            t = pe.go(nc.tensor.matmul(k.ps[:, j, :], k.c("swap64"), x, start=True, stop=True))
            dve.wait(t)
            ta = dve.go(v.tensor_tensor(ROT[:, j, :], k.ps[:, j, :], sin, ALU.mult))
            tb = dve.go(v.tensor_tensor(x, x, cos, ALU.mult))
            dve.wait(ta, tb)
            dve.go(v.tensor_tensor(x, x, ROT[:, j, :], ALU.add))
        k.phase_end()


def odd_mixer2(k, OUT):
    nc, pe, dve, act = k.nc, k.pe, k.dve, k.act
    v = nc.vector
    NC, NL = TA // CH, T // CH
    with ExitStack() as ctx:
        Q = k.sb("Q", [P, RH, T], ctx)
        K = k.sb("Kr", [P, RH, TA], ctx)
        V = k.sb("V", [P, NC, D], ctx)
        G = k.sb("Gr", [P, RH, T], ctx)
        lat = [(TC, T)]
        dense_fm(k, "od_in", 4, k.H, lat, lambda n, b: v.tensor_copy(tile_of(Q, n), b[0]))

        def scaled(n, banks):
            o = tile_of(K, n)
            v.tensor_scalar(o[:, 0:TC], banks[0], P ** -0.5, None, ALU.mult)
            return v.tensor_scalar(o[:, TC:TA], banks[1], P ** -0.5, None, ALU.mult)
        dense_fm(k, "od_in", 4, k.H, [(0, TC), (TC, T)], scaled, first=4)
        values(k, "od_in", 8, V)
        dense_fm(k, "od_in", 4, k.H, lat, lambda n, b: v.tensor_copy(tile_of(G, n), b[0]), first=12)
        O = k.H[:, :, 0:T]
        with ExitStack() as c2:
            C2 = k.sb("consts2_sb", [P, C2_N], c2)
            t = k.load(k.spill, k.XA[:])
            t = k.load(C2[:], k.dram["consts2"])
            for q in (pe, dve, act):
                k.loaded(q, t)
            k.n_loads = 0
            c = lambda name, a=0, n=None: C2[:, C2_AT[name][0] + a:C2_AT[name][0] + a + (n or C2_AT[name][1])]
            act.go(nc.scalar.activation(G[:], G[:], ACT.Silu))
            LG, GC, ZT = k.sb("LG", [P, 16], c2), k.sb("GC", [P, 16], c2), k.sb("ZT", [P, 16], c2)
            DD = k.sb("DD", [P, RH, P], c2)
            XI = k.sb("XI", [P, 2, RH, P], c2)
            tmp = k.H[:, :, T:T + P]
            t = log_sigmoid(k, c2, LG[:], k.p("decay"))
            act.wait(t)
            act.go(nc.scalar.activation(GC[:], LG[:], ACT.Exp, scale=float(CH)))
            act.go(nc.scalar.activation(ZT[:, 0:8], LG[:, 0:8], ACT.Exp, scale=c("zpos", 0, 1)))
            act.go(nc.scalar.activation(ZT[:, 8:16], LG[:, 8:16], ACT.Exp, scale=c("zpos", 1, 1)))
            for h in range(RH):
                f, b = LG[:, h:h + 1], LG[:, 8 + h:9 + h]
                act.go(nc.scalar.activation(XI[:, 0, h, :], c("pos1"), ACT.Exp, scale=f))
                act.go(nc.scalar.activation(XI[:, 1, h, :], c("pos1r"), ACT.Exp, scale=b))
                act.go(nc.scalar.activation(DD[:, h, :], c("dist_f"), ACT.Exp, scale=f))
                t = act.go(nc.scalar.activation(tmp[:, h, :], c("dist_b"), ACT.Exp, scale=b))
            dve.wait(t)
            bc = lambda m: m.unsqueeze(1).broadcast_to([P, RH, P])
            ta = dve.go(v.tensor_tensor(DD[:], DD[:], bc(k.c("incl_up")), ALU.mult))
            tb = dve.go(v.tensor_tensor(tmp, tmp, bc(k.c("strict_low")), ALU.mult))
            dve.wait(ta, tb)
            dve.go(v.tensor_tensor(DD[:], DD[:], tmp, ALU.add))
            k.phase_end()
            with ExitStack() as c3:
                rope_loop(k, c3, Q, 0, c("ax_cos"), c("ax_sin"), "q")
            with ExitStack() as c3:
                rope_loop(k, c3, K, TC, c("ax_cos"), c("ax_sin"), "k")
            xa = k.XA[:].rearrange("p a t -> p (a t)")

            class Head:
                def __init__(b, n):
                    b.bank = 4 * n
                    b.ATT = k.sb(f"ATT_{n}r", [P, NL, P], c2)
                    b.sc = k.sb(f"ret_scal{n}", [P, 4], c2)
                    if n == 0:
                        b.KS, b.VS = k.sb("KS1", [P, TA], c2)[:], k.sb("VS", [P, NC, P], c2)[:]
                        b.KZ = k.sb("KZ", [P, 2, NC, P], c2)[:]
                        b.QX = k.sb("QX", [P, 2, T], c2)[:]
                        R = k.sb("Rst", [P, 2, NL, P], c2)
                        b.R = [R[:, d, :, :] for d in range(2)]
                    else:
                        b.KS = xa[:, 0:TA]
                        b.VS = xa[:, TA:2 * TA].rearrange("p (c i) -> p c i", c=NC)
                        b.KZ = xa[:, 2 * TA:4 * TA].rearrange("p (d c t) -> p d c t", d=2, c=NC)
                        b.QX = xa[:, 4 * TA:4 * TA + 2 * T].rearrange("p (d t) -> p d t", d=2)
                        b.R = [k.ring[:, d, DT * 2 * P:DT * 2 * P + T].rearrange("p (c i) -> p c i", c=NL) for d in range(2)]
                    b.RS = b.KZ[:, 0, 0:NL, :].rearrange("p c t -> p (c t)")

            heads = [Head(0), Head(1)]

            def retention(b, h):
                ds = bass.ds
                KS, VS, KZ, ATT, QX, R, RS, sc = b.KS, b.VS, b.KZ, b.ATT, b.QX, b.R, b.RS, b.sc
                SQ, OS = QX[:, 0, :], QX[:, 1, :]
                bank = lambda j: k.ps[:, b.bank + j, :]
                t_k = act.go(nc.scalar.copy(KS, tile_of(K, h)))
                t_v = act.go(nc.scalar.copy(VS, V[:, :, ds(h * P, P)]))
                for d in range(2):
                    dve.go(v.tensor_copy(sc[:, d:d + 1], ZT[:, ds(h + 8 * d, 1)]))
                    t_c = dve.go(v.tensor_copy(sc[:, 2 + d:3 + d], GC[:, ds(h + 8 * d, 1)]))
                yield
                pe.wait(t_k)
                for c_ in range(NC):
                    mm = nc.tensor.transpose(k.ps[:, b.bank + c_ // 4, (c_ % 4) * P:(c_ % 4 + 1) * P], KS[:, c_ * P:(c_ + 1) * P], k.ident)
                t_t = pe.go(mm)
                for c_ in range(NL):
                    mm = nc.tensor.matmul(bank(2)[:, c_ * P:(c_ + 1) * P], KS[:, TC + c_ * P:TC + (c_ + 1) * P],
                                          Q[:, ds(h, 1), c_ * P:(c_ + 1) * P].rearrange("p a t -> p (a t)"), start=True, stop=True)
                t_s = pe.go(mm)
                yield
                dve.wait(t_c, t_t)
                kt = flat_ps(k, b.bank, TA)
                for d in range(2):
                    t_kz = dve.go(v.tensor_scalar(KZ[:, d, :, :].rearrange("p c t -> p (c t)"), kt, sc[:, d:d + 1], None, ALU.mult))
                yield
                pe.wait(t_kz, t_v)
                ordf, ordb = (0, 1, 2, 3, 4), (1, 0, 5, 4, 3)

                def kv(d, n):
                    i = 5 * d + n
                    return bank((0, 1, 3)[i // 4])[:, (i % 4) * P:(i % 4 + 1) * P]
                for d, order in enumerate((ordf, ordb)):
                    for n, c_ in enumerate(order):
                        mm = nc.tensor.matmul(kv(d, n), KZ[:, d, c_, :], VS[:, c_, :], start=True, stop=True)
                t_kv = pe.go(mm)
                yield
                dve.wait(t_s)
                dd = DD[:, ds(h, 1), :].broadcast_to([P, NL, P])
                t_att = dve.go(v.tensor_tensor(ATT[:], bank(2).rearrange("p (c t) -> p c t", c=NL), dd, ALU.mult))
                for d in range(2):
                    xi = XI[:, d, ds(h, 1), :].broadcast_to([P, NL, P])
                    q = Q[:, ds(h, 1), :].rearrange("p a (c t) -> p (a c) t", t=CH)
                    t_qx = dve.go(v.tensor_tensor(QX[:, d, :].rearrange("p (c t) -> p c t", t=CH), q, xi, ALU.mult))
                yield
                dve.wait(t_kv)
                for d in range(2):
                    t_r = dve.go(v.tensor_copy(R[d][:, 0, :], kv(d, 0)))
                yield
                for n in range(1, 5):
                    dve.wait(t_r)
                    for d in range(2):
                        src, dst = R[d][:, max(n - 2, 0), :], R[d][:, n - 1, :]
                        t_r = dve.go(v.scalar_tensor_tensor(dst, src, sc[:, 2 + d:3 + d], kv(d, n), ALU.mult, ALU.add))
                    yield
                pe.wait(t_att, t_qx, t_r)
                for c_ in range(NL):
                    o = bank(2)[:, c_ * P:(c_ + 1) * P]
                    a = slice(c_ * P, (c_ + 1) * P)
                    nc.tensor.matmul(o, VS[:, 2 + c_, :], ATT[:, c_, :], start=True, stop=False)
                    nc.tensor.matmul(o, R[0][:, c_, :], QX[:, 0, a], start=False, stop=False)
                    mm = nc.tensor.matmul(o, R[1][:, NL - 1 - c_, :], QX[:, 1, a], start=False, stop=True)
                t_o = pe.go(mm)
                yield
                act.wait(t_o)
                t_sq = act.go(nc.scalar.activation(SQ, bank(2), ACT.Square))
                t_os = act.go(nc.scalar.copy(OS, bank(2)))
                yield
                pe.wait(t_sq)
                t = pe.go(nc.tensor.matmul(bank(3), k.ones, SQ, start=True, stop=True))
                yield
                rstd(k, RS, bank(3), 1.0 / P, EPS, t)
                dve.wait(t_os)
                t = dve.go(v.tensor_tensor(OS, OS, RS, ALU.mult))
                yield
                dve.wait(t)
                dve.go(v.tensor_tensor(tile_of(O, h), OS, tile_of(G, h), ALU.mult))

            with nc.Fori(0, RH // 2) as i:
                rounds(retention(heads[0], 2 * i), retention(heads[1], 2 * i + 1))
                k.phase_end()
        t = k.load(k.XA[:], k.spill)
        k.loaded(act, t)
        k.n_loads = 0
        dense_fm(k, "od_out", 4, O, [(0, T)], lambda n, b: v.tensor_copy(tile_of(Q, n), b[0]))
        act.go(nc.scalar.copy(OUT[:, :, 0:T], Q[:]))
        k.phase_end()


def values(k, name, first, V):
    nc, pe = k.nc, k.pe
    w = k.dram[name]
    NC = TA // P
    nc.vector.sem_inc(k.free_a, NSLOT)
    with nc.Fori(0, 2) as i:
        for s in range(NSLOT):
            k.fetch(w[first + i * NSLOT + s], DT, 2 * P, i, 1)
            k.slab_wait(i, 1)
            wv = k.slab_view(DT, 2 * P)
            slot = k.slab_next()
            pe.wait_reg(k.free_a, i * NSLOT + s + 1)
            for t in range(NC):
                for kk in range(DT):
                    mm = nc.tensor.matmul(k.ps[:, 3 * s + t // 2, (t % 2) * 256:(t % 2 + 1) * 256],
                                          k.H[:, kk, t * P:(t + 1) * P], wv[:, kk, :], start=(kk == 0), stop=(kk == DT - 1))
            mm.then_inc(k.mm_a, 1)
            k.dve.wait_reg(k.mm_a, i * NSLOT + s + 1, slot)
            nc.vector.tensor_copy(V[:, :, bass.ds((i * NSLOT + s) * 256, 256)],
                                  k.ps[:, 3 * s:3 * s + 3, :].rearrange("p b (t n) -> p (b t) n", n=256)).then_inc(k.free_a, 1)
    k.slab_loop(2)
    k.phase_end()


def program(nc, dram, upto=99):
    with ExitStack() as ctx:
        k = Core(nc, ctx, dram)
        setup(k)
        ada(k, "ada0", 24, k.p("c").unsqueeze(2), 1, k.MOD[0], k.p("ada_b0"))
        if upto < 5 or upto > 90:
            ada(k, "ada1", 24, k.p("c").unsqueeze(2), 1, k.MOD[1], k.p("ada_b1"))
            block1_input(k, ctx, 0)
            with ExitStack() as c1:
                R = k.sb("R", [P, DT, T], c1)
                even_mixer1(k, R)
                if upto == 1:
                    return finish(k, R)
                residual_norm(k, R, 0, 0)
                if upto == 2:
                    return finish(k, k.XA)
                ffn(k, 0, R)
                residual_norm(k, R, 0, 1)
                if upto == 3:
                    return finish(k, k.XA)
                pool_mixer(k, R)
                residual_norm(k, R, 1, 0)
                ffn(k, 1, R)
                residual_norm(k, R, 1, 1)
                if upto == 4:
                    return finish(k, k.XA)
        MOD = k.sb("mod2", [P, 24, 2])
        c2 = k.p("c2").rearrange("p (a n) -> p a n", n=2)
        ada(k, "ada2_0", 12, c2, 2, MOD, k.p("ada_b2_0"))
        with ExitStack() as c1:
            XC = k.sb("XC", [P, DT, TC], c1)
            t = k.load(XC[:], dram["ctx"])
            k.loaded(k.act, t)
            k.loaded(k.dve, t)
            k.n_loads = 0
            pre_norm(k, c1, 0, MOD, XC)
        spill = nc.dram_tensor("latents", (P, DT, T), F32, kind="Internal").ap()
        k.spill = spill
        t = k.load(spill, k.XA[:])
        for q in (k.act, k.dve, k.pe, k.pool):
            k.loaded(q, t)
        k.n_loads = 0
        OUT = k.H
        even_mixer2(k, ctx, OUT)
        if upto == 5:
            return finish(k, OUT[:, :, TC:TA])
        with ExitStack() as c1:
            XC = k.sb("XC_b", [P, DT, TC], c1)
            t = k.load(k.XA[:], k.spill)
            t = k.load(XC[:], dram["ctx"])
            k.loaded(k.dve, t)
            k.n_loads = 0
            post_norm(k, c1, "l", 0, MOD, OUT, k.XA, 0, TC, T)
            post_norm(k, c1, "c", 0, MOD, OUT, XC, 1, 0, TC)
            if upto == 6:
                return finish(k, k.XA)
            ada(k, "ada2_1", 12, c2, 2, MOD, k.p("ada_b2_1"))
            pre_norm(k, c1, 1, MOD, XC)
        odd_mixer2(k, OUT)
        with ExitStack() as c1:
            post_norm(k, c1, "f", 1, MOD, OUT, k.XA, 0, 0, T)
        finish(k, k.XA)


def finish(k, X):
    nc = k.nc
    nc.scalar.dma_start(k.dram["out"], X[:]).then_inc(k.loads, 16)
    nc.scalar.wait_ge(k.loads, 16)


def columns(a):
    a = np.asarray(a)
    return np.ascontiguousarray(a.reshape(-1, P).T)


def slabs(w, cols, tiles=2):
    w = np.asarray(w)[:, cols] if cols is not None else np.asarray(w)
    K, N = w.shape
    n = tiles * P
    return np.ascontiguousarray(w.reshape(K // P, P, N // n, n).transpose(2, 1, 0, 3)).reshape(N // n, P, -1)


def lay_out(a):
    r = np.arange
    out = {}
    fm = lambda x: np.ascontiguousarray(np.asarray(x).T.reshape(DT, P, -1).transpose(1, 0, 2))
    out["x"] = fm(a["x"][0])
    out["ctx"] = fm(a["ctx_2"][0])
    out["positions"] = np.asarray(a["positions"])[0]
    heads = np.concatenate([np.concatenate([r(64) + 64 * j, r(64) + 64 * (j + 4)]) for j in range(4)])
    aq, af, ai, ag = (r(512) + 512 * i for i in range(4))
    bq, bk, bv = 2048 + heads, 2560 + r(128), 2688 + r(128)
    out["ab_in"] = slabs(a["ab_w_in"][0], np.concatenate([aq, af, ag, bq, bk, bv, ai]))
    rows = np.concatenate([r(512), 512 + heads])
    out["ab_out"] = slabs(np.asarray(a["ab_w_out"][0])[rows], None)
    for l in range(DEPTH):
        out[f"ada{l}"] = slabs(a["ada_w"][l], None)
        out[f"ada2_{l}"] = slabs(a["ada_w_2"][l], None)
        uv = np.concatenate([np.concatenate([n * P + r(P), FF + n * P + r(P)]) for n in range(FT)])
        out[f"w_up{l}"] = slabs(a["ffn_w_up"][l], uv)
        out[f"w_down{l}"] = slabs(a["ffn_w_down"][l], None, 1)
    out["pool_w"] = np.ascontiguousarray(np.asarray(a["pool_w"][0]).reshape(4, 2, P, 256).transpose(2, 0, 1, 3)).reshape(1, P, -1)
    tile = lambda n: n * P + r(P)
    order = [tile(n) for n in (18, 19, 26, 27, 28, 29)]
    for j in range(RT):
        order += [tile(j), tile(6 + j), tile(12 + j), tile(20 + j)]
    out["ev_in"] = slabs(a["ev_w_in_2"][0], np.concatenate(order))
    out["ev_out"] = slabs(a["ev_w_out_2"][0], None)
    w2, a2 = (np.asarray(a[n][0]).reshape(P, RT, 1, P) for n in ("ev_w2_2", "ev_a2_2"))
    out["w2a2"] = np.ascontiguousarray(np.concatenate([w2, a2], 2).transpose(1, 0, 2, 3)).reshape(RT, P, 2 * P)
    out["od_in"] = slabs(a["od_w_in_2"][0], None)
    out["od_out"] = slabs(a["od_w_out_2"][0], None)
    p = {}
    p["c"] = columns(a["c"][0])
    p["c2"] = np.stack([columns(a["c_2"][0]), columns(a["c_ctx_2"])], 2).reshape(P, 16)
    for l in range(DEPTH):
        p[f"ada_b{l}"] = columns(a["ada_b"][l])
        p[f"ada_b2_{l}"] = columns(a["ada_b_2"][l])
        cw, cb = np.asarray(a["ffn_conv_w"][l]), np.asarray(a["ffn_conv_b"][l])
        p[f"conv{l}"] = np.stack([columns(cw[0]), columns(cw[1]), columns(cw[2]), columns(cb)], 2).reshape(P, -1)
    p["ln_g"], p["ln_b"] = columns(a["ln_g"]), columns(a["ln_b"])
    p["lb_raw"] = columns(a["hgrn_lb_raw"][0])
    p["norm_g"] = columns(a["hgrn_norm_g"][0])
    p["sinks"] = np.broadcast_to(np.asarray(a["attn_sinks"][0]).reshape(1, 8), (P, 8))
    p["pool_scale"] = columns(a["pool_scale"][0])
    p["norm_pre"], p["norm_post"] = columns(a["norm_pre_2"]), columns(a["norm_post_2"])
    p["mu"] = columns(a["ev_mu_2"][0])
    rw = [a["ev_w0_2"][0][0], a["ev_w0_2"][0][1], a["ev_a0_2"][0][0], a["ev_a0_2"][0][1], a["ev_k_k_2"][0],
          a["ev_k_a_2"][0], np.asarray(a["ev_r_k_2"][0]).reshape(-1), a["ev_lnx_g_2"][0], a["ev_lnx_b_2"][0]]
    p["rw"] = np.stack([columns(x) for x in rw], 2).reshape(P, -1)
    p["decay"] = np.broadcast_to(np.asarray(a["od_decay_logit_2"][0]).reshape(1, 16), (P, 16))
    out["params"] = np.concatenate([p[n] for n, _ in PARAMS], 1)
    out["consts"], out["consts2"], out["dft"] = constants()
    return out


def kernel(**inputs):
    import concourse.bacc as _bacc
    from concourse.bass_utils import run_bass_kernel_spmd as _run

    arrays = lay_out(inputs)
    nc = _bacc.Bacc("TRN2", target_bir_lowering=False, num_devices=1)
    dram = {n: nc.dram_tensor(n, x.shape, mybir.dt.from_np(x.dtype), kind="ExternalInput").ap()
            for n, x in arrays.items()}
    dram["out"] = nc.dram_tensor("out", (P, DT, T), F32, kind="ExternalOutput").ap()
    program(nc, dram)
    r = _run(nc, [arrays], core_ids=[0])
    y = np.asarray(r.results[0]["out"])
    return np.ascontiguousarray(y.transpose(2, 1, 0).reshape(1, T, D))
```
